# Optimizing a Trainium2 kernel written in Bass

```python
import math
import jax, jax.numpy as jnp
from jax import lax
import numpy as np

D_MODEL = 1024
BATCH = 1
SEQ = 256
DEPTH = 2

GRID_W = 64
CTX_LEN = 256
HEAD_DIM = 64
ROPE_BASE = 10000.0
EPS = 1e-6
NEG_INF = -1e30
ATTN_SCALE = HEAD_DIM ** -0.5
Q_BLOCK = 128
CHUNK = 128
A_GROUPS = 4
A_GROUP_DIM = 128
A_WIDTH = A_GROUPS * A_GROUP_DIM
B_HEADS = 4
B_QK_WIDTH = 2 * B_HEADS * HEAD_DIM
B_V_DIM = 2 * HEAD_DIM
B_V_WIDTH = B_HEADS * B_V_DIM
KV_START = 2 * A_WIDTH + B_QK_WIDTH
EVEN_IN = 2 * A_WIDTH + 2 * B_QK_WIDTH + B_V_WIDTH
EVEN_OUT = A_WIDTH + B_V_WIDTH
C_HEADS = 16
C_KV_HEADS = 4
C_GROUP = C_HEADS // C_KV_HEADS
WINDOW = 128
C_Q_WIDTH = C_HEADS * HEAD_DIM
C_KV_WIDTH = C_KV_HEADS * HEAD_DIM
C_IN = C_Q_WIDTH + 2 * C_KV_WIDTH
FFN_HIDDEN = ((8 * D_MODEL + 3 * 256 - 1) // (3 * 256)) * 256
N_EVEN = (DEPTH + 1) // 2
N_ODD = DEPTH // 2


def rmsnorm(x, g):
    xf = x.astype(jnp.float32)
    y = xf * lax.rsqrt(jnp.mean(xf * xf, axis=-1, keepdims=True) + EPS)
    return (y * g.astype(jnp.float32)).astype(x.dtype)

def modulate(x, g, shift, scale):
    return rmsnorm(x, g) * (1 + scale) + shift

def rope_tables(s_len, dtype):
    rows = s_len // GRID_W
    row = jnp.repeat(jnp.arange(rows), GRID_W).astype(jnp.float32)
    col = jnp.tile(jnp.arange(GRID_W), rows).astype(jnp.float32)
    nf = HEAD_DIM // 4
    inv = ROPE_BASE ** (-jnp.arange(nf, dtype=jnp.float32) / nf)
    ang = jnp.stack([row[:, None] * inv, col[:, None] * inv], axis=1)
    ang = jnp.broadcast_to(ang[:, :, None, :], (s_len, 2, 2, nf)).reshape(s_len, HEAD_DIM)
    return jnp.cos(ang).astype(dtype), jnp.sin(ang).astype(dtype)

def apply_rope(x, cos, sin):
    xr = x.reshape(x.shape[:-1] + (2, 2, HEAD_DIM // 4))
    rot = jnp.stack([-xr[..., 1, :], xr[..., 0, :]], axis=-2).reshape(x.shape)
    return x * cos[None, :, None, :] + rot * sin[None, :, None, :]

def swiglu(h, w_in, w_out):
    g, u = jnp.split(h @ w_in, 2, axis=-1)
    return (jax.nn.silu(g) * u) @ w_out

def chunk_mlp(u, v, w_s, b_s):
    b, t, _ = u.shape
    shp = (b, t // CHUNK, CHUNK, A_GROUPS, A_GROUP_DIM)
    u = jax.nn.gelu(u, approximate=False).reshape(shp)
    vf = jax.nn.gelu(v.astype(jnp.float32), approximate=False).reshape(shp)
    mu = jnp.mean(vf, axis=-1, keepdims=True)
    vf = (vf - mu) * lax.rsqrt(jnp.mean(jnp.square(vf - mu), axis=-1, keepdims=True) + EPS)
    mixed = jnp.einsum('gpq,bnqgc->bnpgc', w_s.astype(jnp.float32), vf) + b_s.astype(jnp.float32).T[None, None, :, :, None]
    return (u * mixed.astype(u.dtype)).reshape(b, t, A_WIDTH)

def diff_attn(q, k, v, lam):
    b, tq = q.shape[0], q.shape[1]
    tk = k.shape[1]
    s = jnp.einsum('bqhd,bkhd->bhqk', q, k).astype(jnp.float32) * ATTN_SCALE
    p = jax.nn.softmax(s, axis=-1).reshape(b, B_HEADS, 2, tq, tk)
    a = p[:, :, 0] - lam * p[:, :, 1]
    return jnp.einsum('bhqk,bkhe->bqhe', a.astype(v.dtype), v)

def diff_out(o, g, lam_init):
    b, t = o.shape[0], o.shape[1]
    return (rmsnorm(o, g) * (1.0 - lam_init)).reshape(b, t, B_V_WIDTH)

def sink_attend(q, kvs, sink):
    scores = []
    for k, v, mask in kvs:
        s = jnp.einsum('bqhgd,bkhd->bhgqk', q, k).astype(jnp.float32) * ATTN_SCALE
        if mask is not None:
            s = jnp.where(mask, s, NEG_INF)
        scores.append(s)
    s_sink = jnp.broadcast_to(sink.astype(jnp.float32).reshape(1, C_KV_HEADS, C_GROUP, 1, 1), scores[0].shape[:-1] + (1,))
    p = jax.nn.softmax(jnp.concatenate(scores + [s_sink], axis=-1), axis=-1)
    out = None
    start = 0
    for k, v, _ in kvs:
        tk = k.shape[1]
        o = jnp.einsum('bhgqk,bkhd->bqhgd', p[..., start:start + tk].astype(v.dtype), v)
        out = o if out is None else out + o
        start += tk
    return out

def even_mixer(h, hc, w_in, w_out, w_s, b_s, lq1, lk1, lq2, lk2, subln_g, lam_init, cos, sin, need_ctx):
    b, s_len, _ = h.shape
    nb = s_len // Q_BLOCK
    f32 = jnp.float32
    lam = (jnp.exp(jnp.sum(lq1.astype(f32) * lk1.astype(f32)))
           - jnp.exp(jnp.sum(lq2.astype(f32) * lk2.astype(f32))) + lam_init)
    u, v, q, k, vv = jnp.split(h @ w_in, [A_WIDTH, 2 * A_WIDTH, KV_START, KV_START + B_QK_WIDTH], axis=-1)
    q = apply_rope(q.reshape(b, s_len, 2 * B_HEADS, HEAD_DIM), cos, sin)
    k = apply_rope(k.reshape(b, s_len, 2 * B_HEADS, HEAD_DIM), cos, sin)
    vv = vv.reshape(b, s_len, B_HEADS, B_V_DIM)
    kc, vvc = jnp.split(hc @ w_in[:, KV_START:], [B_QK_WIDTH], axis=-1)
    kc = kc.reshape(b, -1, 2 * B_HEADS, HEAD_DIM)
    vvc = vvc.reshape(b, -1, B_HEADS, B_V_DIM)
    k_all = jnp.concatenate([k, kc], axis=1)
    v_all = jnp.concatenate([vv, vvc], axis=1)
    q_blocks = q.reshape(b, nb, Q_BLOCK, 2 * B_HEADS, HEAD_DIM).transpose(1, 0, 2, 3, 4)
    o = lax.map(lambda qb: diff_attn(qb, k_all, v_all, lam), q_blocks)
    o = o.transpose(1, 0, 2, 3, 4).reshape(b, s_len, B_HEADS, B_V_DIM)
    y = jnp.concatenate([chunk_mlp(u, v, w_s, b_s), diff_out(o, subln_g, lam_init)], axis=-1) @ w_out
    yc = None
    if need_ctx:
        uc, vc_, qc = jnp.split(hc @ w_in[:, :KV_START], [A_WIDTH, 2 * A_WIDTH], axis=-1)
        qc = qc.reshape(b, -1, 2 * B_HEADS, HEAD_DIM)
        oc = diff_attn(qc, kc, vvc, lam)
        yc = jnp.concatenate([chunk_mlp(uc, vc_, w_s, b_s), diff_out(oc, subln_g, lam_init)], axis=-1) @ w_out
    return y, yc

def odd_mixer(h, hc, w_qkv, w_out, sink, cos, sin, need_ctx):
    b, s_len, _ = h.shape
    nb = s_len // Q_BLOCK
    q, k, v = jnp.split(h @ w_qkv, [C_Q_WIDTH, C_Q_WIDTH + C_KV_WIDTH], axis=-1)
    q = apply_rope(q.reshape(b, s_len, C_HEADS, HEAD_DIM), cos, sin).reshape(b, s_len, C_KV_HEADS, C_GROUP, HEAD_DIM)
    k = apply_rope(k.reshape(b, s_len, C_KV_HEADS, HEAD_DIM), cos, sin)
    v = v.reshape(b, s_len, C_KV_HEADS, HEAD_DIM)
    kc, vc = jnp.split(hc @ w_qkv[:, C_Q_WIDTH:], 2, axis=-1)
    kc = kc.reshape(b, -1, C_KV_HEADS, HEAD_DIM)
    vc = vc.reshape(b, -1, C_KV_HEADS, HEAD_DIM)
    pad = ((0, 0), (WINDOW, WINDOW), (0, 0), (0, 0))
    k_pad = jnp.pad(k, pad)
    v_pad = jnp.pad(v, pad)
    band = Q_BLOCK + 2 * WINDOW
    q_blocks = q.reshape(b, nb, Q_BLOCK, C_KV_HEADS, C_GROUP, HEAD_DIM).transpose(1, 0, 2, 3, 4, 5)

    def block(args):
        i, qb = args
        start = i * Q_BLOCK
        kb = lax.dynamic_slice_in_dim(k_pad, start, band, axis=1)
        vb = lax.dynamic_slice_in_dim(v_pad, start, band, axis=1)
        qpos = start + jnp.arange(Q_BLOCK)
        kpos = start - WINDOW + jnp.arange(band)
        mask = ((kpos >= 0)[None, :] & (kpos < s_len)[None, :]
                & (jnp.abs(qpos[:, None] - kpos[None, :]) <= WINDOW))
        return sink_attend(qb, [(kb, vb, mask), (kc, vc, None)], sink)

    o = lax.map(block, (jnp.arange(nb), q_blocks))
    y = o.transpose(1, 0, 2, 3, 4, 5).reshape(b, s_len, C_Q_WIDTH) @ w_out
    yc = None
    if need_ctx:
        qc = (hc @ w_qkv[:, :C_Q_WIDTH]).reshape(b, -1, C_KV_HEADS, C_GROUP, HEAD_DIM)
        yc = sink_attend(qc, [(kc, vc, None)], sink).reshape(b, -1, C_Q_WIDTH) @ w_out
    return y, yc

def first_inputs(seed: int = 0) -> dict:
    key = jax.random.key(seed)
    ks = jax.random.split(key, 24)
    n = jax.random.normal
    f32 = jnp.float32
    return {
        'x': n(ks[0], (BATCH, SEQ, D_MODEL), f32),
        'c': n(ks[1], (BATCH, D_MODEL), f32),
        'ctx': n(ks[2], (BATCH, CTX_LEN, D_MODEL), f32),
        'c_ctx': n(ks[3], (D_MODEL,), f32),
        'ada_w': n(ks[4], (DEPTH, D_MODEL, 6 * D_MODEL), f32) * (0.5 * D_MODEL ** -0.5),
        'ada_b': n(ks[5], (DEPTH, 6 * D_MODEL), f32) * 0.02,
        'norm1_g': 1.0 + 0.02 * n(ks[6], (DEPTH, D_MODEL), f32),
        'norm2_g': 1.0 + 0.02 * n(ks[7], (DEPTH, D_MODEL), f32),
        'ffn_w_in': n(ks[8], (DEPTH, D_MODEL, 2 * FFN_HIDDEN), f32) * D_MODEL ** -0.5,
        'ffn_w_out': n(ks[9], (DEPTH, FFN_HIDDEN, D_MODEL), f32) * FFN_HIDDEN ** -0.5,
        'even_w_in': n(ks[10], (N_EVEN, D_MODEL, EVEN_IN), f32) * D_MODEL ** -0.5,
        'even_w_out': n(ks[11], (N_EVEN, EVEN_OUT, D_MODEL), f32) * EVEN_OUT ** -0.5,
        'sgu_w': n(ks[12], (N_EVEN, A_GROUPS, CHUNK, CHUNK), f32) * CHUNK ** -0.5,
        'sgu_b': 1.0 + 0.1 * n(ks[13], (N_EVEN, A_GROUPS, CHUNK), f32),
        'diff_lq1': 0.1 * n(ks[14], (N_EVEN, HEAD_DIM), f32),
        'diff_lk1': 0.1 * n(ks[15], (N_EVEN, HEAD_DIM), f32),
        'diff_lq2': 0.1 * n(ks[16], (N_EVEN, HEAD_DIM), f32),
        'diff_lk2': 0.1 * n(ks[17], (N_EVEN, HEAD_DIM), f32),
        'diff_subln_g': 1.0 + 0.02 * n(ks[18], (N_EVEN, B_V_DIM), f32),
        'odd_w_qkv': n(ks[19], (N_ODD, D_MODEL, C_IN), f32) * D_MODEL ** -0.5,
        'odd_w_out': n(ks[20], (N_ODD, C_Q_WIDTH, D_MODEL), f32) * C_Q_WIDTH ** -0.5,
        'odd_sink': 0.5 * n(ks[21], (N_ODD, C_HEADS), f32),
        'final_g': 1.0 + 0.02 * n(ks[22], (D_MODEL,), f32),
    }

def first_block(x, c, ctx, c_ctx, ada_w, ada_b, norm1_g, norm2_g, ffn_w_in, ffn_w_out,
              even_w_in, even_w_out, sgu_w, sgu_b, diff_lq1, diff_lk1, diff_lq2, diff_lk2,
              diff_subln_g, odd_w_qkv, odd_w_out, odd_sink, final_g):
    s_len = x.shape[1]
    cos, sin = rope_tables(s_len, x.dtype)
    silu_c = jax.nn.silu(c)
    silu_cc = jax.nn.silu(c_ctx)
    h, hc = x, ctx
    for l in range(DEPTH):
        need_ctx = l < DEPTH - 1
        j = l // 2
        mod = silu_c @ ada_w[l] + ada_b[l]
        modc = silu_cc @ ada_w[l] + ada_b[l]
        sh1, sc1, g1, sh2, sc2, g2 = [m[:, None, :] for m in jnp.split(mod, 6, axis=-1)]
        csh1, csc1, cg1, csh2, csc2, cg2 = [m[None, None, :] for m in jnp.split(modc, 6, axis=-1)]
        a = modulate(h, norm1_g[l], sh1, sc1)
        ac = modulate(hc, norm1_g[l], csh1, csc1)
        if l % 2 == 0:
            lam_init = 0.8 - 0.6 * math.exp(-0.3 * l)
            y, yc = even_mixer(a, ac, even_w_in[j], even_w_out[j], sgu_w[j], sgu_b[j],
                               diff_lq1[j], diff_lk1[j], diff_lq2[j], diff_lk2[j], diff_subln_g[j],
                               lam_init, cos, sin, need_ctx)
        else:
            y, yc = odd_mixer(a, ac, odd_w_qkv[j], odd_w_out[j], odd_sink[j], cos, sin, need_ctx)
        h = h + g1 * y
        h = h + g2 * swiglu(modulate(h, norm2_g[l], sh2, sc2), ffn_w_in[l], ffn_w_out[l])
        if need_ctx:
            hc = hc + cg1 * yc
            hc = hc + cg2 * swiglu(modulate(hc, norm2_g[l], csh2, csc2), ffn_w_in[l], ffn_w_out[l])
    return rmsnorm(h, final_g)


CHUNK_2 = 64
SWA_HEADS = 8
SWA_KV_HEADS = 2
SWA_GROUP = SWA_HEADS // SWA_KV_HEADS
SWA_WINDOW = 128
SWA_WIN_CHUNKS = (SWA_WINDOW + CHUNK_2 - 1) // CHUNK_2
RWKV_HEADS = 4
RWKV_W_RANK = 64
RWKV_A_RANK = 64
RWKV_G_RANK = 128
RWKV_GN_EPS = 64e-5
FOX_HEADS = 4
FOX_BLOCK = 128
DSA_HEADS = 4
IDX_HEADS = 4
IDX_DIM = 64
DSA_TOPK_MAX = 256
DSA_BLOCK = 128
D_FF = 2816
N_EXPERTS = 8
TOP_K = 2
D_FF_EXPERT = 1408
N_DENSE = (DEPTH + 1) // 2
N_MOE = DEPTH // 2
N_BRANCHES = 4
DN_ALPHA = (2 * DEPTH) ** 0.25
DN_BETA = (8 * DEPTH) ** -0.25
LN_EPS = 1e-5
ATTN_SCALE_2 = HEAD_DIM ** -0.5
IDX_SCALE = IDX_DIM ** -0.5
IDX_W_SCALE = IDX_HEADS ** -0.5

SWA_Q = SWA_HEADS * HEAD_DIM
SWA_KV = SWA_KV_HEADS * HEAD_DIM
RWKV_W = RWKV_HEADS * HEAD_DIM
FOX_W = FOX_HEADS * HEAD_DIM
DSA_W = DSA_HEADS * HEAD_DIM
MIX_WIDTHS = (SWA_Q, RWKV_W, FOX_W, DSA_W)
MIX_WIDTH = SWA_Q + RWKV_W + FOX_W + DSA_W
SWA_SPLITS = (SWA_Q, SWA_KV, SWA_KV)
RWKV_SPLITS = (RWKV_W, RWKV_W, RWKV_W, RWKV_W_RANK, RWKV_A_RANK, RWKV_G_RANK)
FOX_SPLITS = (FOX_W, FOX_W, FOX_W, FOX_HEADS)
DSA_SPLITS = (DSA_W, HEAD_DIM, HEAD_DIM, IDX_HEADS * IDX_DIM, IDX_DIM, IDX_HEADS)
RWKV_IN = sum(RWKV_SPLITS)
GATE_COLS = N_BRANCHES * D_MODEL
IN_GROUPS = (sum(SWA_SPLITS), RWKV_IN, sum(FOX_SPLITS), sum(DSA_SPLITS), GATE_COLS)
D_IN = sum(IN_GROUPS)


def split_cols(t, sizes, axis=-1):
    idx = [int(i) for i in np.cumsum(sizes)[:-1]]
    return jnp.split(t, idx, axis=axis)

def layer_norm(x, g, b):
    xf = x.astype(jnp.float32)
    mu = jnp.mean(xf, axis=-1, keepdims=True)
    var = jnp.mean(jnp.square(xf - mu), axis=-1, keepdims=True)
    return ((xf - mu) * lax.rsqrt(var + LN_EPS) * g + b).astype(x.dtype)

def swa_branch(q, k, v, sinks):
    B, S, _ = q.shape
    nc = S // CHUNK_2
    W = SWA_WIN_CHUNKS
    q = q.reshape(B, nc, CHUNK_2, SWA_KV_HEADS, SWA_GROUP, HEAD_DIM)
    pad = ((0, 0), (W, 0), (0, 0), (0, 0), (0, 0))
    kp = jnp.pad(k.reshape(B, nc, CHUNK_2, SWA_KV_HEADS, HEAD_DIM), pad)
    vp = jnp.pad(v.reshape(B, nc, CHUNK_2, SWA_KV_HEADS, HEAD_DIM), pad)
    kb = jnp.concatenate([kp[:, j:j + nc] for j in range(W + 1)], axis=2)
    vb = jnp.concatenate([vp[:, j:j + nc] for j in range(W + 1)], axis=2)
    key_chunk = jnp.arange(nc)[:, None] - W + jnp.arange(W + 1)[None, :]
    valid = jnp.repeat(key_chunk >= 0, CHUNK_2, axis=1)
    logits = jnp.einsum('bcqhgd,bckhd->bchgqk', q, kb).astype(jnp.float32) * ATTN_SCALE_2
    logits = jnp.where(valid[None, :, None, None, None, :], logits, -jnp.inf)
    sink = sinks.astype(jnp.float32).reshape(1, 1, SWA_KV_HEADS, SWA_GROUP, 1, 1)
    m = jnp.maximum(jnp.max(logits, axis=-1, keepdims=True), sink)
    e = jnp.exp(logits - m)
    p = e / (jnp.sum(e, axis=-1, keepdims=True) + jnp.exp(sink - m))
    o = jnp.einsum('bchgqk,bckhd->bcqhgd', p.astype(v.dtype), vb)
    return o.reshape(B, S, SWA_Q)

def rwkv7_branch(p, mu, w0, w_up, a0, a_up, g_up, k_k, k_a, r_k, gn_g, gn_b):
    B, S, _ = p.shape
    p_prev = jnp.pad(p[:, :-1], ((0, 0), (1, 0), (0, 0)))
    p = p + mu * (p_prev - p)
    r, k, v, w_lo, a_lo, g_lo = split_cols(p, RWKV_SPLITS)
    log_w = -jnp.exp(-jax.nn.softplus(-(w0 + jnp.tanh(w_lo) @ w_up).astype(jnp.float32)) - 0.5)
    a = jax.nn.sigmoid(a0 + a_lo @ a_up)
    g = jax.nn.sigmoid(g_lo) @ g_up
    hd = lambda t: t.reshape(B, S, RWKV_HEADS, HEAD_DIM).astype(jnp.float32)
    kk = hd(k * k_k)
    kk = kk * lax.rsqrt(jnp.sum(kk * kk, axis=-1, keepdims=True) + 1e-12)
    k = k * (1.0 + (a - 1.0) * k_a)
    r_h, k_h, v_h, a_h, w_h = hd(r), hd(k), hd(v), hd(a), hd(jnp.exp(log_w))
    seq = tuple(jnp.moveaxis(t, 1, 0) for t in (r_h, w_h, k_h, v_h, kk, a_h))

    def step(state, inp):
        r_t, w_t, k_t, v_t, kk_t, a_t = inp
        sa = jnp.einsum('bhvk,bhk->bhv', state, -kk_t)
        state = (state * w_t[:, :, None, :]
                 + sa[..., None] * (kk_t * a_t)[:, :, None, :]
                 + v_t[..., None] * k_t[:, :, None, :])
        return state, jnp.einsum('bhvk,bhk->bhv', state, r_t)

    s0 = jnp.zeros((B, RWKV_HEADS, HEAD_DIM, HEAD_DIM), jnp.float32)
    _, y = lax.scan(step, s0, seq)
    y = jnp.moveaxis(y, 0, 1)
    ym = jnp.mean(y, axis=-1, keepdims=True)
    yv = jnp.mean(jnp.square(y - ym), axis=-1, keepdims=True)
    y = ((y - ym) * lax.rsqrt(yv + RWKV_GN_EPS)).reshape(B, S, RWKV_W) * gn_g + gn_b
    bonus = (jnp.sum(r_h * k_h * r_k, axis=-1, keepdims=True) * v_h).reshape(B, S, RWKV_W)
    return ((y + bonus) * g).astype(p.dtype)

def fox_branch(q, k, v, f_logit, f_bias):
    B, S, _ = q.shape
    q = q.reshape(B, S, FOX_HEADS, HEAD_DIM)
    k = k.reshape(B, S, FOX_HEADS, HEAD_DIM)
    v = v.reshape(B, S, FOX_HEADS, HEAD_DIM)
    log_f = jax.nn.log_sigmoid(f_logit.astype(jnp.float32) + f_bias)
    c = jnp.cumsum(log_f, axis=1).transpose(0, 2, 1)
    outs = []
    for blk in range(S // FOX_BLOCK):
        lo, hi = blk * FOX_BLOCK, (blk + 1) * FOX_BLOCK
        logits = jnp.einsum('bqhd,bkhd->bhqk', q[:, lo:hi], k[:, :hi]).astype(jnp.float32) * ATTN_SCALE_2
        logits = logits + c[:, :, lo:hi, None] - c[:, :, None, :hi]
        causal = jnp.arange(lo, hi)[:, None] >= jnp.arange(hi)[None, :]
        logits = jnp.where(causal, logits, -jnp.inf)
        p = jax.nn.softmax(logits, axis=-1)
        outs.append(jnp.einsum('bhqk,bkhd->bqhd', p.astype(v.dtype), v[:, :hi]))
    return jnp.concatenate(outs, axis=1).reshape(B, S, FOX_W)

def dsa_branch(q, k, v, q_idx, k_idx, w_idx):
    B, S, _ = q.shape
    topk = min(DSA_TOPK_MAX, S // 4)
    nb = S // DSA_BLOCK
    qT = jnp.moveaxis(q.reshape(B, nb, DSA_BLOCK, DSA_HEADS, HEAD_DIM), 1, 0)
    qiT = jnp.moveaxis(q_idx.reshape(B, nb, DSA_BLOCK, IDX_HEADS, IDX_DIM), 1, 0)
    wiT = jnp.moveaxis(w_idx.reshape(B, nb, DSA_BLOCK, IDX_HEADS), 1, 0)
    key_chunk = jnp.arange(S) // CHUNK_2

    def block(args):
        blk, qb, qib, wib = args
        t = blk * DSA_BLOCK + jnp.arange(DSA_BLOCK)
        admissible = key_chunk[None, :] <= (t // CHUNK_2)[:, None]
        rel = jax.nn.relu(jnp.einsum('bqhd,bsd->bqhs', qib, k_idx) * IDX_SCALE)
        score = jnp.einsum('bqhs,bqh->bqs', rel, wib * IDX_W_SCALE).astype(jnp.float32)
        score = jnp.where(admissible[None], score, -jnp.inf)
        top_val, top_idx = lax.top_k(score, topk)
        valid = jnp.isfinite(top_val)
        k_sel = jax.vmap(lambda kk, ii: kk[ii])(k, top_idx)
        v_sel = jax.vmap(lambda vv, ii: vv[ii])(v, top_idx)
        logits = jnp.einsum('bqhd,bqkd->bqhk', qb, k_sel).astype(jnp.float32) * ATTN_SCALE_2
        logits = jnp.where(valid[:, :, None, :], logits, -jnp.inf)
        p = jax.nn.softmax(logits, axis=-1)
        return jnp.einsum('bqhk,bqkd->bqhd', p.astype(v.dtype), v_sel)

    outs = lax.map(block, (jnp.arange(nb), qT, qiT, wiT))
    return jnp.moveaxis(outs, 0, 1).reshape(B, S, DSA_W)

def mixer_block(x, w_in, sinks, mu, w0, w_up, a0, a_up, g_up, k_k, k_a, r_k, gn_g, gn_b,
                f_bias, gate_bias, w_branch, w_out):
    B, S, _ = x.shape
    p_swa, p_rwkv, p_fox, p_dsa, p_gate = split_cols(x @ w_in, IN_GROUPS)
    o_swa = swa_branch(*split_cols(p_swa, SWA_SPLITS), sinks)
    o_rwkv = rwkv7_branch(p_rwkv, mu, w0, w_up, a0, a_up, g_up, k_k, k_a, r_k, gn_g, gn_b)
    o_fox = fox_branch(*split_cols(p_fox, FOX_SPLITS), f_bias)
    o_dsa = dsa_branch(*split_cols(p_dsa, DSA_SPLITS))
    gates = jax.nn.sigmoid(p_gate.reshape(B, S, N_BRANCHES, D_MODEL) + gate_bias)
    w_rows = split_cols(w_branch, MIX_WIDTHS, axis=0)
    merged = jnp.zeros_like(x)
    for i, (o, w) in enumerate(zip((o_swa, o_rwkv, o_fox, o_dsa), w_rows)):
        merged = merged + gates[:, :, i] * (o @ w)
    return merged @ w_out

def swiglu_2(x, w1, w3, w2):
    return (jax.nn.silu(x @ w1) * (x @ w3)) @ w2

def moe_ffn(x, router_w, router_b, w1, w3, w2):
    logits = (x @ router_w).astype(jnp.float32) + router_b
    top_val, top_idx = lax.top_k(logits, TOP_K)
    weights = jax.nn.softmax(top_val, axis=-1)
    combine = jnp.sum(jax.nn.one_hot(top_idx, N_EXPERTS, dtype=jnp.float32) * weights[..., None], axis=-2)
    y = jnp.zeros_like(x)
    for e in range(N_EXPERTS):
        y = y + combine[..., e:e + 1].astype(x.dtype) * swiglu_2(x, w1[e], w3[e], w2[e])
    return y

def second_inputs(seed: int = 0) -> dict:
    key = jax.random.key(seed)
    ks = iter(jax.random.split(key, 32))
    nrm = lambda shape, scale: scale * jax.random.normal(next(ks), shape, jnp.float32)
    unif = lambda shape, lo, hi: jax.random.uniform(next(ks), shape, jnp.float32, lo, hi)
    L = DEPTH
    return {
        'x': nrm((BATCH, SEQ, D_MODEL), 1.0),
        'w_in': nrm((L, D_MODEL, D_IN), D_MODEL ** -0.5),
        'swa_sinks': nrm((L, SWA_HEADS), 0.5),
        'rwkv_mu': unif((L, RWKV_IN), 0.0, 1.0),
        'rwkv_w0': unif((L, RWKV_W), -6.0, 1.0),
        'rwkv_w_up': nrm((L, RWKV_W_RANK, RWKV_W), 0.1),
        'rwkv_a0': nrm((L, RWKV_W), 0.1),
        'rwkv_a_up': nrm((L, RWKV_A_RANK, RWKV_W), RWKV_A_RANK ** -0.5),
        'rwkv_g_up': nrm((L, RWKV_G_RANK, RWKV_W), RWKV_G_RANK ** -0.5),
        'rwkv_k_k': 0.85 + nrm((L, RWKV_W), 0.05),
        'rwkv_k_a': 1.0 + nrm((L, RWKV_W), 0.05),
        'rwkv_r_k': nrm((L, RWKV_HEADS, HEAD_DIM), 0.1),
        'rwkv_gn_g': 1.0 + nrm((L, RWKV_W), 0.05),
        'rwkv_gn_b': nrm((L, RWKV_W), 0.02),
        'fox_f_bias': 2.0 + nrm((L, FOX_HEADS), 0.5),
        'gate_bias': nrm((L, N_BRANCHES, D_MODEL), 0.1),
        'w_branch': nrm((L, MIX_WIDTH, D_MODEL), (4 * HEAD_DIM) ** -0.5),
        'w_out': nrm((L, D_MODEL, D_MODEL), DN_BETA * D_MODEL ** -0.5),
        'ln_g': 1.0 + nrm((L, 2, D_MODEL), 0.05),
        'ln_b': nrm((L, 2, D_MODEL), 0.02),
        'ffn_w1': nrm((N_DENSE, D_MODEL, D_FF), D_MODEL ** -0.5),
        'ffn_w3': nrm((N_DENSE, D_MODEL, D_FF), D_MODEL ** -0.5),
        'ffn_w2': nrm((N_DENSE, D_FF, D_MODEL), DN_BETA * D_FF ** -0.5),
        'router_w': nrm((N_MOE, D_MODEL, N_EXPERTS), D_MODEL ** -0.5),
        'router_b': nrm((N_MOE, N_EXPERTS), 0.01),
        'exp_w1': nrm((N_MOE, N_EXPERTS, D_MODEL, D_FF_EXPERT), D_MODEL ** -0.5),
        'exp_w3': nrm((N_MOE, N_EXPERTS, D_MODEL, D_FF_EXPERT), D_MODEL ** -0.5),
        'exp_w2': nrm((N_MOE, N_EXPERTS, D_FF_EXPERT, D_MODEL), DN_BETA * D_FF_EXPERT ** -0.5),
    }

def second_block(x, w_in, swa_sinks, rwkv_mu, rwkv_w0, rwkv_w_up, rwkv_a0, rwkv_a_up, rwkv_g_up,
              rwkv_k_k, rwkv_k_a, rwkv_r_k, rwkv_gn_g, rwkv_gn_b, fox_f_bias, gate_bias, w_branch,
              w_out, ln_g, ln_b, ffn_w1, ffn_w3, ffn_w2, router_w, router_b, exp_w1, exp_w3, exp_w2):
    for layer in range(DEPTH):
        y = mixer_block(x, w_in[layer], swa_sinks[layer], rwkv_mu[layer], rwkv_w0[layer],
                        rwkv_w_up[layer], rwkv_a0[layer], rwkv_a_up[layer], rwkv_g_up[layer],
                        rwkv_k_k[layer], rwkv_k_a[layer], rwkv_r_k[layer], rwkv_gn_g[layer],
                        rwkv_gn_b[layer], fox_f_bias[layer], gate_bias[layer], w_branch[layer],
                        w_out[layer])
        x = layer_norm(DN_ALPHA * x + y, ln_g[layer, 0], ln_b[layer, 0])
        j = layer // 2
        if layer % 2 == 0:
            y = swiglu_2(x, ffn_w1[j], ffn_w3[j], ffn_w2[j])
        else:
            y = moe_ffn(x, router_w[j], router_b[j], exp_w1[j], exp_w3[j], exp_w2[j])
        x = layer_norm(DN_ALPHA * x + y, ln_g[layer, 1], ln_b[layer, 1])
    return x


def setup_inputs(seed=0):
    out = dict(first_inputs(seed))
    for name, value in second_inputs(seed + 1).items():
        if name != "x":
            out[name + "_2"] = value
    return out


def reference(
    x, c, ctx, c_ctx, ada_w, ada_b, norm1_g, norm2_g, ffn_w_in, ffn_w_out, even_w_in,
    even_w_out, sgu_w, sgu_b, diff_lq1, diff_lk1, diff_lq2, diff_lk2, diff_subln_g, odd_w_qkv,
    odd_w_out, odd_sink, final_g, w_in_2, swa_sinks_2, rwkv_mu_2, rwkv_w0_2, rwkv_w_up_2,
    rwkv_a0_2, rwkv_a_up_2, rwkv_g_up_2, rwkv_k_k_2, rwkv_k_a_2, rwkv_r_k_2, rwkv_gn_g_2,
    rwkv_gn_b_2, fox_f_bias_2, gate_bias_2, w_branch_2, w_out_2, ln_g_2, ln_b_2, ffn_w1_2,
    ffn_w3_2, ffn_w2_2, router_w_2, router_b_2, exp_w1_2, exp_w3_2, exp_w2_2,
):
    x = first_block(
        x, c, ctx, c_ctx, ada_w, ada_b, norm1_g, norm2_g, ffn_w_in, ffn_w_out, even_w_in,
        even_w_out, sgu_w, sgu_b, diff_lq1, diff_lk1, diff_lq2, diff_lk2, diff_subln_g,
        odd_w_qkv, odd_w_out, odd_sink, final_g,
    )
    return second_block(
        x, w_in_2, swa_sinks_2, rwkv_mu_2, rwkv_w0_2, rwkv_w_up_2, rwkv_a0_2, rwkv_a_up_2,
        rwkv_g_up_2, rwkv_k_k_2, rwkv_k_a_2, rwkv_r_k_2, rwkv_gn_g_2, rwkv_gn_b_2, fox_f_bias_2,
        gate_bias_2, w_branch_2, w_out_2, ln_g_2, ln_b_2, ffn_w1_2, ffn_w3_2, ffn_w2_2,
        router_w_2, router_b_2, exp_w1_2, exp_w3_2, exp_w2_2,
    )


_drawn_inputs = setup_inputs


def setup_inputs(seed=0):
    import zlib

    import numpy as np

    out = dict(_drawn_inputs(seed))
    spreads = {}
    factors = {'norm1_g': 4.962,
     'norm2_g': 4.889,
     'sgu_b': 2.839,
     'diff_lq1': 8.0,
     'diff_lk1': 2.965,
     'diff_lq2': 2.913,
     'diff_subln_g': 6.918,
     'odd_sink': 8.0,
     'swa_sinks_2': 8.0,
     'rwkv_w_up_2': 4.546,
     'rwkv_a0_2': 8.0,
     'rwkv_k_k_2': 6.424,
     'rwkv_k_a_2': 4.824,
     'rwkv_gn_g_2': 5.117,
     'rwkv_gn_b_2': 8.0,
     'gate_bias_2': 4.828,
     'router_b_2': 5.618}
    for name, (base, spread) in spreads.items():
        noise = np.random.default_rng([zlib.crc32(name.encode()), seed]).standard_normal(out[name].shape)
        drawn = base * np.exp(spread * noise) if base else spread * noise
        out[name] = __import__('jax').numpy.asarray(drawn.astype(out[name].dtype))
    for name, factor in factors.items():
        out[name] = (out[name] * factor).astype(out[name].dtype)
    return out
```

```python
from contextlib import ExitStack

import numpy as np

import concourse.bass as bass
from concourse import mybir

F32 = mybir.dt.float32
U32 = mybir.dt.uint32
ALU = mybir.AluOpType
ACT = mybir.ActivationFunctionType
AX_X = mybir.AxisListType.X

P = 128
D = 1024
KD = D // P
T = 256
TC = 256
TT = T + TC
HD = 64
SCALE = HD ** -0.5
FH = 11
HID = 2 * FH * P
EXPERTS = 8
CHUNK = 8
RING = 11
BANKS = 6
NEG = -1e30
OUT_OF_LIST = -3e38
LAM_INIT = 0.8 - 0.6
BR_K = (4, 2, 2, 2)
UNITS_FFN = 2 * FH + KD
ALPHA = 4.0 ** 0.25

C_SWA, C_RWKV, C_FOX, C_DSA, C_GATE = 0, 768, 1792, 2564, 3272

PARAM_COLS = [
    ("eps6", 1), ("eps5", 1), ("epsgn", 1), ("cvec", 2 * KD),
    ("ada_b0", 48), ("ada_b1", 48), ("n1g0", KD), ("n1g1", KD), ("n2g0", KD), ("n2g1", KD), ("final_g", KD),
    ("sgu_b", 512), ("lqk", 256), ("subln", 1), ("odd_sink", 16), ("sgu_w", 512), ("router_w", 64), ("router_b", 8),
]
for _l in range(2):
    PARAM_COLS += [(f"{n}_{_l}", w) for n, w in (
        ("sinks", 8), ("mu", 8), ("w0", 2), ("a0", 2), ("kk", 2), ("ka", 2), ("rk", 2), ("gng", 2), ("gnb", 2),
        ("fbias", 1), ("gate_b", 32), ("ln1g", 8), ("ln1b", 8), ("ln2g", 8), ("ln2b", 8), ("wa_up", 256), ("g_up", 256))]

CONST_COLS = [
    ("ident", 128), ("mean_d", 128), ("mean_e", 128), ("blk64", 128), ("rot", 128), ("dup0", 128), ("dup1", 128),
    ("cos", 256), ("sin", 256), ("band", 1024), ("swa", 512), ("causal", 512), ("chunks", 512), ("sel8", 1024),
    ("pairmask", 512), ("inv0", 128), ("inv0t", 128), ("levels", 640), ("segs", 256), ("iota8", 8),
]


def offsets(cols):
    at, out = 0, {}
    for name, width in cols:
        out[name] = (at, at + width)
        at += width
    return out, at


PO, NPAR = offsets(PARAM_COLS)
CO, NCON = offsets(CONST_COLS)


def constants():
    c = np.zeros((P, NCON), np.float32)

    def put(name, value):
        a, b = CO[name]
        c[:value.shape[0], a:b] = value.reshape(value.shape[0], -1)

    i, j = np.arange(P)[:, None], np.arange(P)[None, :]
    put("ident", (i == j).astype(np.float32))
    put("mean_d", np.full((P, P), 1.0 / D, np.float32))
    put("mean_e", np.full((P, P), 1.0 / P, np.float32))
    put("blk64", (i // 64 == j // 64).astype(np.float32))
    half = j % 32 < 16
    put("rot", np.where(half & (i == j + 16), -1.0, np.where(~half & (i == j - 16), 1.0, 0.0)).astype(np.float32))
    put("dup0", ((i < 64) & (j % 64 == i)).astype(np.float32))
    put("dup1", ((i >= 64) & (j % 64 == i - 64)).astype(np.float32))
    t = np.arange(T)
    nf = HD // 4
    inv = np.float32(10000.0) ** (-np.arange(nf, dtype=np.float32) / np.float32(nf))
    ang = np.stack([(t // 64).astype(np.float32)[:, None] * inv, (t % 64).astype(np.float32)[:, None] * inv], 1)
    ang = np.broadcast_to(ang[:, :, None, :], (T, 2, 2, nf)).reshape(T, HD).T
    put("cos", np.tile(np.cos(ang), (2, 1)).astype(np.float32))
    put("sin", np.tile(np.sin(ang), (2, 1)).astype(np.float32))

    def mask(allowed, extra=0):
        m = np.zeros((P, 2, T + extra), np.float32)
        for q in range(2):
            m[:, q, :T] = np.where(allowed(q * P + i, np.arange(T)[None, :]), 0.0, NEG)
        return m

    put("band", mask(lambda q, k: np.abs(q - k) <= 128, TC))
    put("swa", mask(lambda q, k: (k // 64 <= q // 64) & (k // 64 >= q // 64 - 2)))
    put("causal", mask(lambda q, k: k <= q))
    put("chunks", mask(lambda q, k: k // 64 <= q // 64))
    put("sel8", np.broadcast_to((np.arange(8)[:, None] == np.arange(8)[None, :])[:, :, None], (8, 8, P)).astype(np.float32))
    same = i // 64 == j // 64
    strict, incl = (same & (i < j)), (same & (i <= j))
    put("pairmask", np.stack([strict, incl, strict, incl], 1).astype(np.float32))
    low = (i // 2 == j // 2) & (i > j)
    put("inv0", -low.astype(np.float32))
    put("inv0t", -low.T.astype(np.float32))
    lev = [((i // (2 * s) == j // (2 * s)) & (i // s < j // s)) for s in (2, 4, 8, 16, 32)]
    put("levels", np.stack(lev, 1).astype(np.float32))
    put("segs", np.broadcast_to((t % 64 != 0).astype(np.float32), (P, T)))
    put("iota8", np.broadcast_to(np.arange(8, dtype=np.float32), (P, 8)))
    return c


def stream_plan():
    blocks = []

    def pad():
        while len(blocks) % CHUNK:
            blocks.append(None)

    def tiles(name, idx, cols, k=KD, row=0, width=P):
        for c in cols:
            for kk in range(k):
                blocks.append((name, idx, row + kk * P, c, width))

    def wide(name, idx, col, n):
        for kk in range(KD):
            for c in range(n):
                blocks.append((name, idx, kk * P, col + c * P, P))

    def ffn(w_up, w_gate_col, w_val, w_val_idx, w_val_col, w_down, idx, didx, row, ada=None):
        for f in range(FH):
            tiles(w_up, idx, [w_gate_col + f * P])
            tiles(w_val, w_val_idx, [w_val_col + f * P])
            if ada is not None:
                tiles("ada_w", (1,), [(ada * 2 * FH + 2 * f) * P, (ada * 2 * FH + 2 * f + 1) * P])
        for j in range(KD):
            tiles(w_down, didx, [j * P], FH, row)

    tiles("ada_w", (0,), [j * P for j in range(16)])
    tiles("even_w_in", (0,), [j * P for j in (*range(4), *range(8, 16))])
    wide("even_w_in", (0,), 512, 4)
    wide("even_w_in", (0,), 2048, 4)
    tiles("ada_w", (0,), [j * P for j in range(16, 48)])
    tiles("even_w_out", (0,), [j * P for j in range(KD)])
    for half in range(2):
        ffn("ffn_w_in", half * FH * P, "ffn_w_in", (0,), HID + half * FH * P, "ffn_w_out", (0,), (0,), half * FH * P, half)
    tiles("ada_w", (1,), [j * P for j in range(44, 48)])
    tiles("odd_w_qkv", (0,), [j * P for j in range(10)])
    wide("odd_w_qkv", (0,), 1280, 2)
    tiles("odd_w_out", (0,), [j * P for j in range(KD)])
    for half in range(2):
        ffn("ffn_w_in", half * FH * P, "ffn_w_in", (1,), HID + half * FH * P, "ffn_w_out", (1,), (1,), half * FH * P)
    for l in range(2):
        w = "w_in_2"
        tiles(w, (l,), [C_SWA + j * P for j in range(5)] + [C_RWKV + j * P for j in range(8)]
              + [C_FOX + j * P for j in range(4)] + [C_DSA, C_DSA + P, C_DSA + 384, C_DSA + 512])
        for kk in range(KD):
            blocks.append((w, (l,), kk * P, (C_DSA + 256, C_DSA + 640), 64))
        tiles(w, (l,), [C_FOX + 768], width=4)
        tiles(w, (l,), [C_SWA + 640])
        for kk in range(KD):
            blocks.append((w, (l,), kk * P, (C_DSA + 320, C_DSA + 704), (64, 4)))
        wide(w, (l,), C_FOX + 512, 2)
        for j in range(KD):
            row = 0
            for i in range(4):
                tiles(w, (l,), [C_GATE + i * D + j * P])
                tiles("w_branch_2", (l,), [j * P], BR_K[i], row)
                row += BR_K[i] * P
        pad()
        tiles("w_out_2", (l,), [j * P for j in range(KD)])
        if l == 0:
            for half in range(2):
                c = half * FH * P
                ffn("ffn_w1_2", c, "ffn_w3_2", (0,), c, "ffn_w2_2", (0,), (0,), c)
        else:
            for e in range(EXPERTS):
                ffn("exp_w1_2", 0, "exp_w3_2", (0, e), 0, "exp_w2_2", (0, e), (0, e), 0)
    while len(blocks) % (CHUNK * RING):
        blocks.append(None)
    return blocks


def build(nc, stream, params, consts, xin, out):
    rounds = stream.shape[0] // RING
    with ExitStack() as ctx:
        def sb(name, *shape, dt=F32):
            return ctx.enter_context(nc.sbuf_tensor(name, [P, *shape], dt))

        def sem(name):
            return ctx.enter_context(nc.semaphore(name))

        ring = sb("ring", RING, CHUNK * P)
        X = sb("X", KD, TT)
        A = sb("A", KD, TT)
        par = sb("par", NPAR)
        con = sb("con", NCON)
        S = sb("S", 23600)
        smalls = sb("smalls", 160)
        mod = sb("mod", 2, 48, 2)
        modg = sb("modg", 4, KD, 2)
        idx8 = sb("idx8", 2, 8, dt=U32)

        bank = [ctx.enter_context(nc.psum_tensor(f"bank{i}", [P, 512], F32)) for i in range(8)]
        NORM, ADA = bank[6], bank[7]
        MEAN = bank[7]

        def pr(name, a=0, b=None):
            lo, hi = PO[name]
            return par[:, lo + a:(hi if b is None else lo + b)]

        def cn(name, a=0, b=None):
            lo, hi = CO[name]
            return con[:, lo + a:(hi if b is None else lo + b)]

        def view(at, *shape):
            n = int(np.prod(shape))
            assert at + n <= 23600
            v = S[:, at:at + n]
            if len(shape) == 2:
                v = v.rearrange("p (a b) -> p a b", a=shape[0])
            if len(shape) == 3:
                v = v.rearrange("p (a b c) -> p a b c", a=shape[0], b=shape[1])
            return v

        def small(at, n):
            return smalls[:, at:at + n]

        def over(ap, n):
            return ap.unsqueeze(1).broadcast_to([P, n, ap.shape[1]])

        ident, sel8 = cn("ident"), cn("sel8").rearrange("p (e c) -> p e c", e=8)

        SQ = view(18432 - 4096, KD, TT)
        H = view(0, FH, TT)
        TMP = view(6144, 2, TT)
        CW = view(10240, EXPERTS, T)
        RS = view(18432, TT)
        AT = 18432
        SM = view(AT, 2, 512)
        E = view(AT + 1024, 4, 512)
        ET = view(AT + 3072, 2, 512)
        mx, nm, sm, es, rc, r2 = (small(4 * n, 4) for n in range(6))
        nsink = small(24, 32)
        lam = small(60, 8)
        cs = small(70, 16)
        Q0, K0, U0, VG, VV = (view(2048 * n, 4, TT) for n in range(5))
        CAT0 = view(10240, KD, TT)
        VT = view(14336, 4, TT)
        ST6 = view(AT, 16, 6)
        MV2 = view(AT + 96, 16, 2)
        VRS = view(AT + 128, 16)
        RT1 = view(AT + 1024, 2, T)
        Q1, K1, KD1, V1 = view(0, KD, T), view(2048, 2, TT), view(3072, 4, TT), view(5120, 4, T)
        CAT1 = view(10240, KD, T)
        SQ_, SK, SKD = view(0, 4, T), view(1024, 1, T), view(1280, 2, T)
        FQ, FK, DQ, DQI = view(1792, 2, T), view(2304, 2, T), view(2816, 2, T), view(3328, 2, T)
        DKI, DKD, DKID, FC = view(3840, 1, T), view(4096, 1, T), view(4352, 1, T), view(4608, 4, T)
        SV, FV, DV = view(5632, 2, P), view(5888, 2, T), view(6400, 2, 68)
        RP = view(6656, KD, T)
        DSC, DWK, DMK, DT = view(8704, T), view(8960, T), view(9216, 2, T), view(9728, T)
        CAT2 = A[:, :, :].rearrange("p a b -> p (a b)")[:, 0:2560].rearrange("p (a b) -> p a b", a=10)
        W0 = 8704
        (SHD, LWV, AV, GV, CC, CX, KK, EC, EN, EX) = (view(W0 + 512 * n, 2, T) for n in range(10))
        DELTA = view(W0, KD, T)
        KNORM, RKK, BON = CX, SHD, view(W0 + 5120, 2, T)
        KR = view(W0 + 5632, 2, 2, T)
        BH, KH = view(W0 + 6656, 2, T), view(W0 + 7168, 2, T)
        LOW = view(W0 + 7680, 2, T)
        TOK = [view(W0 + 8192 + 512 * n, 2, T) for n in range(4)]
        MM = view(W0 + 10240, 8, 512)
        XX = view(0, 8, 256)
        LK = view(2048, 8, P)
        PP = view(3072, 8, P)
        MVS, U0N, GTN = view(4096, 8, 64), view(4608, 8, 64), view(5120, 4, P)
        SA = view(5632, 4, 64)
        STATE = view(5888, 5, P)
        YT = view(W0 + 5632, 2, T)
        YC, YS = view(W0 + 6656, 2, T), view(W0 + 7168, 2, T)
        ACC = view(0, KD, T)
        GATE, PROD = view(2048, 2, T), view(2560, 2, T)
        LG, M8, EE = small(90, 16), small(106, 16), small(122, 8)
        IDXF, CWT = small(130, 4), view(W0, 2, 8)
        CWR, OH = view(W0 + 64, T), view(W0 + 320, 2, 8)

        w_loaded = [sem(f"w_loaded{i}") for i in range(RING)]
        w_free = sem("w_free")
        inputs_in = sem("inputs_in")
        gemm_done, gemm_free = sem("gemm_done"), sem("gemm_free")
        act_tmp, cw_done = sem("act_tmp"), sem("cw_done")
        silu_c = sem("silu_c")
        ada_done, mod_ready = sem("ada_done"), sem("mod_ready")
        n_sq, n_mm, n_root, n_x, n_a = sem("norm_sq"), sem("norm_mm"), sem("norm_root"), sem("norm_x"), sem("norm_a")
        n_mean, n_c = sem("norm_mean"), sem("norm_centred")
        dve_chain, act_chain = sem("dve_chain"), sem("act_chain")
        at_s, at_m, at_e, at_n = sem("att_scores"), sem("att_max"), sem("att_exp"), sem("att_normed")
        at_t, at_tv, at_o, at_out = sem("att_turned"), sem("att_turned_copy"), sem("att_pv"), sem("att_out")
        lam_sum, lam_exp = sem("lam_sum"), sem("lam_exp")
        gelu_v, v_var, v_root, v_normed = sem("gelu_v"), sem("v_var"), sem("v_root"), sem("v_normed")
        ready = sem("ready")
        diff_sq, diff_var, diff_root = sem("diff_sq"), sem("diff_var"), sem("diff_root")
        fox_pre, fox_e, fox_ln = sem("fox_pre"), sem("fox_exp"), sem("fox_log")
        rw_shift, rw_low, rw_pre, rw_sig = sem("rw_shift"), sem("rw_low"), sem("rw_pre"), sem("rw_sig")
        rw_c, rw_exp, rw_ks, rw_kroot = sem("rw_c"), sem("rw_exp"), sem("rw_ks"), sem("rw_kroot")
        rw_var, rw_vroot = sem("rw_var"), sem("rw_vroot")
        top_v, top_e = sem("top_v"), sem("top_e")
        out_done = sem("out_done")

        def keys(kap, n0, n1):
            return lambda base, h: kap(h)[base:base + HD, n0:n1]

        def unit(q, k, nk, mask, sink, vals, dst, last=True, bias=None):
            return dict(q=q, k=k, nk=nk, mask=mask, sink=sink, vals=vals, dst=dst, last=last, bias=bias)

        def units_even():
            us = []
            for half in range(2):
                k0 = half * T
                for h in range(4):
                    for qt in range(2):
                        q0 = half * T + qt * P
                        for s in range(2):
                            b = s * HD
                            us.append(unit(Q0[b:b + HD, h, q0:q0 + P], K0[b:b + HD, h, k0:TT], TT - k0, None, None,
                                           [VV[:, t, h * P:(h + 1) * P] for t in range(2 * half, 4)],
                                           CAT0[:, 4 + h, q0:q0 + P], last=s == 1))
            return us

        def units_odd():
            us = []
            for h in range(16):
                b, kv = (h % 2) * HD, h // 4
                for qt in range(2):
                    us.append(unit(Q1[b:b + HD, h // 2, qt * P:(qt + 1) * P], KD1[b:b + HD, kv, :], TT,
                                   cn("band", qt * TT, (qt + 1) * TT), h,
                                   [V1[:, t, kv * HD:(kv + 1) * HD] for t in range(4)],
                                   CAT1[b:b + HD, h // 2, qt * P:(qt + 1) * P]))
            return us

        def units_second(l):
            us = []
            for h in range(8):
                b, kv = (h % 2) * HD, h // 4
                for qt in range(2):
                    nk = (qt + 1) * P
                    us.append(unit(SQ_[b:b + HD, h // 2, qt * P:nk], SKD[b:b + HD, kv, 0:nk], nk,
                                   cn("swa", qt * T, qt * T + nk), h,
                                   [SV[:, t, kv * HD:(kv + 1) * HD] for t in range(qt + 1)],
                                   CAT2[b:b + HD, h // 2, qt * P:nk]))
            for h in range(4):
                b = (h % 2) * HD
                for qt in range(2):
                    nk = (qt + 1) * P
                    us.append(unit(FQ[b:b + HD, h // 2, qt * P:nk], FK[b:b + HD, h // 2, 0:nk], nk,
                                   cn("causal", qt * T, qt * T + nk), None,
                                   [FV[:, t, h * HD:(h + 1) * HD] for t in range(qt + 1)],
                                   CAT2[b:b + HD, 6 + h // 2, qt * P:nk], bias=(h, qt)))
            for h in range(4):
                b = (h % 2) * HD
                for qt in range(2):
                    nk = (qt + 1) * P
                    us.append(unit(DQ[b:b + HD, h // 2, qt * P:nk], DKD[b:b + HD, 0, 0:nk], nk,
                                   DMK[:, qt, 0:nk], None, [DV[:, t, 0:HD] for t in range(qt + 1)],
                                   CAT2[b:b + HD, 8 + h // 2, qt * P:nk]))
            return us

        def groups(us):
            g, out_ = 0, []
            for u in us:
                out_.append(g)
                g += u["last"]
            return out_, g

        def head_cols(m):
            h = 2 * (m % 2) + m // 4
            return slice(h * 64, (h + 1) * 64)

        block = ctx.enter_context(nc.Block())

        @block.sync
        def _(sp):
            sp.dma_start(par[:, :], params).then_inc(inputs_in, 16)
            for s in range(RING):
                sp.dma_start(ring[:, s, :], stream[s]).then_inc(w_loaded[s], 16)
                if s == 0:
                    sp.dma_start(X[:, :, :], xin).then_inc(inputs_in, 16)
                    sp.dma_start(con[:, :], consts).then_inc(inputs_in, 16)
            with sp.Fori(1, rounds) as r:
                for s in range(RING):
                    sp.wait_ge(w_free, r * RING + (s - RING + 2))
                    sp.dma_start(ring[:, s, :], stream[r * RING + s]).then_inc(w_loaded[s], 16)
            sp.wait_ge(n_a, 8 * 9)
            sp.dma_start(out, X[:, :, 0:T]).then_inc(out_done, 16)
            sp.wait_ge(out_done, 16)

        @block.tensor
        def _(pe):
            st = dict(n=0, u=0, a=0, g=0, free=False, i=None, per_u=0, per_r=0, ada=0, ready=0)

            def val(x, per):
                return x if st["i"] is None else st["i"] * per + x

            def weight(n, signal=True):
                slot, c = (n // CHUNK) % RING, n % CHUNK
                if c == 0:
                    pe.wait_ge(w_loaded[slot], val(16 * (n // CHUNK // RING + 1), 16 * st["per_r"]))
                    st["free"] = st["free"] or signal
                return ring[:, slot, c * P:(c + 1) * P]

            def mm(o, l, r, start, stop, end=False, sig=True):
                ins = pe.matmul(o, l, r, start=start, stop=stop)
                if end:
                    ins.then_inc(gemm_done, 1)
                elif st["free"] and sig:
                    ins.then_inc(w_free, 1)
                    st["free"] = False
                return ins

            def unit_begin():
                u = st["u"]
                if u >= BANKS:
                    pe.wait_ge(gemm_free, val(u - BANKS + 1, st["per_u"]))
                st["u"] += 1
                return bank[u % BANKS]

            def tile(rhs, k, tt, m=P):
                b = unit_begin()
                for kk in range(k):
                    w = weight(st["n"])
                    mm(b[0:m, 0:tt], w[:, 0:m], rhs(kk), kk == 0, kk == k - 1, kk == k - 1)
                    st["n"] += 1

            def tok_tiles(src, tiles, n):
                n0 = st["n"]
                for t in range(tiles):
                    b = unit_begin()
                    for kk in range(KD):
                        w = weight(n0 + kk * n, signal=t == tiles - 1)
                        slot, c = ((n0 + kk * n) // CHUNK) % RING, (n0 + kk * n) % CHUNK
                        w = ring[:, slot, c * P:(c + n) * P]
                        mm(b[:, 0:n * P], src(kk, t), w, kk == 0, kk == KD - 1, kk == KD - 1)
                st["n"] = n0 + KD * n

            def skip_to_chunk():
                st["n"] += -st["n"] % CHUNK

            def ada_tile(col):
                for kk in range(KD):
                    w = weight(st["n"])
                    mm(col, w, cs[:, 2 * kk:2 * kk + 2], kk == 0, kk == KD - 1, sig=kk < KD - 1 or True)
                    st["n"] += 1

            def ada_end():
                pe.matmul(NORM[0:2, 0:2], cs[:, 0:2], cs[:, 0:2], start=True, stop=True).then_inc(ada_done, 1)

            def small_unit(pairs, tt, m=P):
                b = unit_begin()
                for j, (o, l, r, s, e) in enumerate(pairs(b)):
                    mm(o, l, r, s, e, j == len(pairs(b)) - 1)

            def dup_unit(lhs, rhs, tt):
                b = unit_begin()
                mm(b[:, 0:tt], lhs, rhs, True, True, True)

            def norm(ni, tt, layer_norm=False):
                if layer_norm:
                    pe.wait_ge(gemm_free, st["u"])
                    for j in range(KD):
                        ins = pe.matmul(MEAN[:, 0:tt], cn("mean_d"), X[:, j, 0:tt], start=j == 0, stop=j == KD - 1)
                    ins.then_inc(n_mean, 1)
                for j in range(KD):
                    pe.wait_ge(n_sq, KD * ni + j + 1)
                    ins = pe.matmul(NORM[:, 0:tt], cn("mean_d"), SQ[:, j, 0:tt], start=j == 0, stop=j == KD - 1)
                ins.then_inc(n_mm, 1)

            def attention(us, extra=None):
                gs, ng = groups(us)
                a0, g0 = st["a"], st["g"]
                for s in range(len(us) + 3):
                    if s < len(us):
                        u = us[s]
                        if s >= 2:
                            pe.wait_ge(at_e, a0 + s - 1)
                        b = bank[s % 2]
                        ins = pe.matmul(b[:, 0:u["nk"]], u["q"], u["k"], start=True, stop=u["bias"] is None)
                        if u["bias"] is not None:
                            h, qt = u["bias"]
                            pe.matmul(b[:, 0:u["nk"]], sel8[0:4, h, :], FC[0:4, 1, 0:u["nk"]], start=False, stop=False)
                            for kt in range(qt + 1):
                                ins = pe.matmul(b[:, kt * P:(kt + 1) * P], FC[0:4, 0, qt * P:(qt + 1) * P],
                                                sel8[0:4, h, :], start=False, stop=kt == qt)
                        ins.then_inc(at_s, 1)
                    if extra is not None and s < len(us):
                        extra(s)
                    if 2 <= s < len(us) + 2 and us[s - 2]["last"]:
                        u, g = us[s - 2], gs[s - 2]
                        pe.wait_ge(at_n, a0 + s - 1)
                        if g >= 2:
                            pe.wait_ge(at_tv, g0 + g - 1)
                        for kt in range(u["nk"] // P):
                            ins = pe.transpose(bank[2 + g % 2][:, kt * P:(kt + 1) * P],
                                               E[:, (a0 + s - 2) % 4, kt * P:(kt + 1) * P], ident)
                        ins.then_inc(at_t, 1)
                    if s >= 3 and us[s - 3]["last"]:
                        u, g = us[s - 3], gs[s - 3]
                        pe.wait_ge(at_tv, g0 + g + 1)
                        if g >= 2:
                            pe.wait_ge(at_out, g0 + g - 1)
                        b, m = u["dst"].base_partition(), u["dst"].shape[0]
                        for kt, v in enumerate(u["vals"]):
                            ins = pe.matmul(bank[4 + g % 2][b:b + m, 0:P], v, ET[:, g % 2, kt * P:(kt + 1) * P],
                                            start=kt == 0, stop=kt == len(u["vals"]) - 1)
                        ins.then_inc(at_o, 1)
                st["a"] += len(us)
                st["g"] += ng
                pe.wait_ge(at_out, st["g"])

            def ready_wait():
                st["ready"] += 1
                pe.wait_ge(ready, st["ready"])

            def ffn(count, tt, src, ada=False):
                skip_to_chunk()
                per = (2 * FH * KD + KD * FH + (2 * FH * KD if ada else 0))
                n0, u0 = st["n"], st["u"]
                with pe.Fori(0, count) as i:
                    st["i"], st["per_u"], st["per_r"] = i, UNITS_FFN, per // CHUNK // RING
                    for f in range(FH):
                        tile(lambda kk: src[:, kk, 0:tt], KD, tt)
                        tile(lambda kk: src[:, kk, 0:tt], KD, tt)
                        if ada:
                            for e in range(2):
                                ada_tile(ADA[:, bass.ds(i * (4 * FH) + (4 * f + 2 * e), 2)])
                    pe.wait_ge(gemm_free, val(u0 + 2 * FH, UNITS_FFN))
                    for j in range(KD):
                        tile(lambda kk: H[:, kk, 0:tt], FH, tt)
                    assert st["n"] - n0 == per and per % (CHUNK * RING) == 0
                st["i"] = None
                st["n"], st["u"] = n0 + count * per, u0 + count * UNITS_FFN

            pe.wait_ge(silu_c, 1)
            for j in range(16):
                ada_tile(ADA[:, 2 * j:2 * j + 2])
            ada_end()
            norm(0, TT)
            for j in range(12):
                if j == 0:
                    for kk in range(KD):
                        pass
                    pe.wait_ge(n_a, 8)
                tile(lambda kk: A[:, kk, :], KD, TT)
            tok_tiles(lambda kk, t: A[:, kk, t * P:(t + 1) * P], 4, 4)
            tok_tiles(lambda kk, t: A[:, kk, t * P:(t + 1) * P], 4, 4)
            u_q = 4
            for j in range(8):
                t = (Q0 if j < 4 else K0)[:, j % 4, 0:T]
                pe.wait_ge(gemm_free, u_q + j + 1)
                dup_unit(cn("rot"), t, T)
            pe.wait_ge(v_normed, 1)
            for t in range(4):
                b = unit_begin()
                for g in range(4):
                    mm(b[:, g * P:(g + 1) * P], VG[:, t, g * P:(g + 1) * P], pr("sgu_w", g * P, (g + 1) * P),
                       True, True, g == 3)
            ready_wait()
            attention(units_even(), lambda s: ada_tile(ADA[:, 32 + 2 * s:34 + 2 * s]))
            ada_end()
            for h in range(4):
                pe.wait_ge(diff_sq, h + 1)
                dup_unit(cn("mean_e"), SQ[:, h, :], TT)
            ready_wait()
            for j in range(KD):
                tile(lambda kk: CAT0[:, kk, :], KD, TT)
            norm(1, TT)
            pe.wait_ge(n_a, 16)
            ffn(2, TT, A, ada=True)
            for j in range(44, 48):
                ada_tile(ADA[:, 2 * j:2 * j + 2])
            ada_end()

            norm(2, TT)
            pe.wait_ge(n_a, 24)
            u_q = st["u"]
            for j in range(10):
                tt = T if j < 8 else TT
                tile(lambda kk: A[:, kk, 0:tt], KD, tt)
            tok_tiles(lambda kk, t: A[:, kk, t * P:(t + 1) * P], 4, 2)
            for j in range(10):
                t = Q1[:, j, :] if j < 8 else K1[:, j - 8, 0:T]
                pe.wait_ge(gemm_free, u_q + j + 1)
                dup_unit(cn("rot"), t, T)
            ready_wait()
            for kv in range(4):
                dup_unit(cn(f"dup{kv % 2}"), K1[:, kv // 2, :], TT)
            ready_wait()
            attention(units_odd())
            ready_wait()
            for j in range(KD):
                tile(lambda kk: CAT1[:, kk, :], KD, T)
            norm(3, T)
            pe.wait_ge(n_a, 32)
            ffn(2, T, A)
            norm(4, T)
            pe.wait_ge(n_a, 40)

            for l in range(2):
                for j in range(22):
                    tile(lambda kk: X[:, kk, 0:T], KD, T)
                tile(lambda kk: X[:, kk, 0:T], KD, T, m=4)
                tok_tiles(lambda kk, t: X[:, kk, t * P:(t + 1) * P], 2, 1)
                tok_tiles(lambda kk, t: X[:, kk, t * P:(t + 1) * P], 2, 1)
                tok_tiles(lambda kk, t: X[:, kk, t * P:(t + 1) * P], 2, 2)
                ready_wait()
                dup_unit(cn("dup0"), SK[:, 0, :], T)
                dup_unit(cn("dup1"), SK[:, 0, :], T)
                dup_unit(cn("dup0"), DKI[:, 0, :], T)
                dup_unit(cn("dup1"), DKI[:, 0, :], T)
                ready_wait()
                for qt in range(2):
                    for h in range(4):
                        b = (h % 2) * HD
                        dup_unit(DQI[b:b + HD, h // 2, qt * P:(qt + 1) * P], DKID[b:b + HD, 0, :], T)
                ready_wait()
                attention(units_second(l))

                pe.wait_ge(rw_low, l + 1)
                for j in range(2):
                    dup_unit(pr(f"wa_up_{l}", j * P, (j + 1) * P)[0:64], LOW[0:64, 0, :], T)
                for j in range(2):
                    dup_unit(pr(f"wa_up_{l}", j * P, (j + 1) * P)[64:128], RP[64:128, 6, :], T)
                for j in range(2):
                    dup_unit(pr(f"g_up_{l}", j * P, (j + 1) * P), LOW[:, 1, :], T)
                ready_wait()
                b = unit_begin()
                mm(b[:, :], cn("blk64"), KNORM[:, :, :].rearrange("p a b -> p (a b)"), True, True, True)
                b = unit_begin()
                mm(b[:, :], cn("blk64"), RKK[:, :, :].rearrange("p a b -> p (a b)"), True, True, True)
                ready_wait()
                for src in (lambda j: KR[:, j, 0, :], lambda j: BH[:, j, :], lambda j: KH[:, j, :], lambda j: RP[:, 4 + j, :]):
                    b = unit_begin()
                    for cp in range(2):
                        for j in range(2):
                            ins = pe.transpose(b[:, (2 * cp + j) * P:(2 * cp + j + 1) * P], src(j)[:, cp * P:(cp + 1) * P], ident)
                    ins.then_inc(gemm_done, 1)
                for m in range(8):
                    b0, cp, j = m // 4 * HD, m // 2 % 2, m % 2
                    tok = slice(cp * P, (cp + 1) * P)
                    b = unit_begin()
                    rhs = KR[b0:b0 + HD, j, :, tok]
                    mm(b[:, 0:256].rearrange("p (a b) -> p a b", a=2), BH[b0:b0 + HD, j, tok], rhs, True, True)
                    mm(b[:, 256:512].rearrange("p (a b) -> p a b", a=2), KH[b0:b0 + HD, j, tok], rhs, True, True, True)
                for par in range(2):
                    b = unit_begin()
                    for h in range(4):
                        b0, cp, j = par * HD, h // 2, h % 2
                        tok = slice(cp * P, (cp + 1) * P)
                        mm(b[:, h * P:(h + 1) * P], KR[b0:b0 + HD, j, 0, tok], BH[b0:b0 + HD, j, tok], True, True, h == 3)
                for lev in range(5):
                    ready_wait()
                    for q in range(2):
                        b = unit_begin()
                        for h in range(4):
                            m = 4 * q + h
                            mm(b[:, h * P:(h + 1) * P], LK[:, m, :], XX[:, m, 0:P], True, True, h == 3)
                    ready_wait()
                    for q in range(4):
                        b = unit_begin()
                        for h in range(2):
                            m = 2 * q + h
                            mm(b[:, 2 * h * P:(2 * h + 1) * P], XX[:, m, P:2 * P], PP[:, m, :], True, True)
                            mm(b[:, (2 * h + 1) * P:(2 * h + 2) * P], PP[:, m, :], XX[:, m, P:2 * P], True, True, h == 1)
                ready_wait()
                b = unit_begin()
                for m in range(8):
                    mm(b[:, m * 64:(m + 1) * 64], MM[:, m, 256:384], TOK[3][:, m // 2 % 2, head_cols(m)],
                       True, True, m == 7)
                b = unit_begin()
                for m in range(8):
                    b0, cp, j = m // 4 * HD, m // 2 % 2, m % 2
                    mm(b[b0:b0 + HD, (2 * cp + j) * P:(2 * cp + j + 1) * P], TOK[0][:, cp, head_cols(m)],
                       XX[:, m, P:2 * P], True, True, m == 7)
                ready_wait()
                b = unit_begin()
                for m in range(8):
                    mm(b[:, m * 64:(m + 1) * 64], XX[:, m, P:2 * P], MVS[:, m, :], True, True, m == 7)
                ready_wait()
                for c in range(4):
                    cp, rb = c // 2, (c % 2) * 64
                    if c:
                        ready_wait()
                    for par in range(2):
                        b, b0 = unit_begin(), par * HD
                        for j in range(2):
                            mm(b[rb:rb + 64, j * 64:(j + 1) * 64], GTN[b0:b0 + HD, 2 * cp + j, rb:rb + 64],
                               STATE[b0:b0 + HD, c, j * 64:(j + 1) * 64], True, True, j == 1)
                    ready_wait()
                    b = unit_begin()
                    for n in range(4):
                        b0, j = n // 2 * HD, n % 2
                        o, hc = b[b0:b0 + HD, j * 64:(j + 1) * 64], head_cols(4 * (n // 2) + j)
                        mm(o, TOK[1][rb:rb + 64, cp, hc], SA[rb:rb + 64, n, :], True, False)
                        mm(o, TOK[2][rb:rb + 64, cp, hc], TOK[3][rb:rb + 64, cp, hc], False, True, n == 3)
                    b = unit_begin()
                    for n in range(4):
                        b0, j = n // 2 * HD, n % 2
                        mm(b[b0:b0 + HD, j * 64:(j + 1) * 64], STATE[b0:b0 + HD, c, j * 64:(j + 1) * 64],
                           KR[b0:b0 + HD, j, 1, c * 64:(c + 1) * 64], True, True, n == 3)
                    b = unit_begin()
                    for n in range(4):
                        b0, j = n // 2 * HD, n % 2
                        m = 4 * (n // 2) + 2 * cp + j
                        o = b[b0:b0 + HD, j * 64:(j + 1) * 64]
                        mm(o, SA[rb:rb + 64, n, :], MM[rb:rb + 64, m, 128 + rb:192 + rb], True, False)
                        mm(o, TOK[3][rb:rb + 64, cp, head_cols(m)], MM[rb:rb + 64, m, 384 + rb:448 + rb],
                           False, True, n == 3)
                ready_wait()
                dup_unit(cn("blk64"), YT[:, :, :].rearrange("p a b -> p (a b)"), 512)
                ready_wait()
                dup_unit(cn("blk64"), YS[:, :, :].rearrange("p a b -> p (a b)"), 512)
                ready_wait()

                for j in range(KD):
                    kb = 0
                    for i in range(4):
                        tile(lambda kk: X[:, kk, 0:T], KD, T)
                        tile(lambda kk: CAT2[:, kb + kk, :], BR_K[i], T)
                        kb += BR_K[i]
                skip_to_chunk()
                ready_wait()
                for j in range(KD):
                    tile(lambda kk: ACC[:, kk, :], KD, T)
                ready_wait()
                norm(5 + 2 * l, T, layer_norm=True)
                pe.wait_ge(n_a, 8 * (6 + 2 * l))
                if l == 1:
                    rw = pr("router_w").rearrange("p (k e) -> p k e", k=KD)
                    for t in range(2):
                        b = unit_begin()
                        for kk in range(KD):
                            mm(b[:, 0:8], X[:, kk, t * P:(t + 1) * P], rw[:, kk, :], kk == 0, kk == KD - 1, kk == KD - 1)
                    ready_wait()
                    b = unit_begin()
                    for t in range(2):
                        ins = pe.transpose(b[0:8, t * P:(t + 1) * P], CWT[:, t, :], ident)
                    ins.then_inc(gemm_done, 1)
                    ready_wait()
                    for e in range(EXPERTS):
                        dup_unit(sel8[0:8, e, :], CWR[0:8, :], T)
                    ready_wait()
                ready_wait()
                ffn(2 if l == 0 else EXPERTS, T, A)
                norm(6 + 2 * l, T, layer_norm=True)
                if l == 0:
                    pe.wait_ge(n_a, 8 * 7)

        @block.scalar
        def _(act):
            st = dict(u=0, a=0, g=0, tmp=0)

            def f(o, i, fn, **kw):
                return nc.scalar.activation(o, i, fn, **kw)

            def norm(ni, tt, src, dst, scale, shift, eps):
                for j in range(KD):
                    if ni >= 5:
                        act.wait_ge(n_c, KD * (ni - 5) + j + 1)
                    f(SQ[:, j, 0:tt], src[:, j, 0:tt], ACT.Square).then_inc(n_sq, 1)
                act.wait_ge(n_mm, ni + 1)
                f(RS[:, 0:tt], NORM[:, 0:tt], ACT.Sqrt, bias=eps).then_inc(n_root, 1)
                for j in range(KD):
                    act.wait_ge(n_x, KD * ni + j + 1)
                    for s in range(tt // T):
                        d = dst[:, j, s * T:(s + 1) * T]
                        if shift is None:
                            ins = f(d, d, ACT.Copy, scale=scale(j, s))
                        else:
                            ins = f(d, d, ACT.Identity, scale=scale(j, s), bias=shift(j, s))
                    ins.then_inc(n_a, 1)

            def attention(us):
                gs, ng = groups(us)
                a0, g0 = st["a"], st["g"]
                for s in range(len(us) + 2):
                    if s < len(us):
                        u, a = us[s], a0 + s
                        act.wait_ge(at_m, a + 1)
                        if s >= 4:
                            if us[s - 4]["last"]:
                                act.wait_ge(at_t, g0 + gs[s - 4] + 1)
                            else:
                                act.wait_ge(at_n, a - 2)
                        src = bank[s % 2][:, 0:u["nk"]] if u["mask"] is None else SM[:, a % 2, 0:u["nk"]]
                        c = slice(a % 4, a % 4 + 1)
                        ins = f(E[:, a % 4, 0:u["nk"]], src, ACT.Exp, bias=nm[:, c], scale=SCALE, accum_out=sm[:, c])
                        if u["sink"] is not None:
                            ins = f(es[:, c], SINK(u["sink"]), ACT.Exp, bias=nm[:, c])
                        ins.then_inc(at_e, 1)
                    if s >= 2 and us[s - 2]["last"]:
                        u, g = us[s - 2], gs[s - 2]
                        act.wait_ge(at_t, g0 + g + 1)
                        if g >= 2:
                            act.wait_ge(at_o, g0 + g - 1)
                        f(ET[:, g % 2, 0:u["nk"]], bank[2 + g % 2][:, 0:u["nk"]], ACT.Copy).then_inc(at_tv, 1)
                st["a"] += len(us)
                st["g"] += ng

            def ffn(count, tt):
                u0, t0 = st["u"], st["tmp"]
                with act.Fori(0, count) as i:
                    for q in range(FH):
                        u = u0 + 2 * q
                        act.wait_ge(gemm_done, i * UNITS_FFN + (u + 1))
                        act.wait_ge(gemm_free, i * UNITS_FFN + (u0 - KD if q < 2 else u - 2))
                        f(TMP[:, q % 2, 0:tt], bank[u % BANKS][:, 0:tt], ACT.Silu).then_inc(act_tmp, 1)
                st["u"], st["tmp"] = u0 + count * UNITS_FFN, t0 + count * FH

            act.wait_ge(inputs_in, 48)
            f(cs, pr("cvec"), ACT.Silu).then_inc(silu_c, 1)
            norm_mod = lambda l, n: (lambda j, s: modg[:, 2 * l + n, j, s:s + 1])
            norm_sh = lambda l, n: (lambda j, s: mod[:, l, 24 * n + j, s:s + 1])
            norm(0, TT, X, A, norm_mod(0, 0), norm_sh(0, 0), pr("eps6"))
            for j in range(4):
                act.wait_ge(gemm_free, j + 1)
                f(U0[:, j, :], U0[:, j, :], ACT.Gelu)
            for t in range(4):
                act.wait_ge(gemm_free, 12 + t + 1)
                f(VT[:, t, :], VT[:, t, :], ACT.Gelu).then_inc(gelu_v, 1)
            act.wait_ge(v_var, 1)
            f(VRS, VRS, ACT.Sqrt, bias=pr("eps6")).then_inc(v_root, 1)
            act.wait_ge(lam_sum, 1)
            f(lam[:, 2:4], lam[:, 0:2], ACT.Exp).then_inc(lam_exp, 1)
            st["u"] = 20
            attention(units_even())
            for h in range(4):
                act.wait_ge(at_out, 8 + 2 * (h + 1))
                f(SQ[:, h, :], CAT0[:, 4 + h, :], ACT.Square).then_inc(diff_sq, 1)
            act.wait_ge(diff_var, 1)
            f(SQ[:, 4:8, :], SQ[:, 4:8, :], ACT.Sqrt, bias=pr("eps6")).then_inc(diff_root, 1)
            act.wait_ge(gemm_free, 20 + 8 + 4 + 4 + 8)
            norm(1, TT, X, A, norm_mod(0, 1), norm_sh(0, 1), pr("eps6"))
            st["u"] = 44
            ffn(2, TT)
            act.wait_ge(gemm_free, st["u"])
            act.wait_ge(mod_ready, 1)
            norm(2, TT, X, A, norm_mod(1, 0), norm_sh(1, 0), pr("eps6"))
            st["u"] += 10 + 4 + 10 + 4
            SINK = lambda h: pr("odd_sink", h, h + 1)
            attention(units_odd())
            st["u"] += KD
            act.wait_ge(gemm_free, st["u"])
            norm(3, T, X, A, norm_mod(1, 1), norm_sh(1, 1), pr("eps6"))
            ffn(2, T)
            act.wait_ge(gemm_free, st["u"])
            norm(4, T, X, X, lambda j, s: pr("final_g", j, j + 1), None, pr("eps6"))

            for l in range(2):
                SINK = lambda h: pr(f"sinks_{l}", h, h + 1)
                act.wait_ge(fox_pre, l + 1)
                f(FC[0:4, 3, :], FC[0:4, 2, :], ACT.Exp).then_inc(fox_e, 1)
                act.wait_ge(fox_e, l + 1)
                f(FC[0:4, 3, :], FC[0:4, 3, :], ACT.Ln, bias=1.0).then_inc(fox_ln, 1)
                attention(units_second(l))
                act.wait_ge(rw_shift, l + 1)
                f(LOW[0:64, 0, :], RP[0:64, 6, :], ACT.Tanh)
                f(LOW[:, 1, :], RP[:, 7, :], ACT.Sigmoid).then_inc(rw_low, 1)
                act.wait_ge(rw_sig, l + 1)
                f(LWV, LWV, ACT.Sigmoid)
                f(AV, AV, ACT.Sigmoid).then_inc(rw_pre, 1)
                act.wait_ge(rw_c, l + 1)
                f(EC, CC, ACT.Exp)
                f(EN, CC, ACT.Exp, scale=-1.0)
                f(EX, EX, ACT.Exp).then_inc(rw_exp, 1)
                act.wait_ge(rw_ks, l + 1)
                f(KNORM, KNORM, ACT.Sqrt).then_inc(rw_kroot, 1)
                act.wait_ge(rw_var, l + 1)
                f(YS, YS, ACT.Sqrt, bias=pr("epsgn")).then_inc(rw_vroot, 1)
                st["u"] = UB[l]["merge"]
                for j in range(KD):
                    for i in range(4):
                        c = st["u"]
                        act.wait_ge(gemm_done, c + 1)
                        act.wait_ge(gemm_free, c - 2)
                        f(GATE[:, i % 2, :], bank[c % BANKS][:, 0:T], ACT.Sigmoid,
                          bias=pr(f"gate_b_{l}", i * KD + j, i * KD + j + 1)).then_inc(act_tmp, 1)
                        st["u"] += 2
                        st["tmp"] += 1
                norm(5 + 2 * l, T, X, X, lambda j, s: pr(f"ln1g_{l}", j, j + 1),
                     lambda j, s: pr(f"ln1b_{l}", j, j + 1), pr("eps5"))
                if l == 1:
                    act.wait_ge(top_v, 1)
                    f(EE[:, 0:2], EE[:, 0:2], ACT.Exp).then_inc(top_e, 1)
                st["u"] = UB[l]["ffn"]
                ffn(2 if l == 0 else EXPERTS, T)
                norm(6 + 2 * l, T, X, X, lambda j, s: pr(f"ln2g_{l}", j, j + 1),
                     lambda j, s: pr(f"ln2b_{l}", j, j + 1), pr("eps5"))

        @block.vector
        def _(dve):
            V = nc.vector
            st = dict(u=0, a=0, g=0, tmp=0, chain=0)

            def link(ins):
                st["chain"] += 1
                ins.then_inc(dve_chain, 1)
                dve.wait_ge(dve_chain, st["chain"])

            def take():
                dve.wait_ge(gemm_done, st["u"] + 1)
                st["u"] += 1
                return bank[(st["u"] - 1) % BANKS]

            def free(ins):
                ins.then_inc(gemm_free, 1)

            def settled_but_last():
                dve.wait_ge(gemm_free, st["u"] - 1)

            def settled():
                dve.wait_ge(gemm_free, st["u"])

            marks = {}

            def mark(semaphore):
                n, slot = marks.get(semaphore.name, (0, len(marks)))
                if n:
                    dve.wait_ge(semaphore, n)
                marks[semaphore.name] = (n + 1, slot)
                V.memset(small(140 + slot, 1), 0.0).then_inc(semaphore, 1)

            def go():
                mark(ready)

            def copy_units(dsts, m=P):
                for d in dsts:
                    free(V.tensor_copy(d, take()[0:d.shape[0], 0:d.shape[1]]))

            def norm(ni, tt, src, dst):
                if ni >= 5:
                    dve.wait_ge(n_mean, ni - 4)
                    for j in range(KD):
                        V.tensor_tensor(src[:, j, 0:tt], src[:, j, 0:tt], MEAN[:, 0:tt], ALU.subtract).then_inc(n_c, 1)
                dve.wait_ge(n_root, ni + 1)
                link(V.reciprocal(RS[:, 0:tt], RS[:, 0:tt]))
                if ni >= 5:
                    dve.wait_ge(n_c, KD * (ni - 4))
                for j in range(KD):
                    V.tensor_tensor(dst[:, j, 0:tt], src[:, j, 0:tt], RS[:, 0:tt], ALU.mult).then_inc(n_x, 1)

            def rope(q, j):
                b = take()[:, 0:T]
                dve.wait_ge(gemm_free, st["u"] - 1)
                link(V.tensor_tensor(RT1[:, 0, :], b, cn("sin"), ALU.mult))
                link(V.tensor_tensor(RT1[:, 1, :], q, cn("cos"), ALU.mult))
                free(V.tensor_tensor(q, RT1[:, 0, :], RT1[:, 1, :], ALU.add))

            def attention(us, diff=False):
                gs, ng = groups(us)
                a0, g0 = st["a"], st["g"]
                for s in range(len(us) + 4):
                    if s < len(us):
                        u, a = us[s], a0 + s
                        c = slice(a % 4, a % 4 + 1)
                        b = bank[s % 2][:, 0:u["nk"]]
                        dve.wait_ge(at_s, a + 1)
                        if s >= 2:
                            dve.wait_ge(at_e, a - 1)
                        if u["mask"] is not None:
                            link(V.tensor_tensor_reduce(SM[:, a % 2, 0:u["nk"]], b, u["mask"], 1.0, OUT_OF_LIST,
                                                        ALU.add, ALU.max, mx[:, c]))
                        else:
                            link(V.reduce_max(mx[:, c], b, AX_X))
                        if u["sink"] is not None:
                            V.tensor_scalar(nm[:, c], mx[:, c], -SCALE, nsink[:, u["sink"]:u["sink"] + 1],
                                            ALU.mult, ALU.min).then_inc(at_m, 1)
                        else:
                            V.tensor_scalar(nm[:, c], mx[:, c], -SCALE, None, ALU.mult).then_inc(at_m, 1)
                    if 1 <= s <= len(us):
                        u, a = us[s - 1], a0 + s - 1
                        c = slice(a % 4, a % 4 + 1)
                        e = E[:, a % 4, 0:u["nk"]]
                        dve.wait_ge(at_e, a + 1)
                        if u["sink"] is not None:
                            link(V.tensor_tensor(sm[:, c], sm[:, c], es[:, c], ALU.add))
                        link(V.reciprocal(rc[:, c], sm[:, c]))
                        if not diff or not u["last"]:
                            V.tensor_scalar(e, e, rc[:, c], None, ALU.mult).then_inc(at_n, 1)
                        else:
                            link(V.tensor_tensor(r2[:, c], rc[:, c], lam[:, 4:5], ALU.mult))
                            dve.wait_ge(at_n, a)
                            V.scalar_tensor_tensor(e, e, r2[:, c], E[:, (a - 1) % 4, 0:u["nk"]],
                                                   ALU.mult, ALU.add).then_inc(at_n, 1)
                    if s >= 4 and us[s - 4]["last"]:
                        u, g = us[s - 4], gs[s - 4]
                        b0, m = u["dst"].base_partition(), u["dst"].shape[0]
                        dve.wait_ge(at_o, g0 + g + 1)
                        V.tensor_copy(u["dst"], bank[4 + g % 2][b0:b0 + m, 0:P]).then_inc(at_out, 1)
                st["a"] += len(us)
                st["g"] += ng

            def ffn(count, tt, gate, experts=False):
                u0, t0 = st["u"], st["tmp"]
                h = tt // 2
                with dve.Fori(0, count) as i:
                    for q in range(FH):
                        u = u0 + 2 * q + 1
                        dve.wait_ge(gemm_done, i * UNITS_FFN + (u + 1))
                        dve.wait_ge(act_tmp, i * FH + (t0 + q + 1))
                        if experts:
                            V.tensor_tensor(TMP[:, q % 2, 0:T], TMP[:, q % 2, 0:T], CW[:, i, :], ALU.mult).then_inc(cw_done, 1)
                            dve.wait_ge(cw_done, i * FH + (q + 1))
                        for s in range(2):
                            free(V.tensor_tensor(H[:, q, s * h:(s + 1) * h], TMP[:, q % 2, s * h:(s + 1) * h],
                                                 bank[u % BANKS][:, s * h:(s + 1) * h], ALU.mult))
                    for j in range(KD):
                        u = u0 + 2 * FH + j
                        dve.wait_ge(gemm_done, i * UNITS_FFN + (u + 1))
                        dve.wait_ge(gemm_free, i * UNITS_FFN + (u - UNITS_FFN + 1))
                        residual(j, bank[u % BANKS], tt, gate)
                st["u"], st["tmp"] = u0 + count * UNITS_FFN, t0 + count * FH

            def residual(j, b, tt, gate):
                for s in range(tt // T):
                    cols = slice(s * T, (s + 1) * T)
                    if gate is None:
                        ins = V.tensor_tensor(X[:, j, cols], X[:, j, cols], b[:, cols], ALU.add)
                    else:
                        ins = V.scalar_tensor_tensor(X[:, j, cols], b[:, cols], gate(j, s), X[:, j, cols],
                                                     ALU.mult, ALU.add)
                free(ins)

            def modulation(l, lo, hi):
                n = 2 * (hi - lo)
                src = ADA[:, 2 * lo:2 * hi].rearrange("p (j s) -> p j s", s=2)
                bias = pr(f"ada_b{l}", lo, hi).unsqueeze(2).broadcast_to([P, hi - lo, 2])
                link(V.tensor_tensor(mod[:, l, lo:hi, :], src, bias, ALU.add))

            def gains(l, n, name):
                g = pr(f"{name}{l}").unsqueeze(2).broadcast_to([P, KD, 2])
                return V.scalar_tensor_tensor(modg[:, 2 * l + n, :, :], mod[:, l, 24 * n + 8:24 * n + 16, :], 1.0, g,
                                              ALU.add, ALU.mult)

            dve.wait_ge(ada_done, 1)
            modulation(0, 0, 16)
            link(gains(0, 0, "n1g"))
            norm(0, TT, X, A)
            copy_units([U0[:, j, :] for j in range(4)] + [Q0[:, j, :] for j in range(4)] + [K0[:, j, :] for j in range(4)])
            copy_units([VT[:, t, :] for t in range(4)] + [VV[:, t, :] for t in range(4)])
            settled()
            for j in range(8):
                rope((Q0 if j < 4 else K0)[:, j % 4, 0:T], j)
            settled()
            dve.wait_ge(gelu_v, 4)
            for t in range(4):
                for g in range(4):
                    V.bn_stats(ST6[:, 4 * t + g, :], VT[:, t, g * P:(g + 1) * P])
            link(V.memset(small(159, 1), 0.0))
            for n in range(16):
                ins = V.bn_aggr(MV2[:, n, :], ST6[:, n, :])
            link(ins)
            V.tensor_copy(VRS, MV2[:, :, 1]).then_inc(v_var, 1)
            ll = pr("lqk").rearrange("p (a b) -> p a b", a=4)
            V.tensor_tensor_reduce(SQ[:, 7, 0:64], ll[:, 0, :], ll[:, 1, :], 1.0, 0.0, ALU.mult, ALU.add, lam[:, 0:1])
            V.tensor_tensor_reduce(SQ[:, 7, 64:128], ll[:, 2, :], ll[:, 3, :], 1.0, 0.0, ALU.mult, ALU.add,
                                   lam[:, 1:2]).then_inc(lam_sum, 1)
            dve.wait_ge(v_root, 1)
            link(V.reciprocal(VRS, VRS))
            for t in range(4):
                for g in range(4):
                    n = 4 * t + g
                    ins = V.tensor_scalar(VG[:, t, g * P:(g + 1) * P], VT[:, t, g * P:(g + 1) * P], MV2[:, n, 0:1],
                                          VRS[:, n:n + 1], ALU.subtract, ALU.mult)
            ins.then_inc(v_normed, 1)
            dve.wait_ge(lam_exp, 1)
            link(V.tensor_tensor(lam[:, 5:6], lam[:, 3:4], lam[:, 2:3], ALU.subtract))
            link(V.tensor_scalar(lam[:, 4:5], lam[:, 5:6], -LAM_INIT, None, ALU.add))
            link(V.tensor_scalar(lam[:, 6:7], pr("subln"), 1.0 - LAM_INIT, None, ALU.mult))
            sgub = pr("sgu_b").rearrange("p (g c) -> p g c", g=4)
            for t in range(4):
                b = take()[:, :].rearrange("p (g c) -> p g c", g=4)
                link(V.tensor_tensor(CAT0[:, 0:4, t * P:(t + 1) * P], b, sgub, ALU.add))
                free(V.tensor_tensor(CAT0[:, 0:4, t * P:(t + 1) * P], CAT0[:, 0:4, t * P:(t + 1) * P],
                                     U0[:, :, t * P:(t + 1) * P], ALU.mult))
            settled()
            go()
            attention(units_even(), diff=True)
            dve.wait_ge(ada_done, 2)
            modulation(0, 16, 48)
            link(gains(0, 1, "n2g"))
            copy_units([SQ[:, 4 + h, :] for h in range(4)])
            settled()
            mark(diff_var)
            dve.wait_ge(diff_root, 1)
            link(V.reciprocal(SQ[:, 4:8, :], SQ[:, 4:8, :]))
            link(V.scalar_tensor_tensor(CAT0[:, 4:8, :], CAT0[:, 4:8, :], lam[:, 6:7], SQ[:, 4:8, :], ALU.mult, ALU.mult))
            go()
            for j in range(KD):
                residual(j, take(), TT, lambda j, s: mod[:, 0, 16 + j, s:s + 1])
            settled()
            norm(1, TT, X, A)
            ffn(2, TT, lambda j, s: mod[:, 0, 40 + j, s:s + 1])
            dve.wait_ge(ada_done, 3)
            modulation(1, 0, 48)
            link(gains(1, 0, "n1g"))
            gains(1, 1, "n2g").then_inc(mod_ready, 1)

            settled()
            norm(2, TT, X, A)
            copy_units([Q1[:, j, :] for j in range(8)] + [K1[:, j, :] for j in range(2)] + [V1[:, t, :] for t in range(4)])
            link(V.tensor_scalar(nsink[:, 0:16], pr("odd_sink"), -1.0, None, ALU.mult))
            settled()
            for j in range(10):
                rope(Q1[:, j, :] if j < 8 else K1[:, j - 8, 0:T], j)
            settled()
            go()
            copy_units([KD1[:, kv, :] for kv in range(4)])
            settled()
            go()
            attention(units_odd())
            go()
            for j in range(KD):
                residual(j, take(), T, lambda j, s: mod[:, 1, 16 + j, s:s + 1])
            settled()
            norm(3, T, X, A)
            ffn(2, T, lambda j, s: mod[:, 1, 40 + j, s:s + 1])
            settled()
            norm(4, T, X, X)

            for l in range(2):
                copy_units([SQ_[:, j, :] for j in range(4)] + [SK[:, 0, :]] + [RP[:, j, :] for j in range(8)]
                           + [FQ[:, j, :] for j in range(2)] + [FK[:, j, :] for j in range(2)]
                           + [DQ[:, j, :] for j in range(2)] + [DQI[:, j, :] for j in range(2)] + [DKI[:, 0, :]])
                free(V.tensor_scalar(FC[0:4, 1, :], take()[0:4, 0:T], pr(f"fbias_{l}")[0:4], None, ALU.add))
                copy_units([SV[:, t, :] for t in range(2)] + [DV[:, t, :] for t in range(2)] + [FV[:, t, :] for t in range(2)])
                link(V.tensor_scalar(nsink[:, 0:8], pr(f"sinks_{l}"), -1.0, None, ALU.mult))
                settled()
                go()
                link(V.tensor_scalar(FC[0:4, 0, :], FC[0:4, 1, :], -1.0, None, ALU.mult))
                V.tensor_tensor(FC[0:4, 2, :], FC[0:4, 0, :], FC[0:4, 1, :], ALU.min).then_inc(fox_pre, 1)
                copy_units([SKD[:, 0, :], SKD[:, 1, :], DKD[:, 0, :], DKID[:, 0, :]])
                settled()
                go()
                dve.wait_ge(fox_ln, l + 1)
                link(V.tensor_scalar(FC[0:4, 1, :], FC[0:4, 1, :], 0.0, None, ALU.min))
                link(V.tensor_tensor(FC[0:4, 1, :], FC[0:4, 1, :], FC[0:4, 3, :], ALU.subtract))
                link(V.memset(FC[0:4, 3, :], 1.0))
                link(V.tensor_tensor_scan(FC[0:4, 2, :], FC[0:4, 3, :], FC[0:4, 1, :], 0.0, ALU.mult, ALU.add))
                V.tensor_scalar(FC[0:4, 0, :], FC[0:4, 2, :], 1.0 / SCALE, None, ALU.mult)
                link(V.tensor_scalar(FC[0:4, 1, :], FC[0:4, 2, :], -1.0 / SCALE, None, ALU.mult))
                for qt in range(2):
                    for h in range(4):
                        b = take()[:, 0:T]
                        w = DV[:, qt, HD + h:HD + h + 1]
                        if h == 0:
                            ins = V.tensor_scalar(DSC, b, 0.0, w, ALU.max, ALU.mult)
                            free(ins)
                        else:
                            free(V.tensor_scalar(DT, b, 0.0, w, ALU.max, ALU.mult))
                            settled()
                            link(V.tensor_tensor(DSC, DSC, DT, ALU.add))
                    link(V.tensor_tensor(DSC, DSC, cn("chunks", qt * T, (qt + 1) * T), ALU.add))
                    src = DSC
                    for r in range(8):
                        link(V.max(M8[:, 0:8], src))
                        link(V.match_replace(DWK, M8[:, 0:8], src, OUT_OF_LIST))
                        src = DWK
                    link(V.tensor_scalar(DMK[:, qt, :], DWK, OUT_OF_LIST / 2, NEG, ALU.is_gt, ALU.mult))
                go()
                attention(units_second(l))

                dve.wait_ge(at_out, st["g"])
                V.tensor_tensor(DELTA[:, :, 1:T], RP[:, :, 0:T - 1], RP[:, :, 1:T], ALU.subtract)
                link(V.tensor_scalar(DELTA[:, :, 0:1], RP[:, :, 0:1], -1.0, None, ALU.mult))
                for j in range(KD):
                    ins = V.scalar_tensor_tensor(RP[:, j, :], DELTA[:, j, :], pr(f"mu_{l}", j, j + 1), RP[:, j, :],
                                                 ALU.mult, ALU.add)
                link(ins)
                mark(rw_shift)
                for j in range(2):
                    free(V.tensor_scalar(LWV[:, j, :], take()[:, 0:T], pr(f"w0_{l}", j, j + 1), None, ALU.add))
                for j in range(2):
                    free(V.tensor_scalar(AV[:, j, :], take()[:, 0:T], pr(f"a0_{l}", j, j + 1), None, ALU.add))
                copy_units([GV[:, j, :] for j in range(2)])
                settled()
                mark(rw_sig)
                dve.wait_ge(rw_pre, l + 1)
                link(V.tensor_scalar(LWV, LWV, -float(np.exp(-0.5)), None, ALU.mult))
                for j in range(2):
                    ins = V.tensor_tensor_scan(CC[:, j, :], cn("segs"), LWV[:, j, :], 0.0, ALU.mult, ALU.add)
                link(ins)
                V.tensor_tensor(EX, CC, LWV, ALU.subtract).then_inc(rw_c, 1)
                for j in range(2):
                    ins = V.tensor_scalar(KK[:, j, :], RP[:, 2 + j, :], pr(f"kk_{l}", j, j + 1), None, ALU.mult)
                link(ins)
                V.tensor_tensor(KNORM, KK, KK, ALU.mult)
                for j in range(2):
                    ins = V.tensor_scalar(BON[:, j, :], AV[:, j, :], -1.0, pr(f"ka_{l}", j, j + 1), ALU.add, ALU.mult)
                link(ins)
                link(V.scalar_tensor_tensor(RP[:, 2:4, :], BON, 1.0, RP[:, 2:4, :], ALU.add, ALU.mult))
                for j in range(2):
                    ins = V.scalar_tensor_tensor(RKK[:, j, :], RP[:, j, :], pr(f"rk_{l}", j, j + 1), RP[:, 2 + j, :],
                                                 ALU.mult, ALU.mult)
                link(ins)
                go()
                b = take()
                kn = KNORM[:, :, :].rearrange("p a b -> p (a b)")
                free(V.tensor_scalar(kn, b[:, :], 1e-12, None, ALU.add))
                settled()
                mark(rw_ks)
                b = take()
                free(V.tensor_tensor(BON, b[:, :].rearrange("p (a b) -> p a b", a=2), RP[:, 4:6, :], ALU.mult))
                dve.wait_ge(rw_kroot, l + 1)
                link(V.reciprocal(KNORM, KNORM))
                link(V.tensor_tensor(KK, KK, KNORM, ALU.mult))
                dve.wait_ge(rw_exp, l + 1)
                V.tensor_tensor(KR[:, :, 0, :], KK, EX, ALU.mult)
                V.tensor_tensor(KR[:, :, 1, :], RP[:, 0:2, :], EC, ALU.mult)
                V.tensor_tensor(KH, RP[:, 2:4, :], EN, ALU.mult)
                link(V.tensor_tensor(BH, KK, AV, ALU.mult))
                link(V.tensor_tensor(BH, BH, EN, ALU.mult))
                go()
                for n in range(4):
                    free(V.tensor_copy(TOK[n][:, :, :].rearrange("p a b -> p (a b)"), take()[:, :]))
                for m in range(8):
                    free(V.tensor_tensor(MM[:, m, :], take()[:, :], cn("pairmask"), ALU.mult))
                for cp in range(2):
                    b = take()[:, :].rearrange("p (m c) -> p m c", m=4)
                    free(V.tensor_tensor(XX[:, 4 * cp:4 * cp + 4, 0:P], b, over(cn("inv0"), 4), ALU.mult))
                settled()
                link(V.tensor_tensor(XX[:, :, P:2 * P], MM[:, :, 0:P], over(cn("inv0t"), 8), ALU.mult))
                xx = XX[:, :, :].rearrange("p m (a c) -> p (m a) c", a=2)
                link(V.tensor_tensor(xx, xx, over(ident, 16), ALU.add))
                for lev in range(5):
                    link(V.tensor_tensor(LK, MM[:, :, 0:P], over(cn("levels", lev * P, (lev + 1) * P), 8), ALU.mult))
                    go()
                    for q in range(2):
                        free(V.tensor_copy(PP[:, 4 * q:4 * q + 4, :].rearrange("p a b -> p (a b)"), take()[:, :]))
                    settled()
                    go()
                    for q in range(4):
                        x2 = XX[:, 2 * q:2 * q + 2, :].rearrange("p a b -> p (a b)")
                        free(V.tensor_tensor(x2, x2, take()[:, :], ALU.subtract))
                    settled()
                go()
                free(V.tensor_copy(MVS[:, :, :].rearrange("p a b -> p (a b)"), take()[:, :]))
                free(V.tensor_scalar(GTN[:, :, :].rearrange("p a b -> p (a b)"), take()[:, :], -1.0, None, ALU.mult))
                settled()
                go()
                free(V.tensor_scalar(U0N[:, :, :].rearrange("p a b -> p (a b)"), take()[:, :], -1.0, None, ALU.mult))
                link(V.memset(STATE[:, 0, :], 0.0))
                settled()
                go()
                for c in range(4):
                    cp, rb = c // 2, (c % 2) * 64
                    for par in range(2):
                        b = take()[rb:rb + 64, 0:P].rearrange("p (a b) -> p a b", a=2)
                        m = 4 * par + 2 * cp
                        free(V.tensor_tensor(SA[rb:rb + 64, 2 * par:2 * par + 2, :], b, U0N[rb:rb + 64, m:m + 2, :], ALU.add))
                    settled()
                    go()
                    b = take()
                    if c < 3:
                        link(V.tensor_tensor(STATE[:, 4, :], STATE[:, c, :], b[:, 0:P], ALU.add))
                        for j in range(2):
                            ins = V.tensor_scalar(STATE[:, c + 1, j * 64:(j + 1) * 64], STATE[:, 4, j * 64:(j + 1) * 64],
                                                  EC[:, j, c * 64 + 63:c * 64 + 64], None, ALU.mult)
                        link(ins)
                    free(V.tensor_copy(small(158, 1), b[:, 0:1]))
                    if c < 3:
                        go()
                    yc = YC[:, :, c * 64:(c + 1) * 64]
                    for part in range(2):
                        b = take()[:, 0:P].rearrange("p (a b) -> p a b", a=2)
                        if part:
                            settled_but_last()
                        free(V.tensor_tensor(yc, yc, b, ALU.add) if part else V.tensor_copy(yc, b))
                    settled()
                link(V.tensor_copy(YT, YC))
                go()
                b = take()[:, :].rearrange("p (a b) -> p a b", a=2)
                link(V.scalar_tensor_tensor(YC, b, -1.0 / HD, YT, ALU.mult, ALU.add))
                free(V.tensor_tensor(YS, YC, YC, ALU.mult))
                settled()
                go()
                b = take()[:, :].rearrange("p (a b) -> p a b", a=2)
                free(V.tensor_scalar(YS, b, 1.0 / HD, None, ALU.mult))
                settled()
                mark(rw_var)
                dve.wait_ge(rw_vroot, l + 1)
                link(V.reciprocal(YS, YS))
                link(V.tensor_tensor(YC, YC, YS, ALU.mult))
                for j in range(2):
                    ins = V.tensor_scalar(YC[:, j, :], YC[:, j, :], pr(f"gng_{l}", j, j + 1), pr(f"gnb_{l}", j, j + 1),
                                          ALU.mult, ALU.add)
                link(ins)
                link(V.tensor_tensor(YC, YC, BON, ALU.add))
                link(V.tensor_tensor(CAT2[:, 4:6, :], YC, GV, ALU.mult))
                go()

                assert st["u"] == UB[l]["merge"], (st["u"], UB)
                for j in range(KD):
                    for i in range(4):
                        st["u"] += 1
                        b = take()[:, 0:T]
                        st["tmp"] += 1
                        dve.wait_ge(act_tmp, st["tmp"])
                        if i == 0:
                            for s in range(2):
                                c = slice(s * P, (s + 1) * P)
                                free(V.tensor_tensor(ACC[:, j, c], b[:, c], GATE[:, i % 2, c], ALU.mult))
                        else:
                            free(V.tensor_tensor(PROD[:, i % 2, :], b, GATE[:, i % 2, :], ALU.mult))
                            dve.wait_ge(gemm_free, st["u"] - 1)
                            free(V.tensor_tensor(ACC[:, j, :], ACC[:, j, :], PROD[:, i % 2, :], ALU.add))
                settled()
                for j in range(KD):
                    ins = V.tensor_scalar(X[:, j, 0:T], X[:, j, 0:T], ALPHA, None, ALU.mult)
                link(ins)
                go()
                for j in range(KD):
                    residual(j, take(), T, None)
                settled()
                go()
                norm(5 + 2 * l, T, X, X)
                dve.wait_ge(n_a, 8 * (6 + 2 * l))
                if l == 1:
                    for t in range(2):
                        free(V.tensor_tensor(LG[:, 8 * t:8 * t + 8], take()[:, 0:8], pr("router_b"), ALU.add))
                    settled()
                    for t in range(2):
                        lg, m8 = LG[:, 8 * t:8 * t + 8], M8[:, 8 * t:8 * t + 8]
                        link(V.max(m8, lg))
                        link(V.max_index(idx8[:, t, :], m8, lg))
                        V.tensor_copy(IDXF[:, 2 * t:2 * t + 2], idx8[:, t, 0:2])
                        link(V.tensor_tensor(EE[:, t:t + 1], m8[:, 1:2], m8[:, 0:1], ALU.subtract))
                    mark(top_v)
                    dve.wait_ge(top_e, 1)
                    link(V.tensor_scalar(EE[:, 2:4], EE[:, 0:2], 1.0, None, ALU.add))
                    link(V.reciprocal(EE[:, 4:6], EE[:, 2:4]))
                    link(V.tensor_tensor(EE[:, 6:8], EE[:, 4:6], EE[:, 0:2], ALU.mult))
                    for t in range(2):
                        V.tensor_scalar(OH[:, 0, :], cn("iota8"), IDXF[:, 2 * t:2 * t + 1], EE[:, 4 + t:5 + t],
                                        ALU.is_equal, ALU.mult)
                        link(V.tensor_scalar(OH[:, 1, :], cn("iota8"), IDXF[:, 2 * t + 1:2 * t + 2], EE[:, 6 + t:7 + t],
                                             ALU.is_equal, ALU.mult))
                        link(V.tensor_tensor(CWT[:, t, :], OH[:, 0, :], OH[:, 1, :], ALU.add))
                    go()
                    copy_units([CWR[0:8, :]])
                    settled()
                    go()
                    copy_units([CW[:, e, :] for e in range(EXPERTS)])
                    settled()
                    go()
                for j in range(KD):
                    ins = V.tensor_copy(A[:, j, 0:T], X[:, j, 0:T])
                link(ins)
                for j in range(KD):
                    ins = V.tensor_scalar(X[:, j, 0:T], X[:, j, 0:T], ALPHA, None, ALU.mult)
                link(ins)
                go()
                assert st["u"] == UB[l]["ffn"], (st["u"], UB)
                if l == 1:
                    assert st["tmp"] == UB["tmp_experts"], (st, UB)
                ffn(2 if l == 0 else EXPERTS, T, None, experts=l == 1)
                settled()
                norm(6 + 2 * l, T, X, X)
                if l == 0:
                    dve.wait_ge(n_a, 8 * 7)


def _unit_bases():
    u = 20 + 8 + 4 + 4 + KD + 2 * UNITS_FFN
    u += 10 + 4 + 10 + 4 + KD + 2 * UNITS_FFN
    out = {}
    for l in range(2):
        u += 23 + 6 + 4 + 8
        u += 6 + 2 + 4 + 8 + 2 + 5 * 6 + 3 + 20 + 2
        out[l] = {"merge": u}
        u += 8 * KD + KD
        if l:
            u += 2 + 1 + EXPERTS
        out[l]["ffn"] = u
        u += (2 if l == 0 else EXPERTS) * UNITS_FFN
    out["tmp_experts"] = 2 * FH * 3 + 2 * 4 * KD
    return out


UB = _unit_bases()


def kernel(**inputs):
    import concourse.bacc as bacc
    from concourse.bass_utils import run_bass_kernel_spmd as run

    a = {k: np.asarray(v) for k, v in inputs.items()}
    plan = stream_plan()
    chunks = len(plan) // CHUNK
    stream = np.zeros((chunks, P, CHUNK * P), np.float32)
    for n, blk in enumerate(plan):
        if blk is None:
            continue
        name, idx, row, col, width = blk
        w = a[name][idx]
        dst = stream[n // CHUNK, :, (n % CHUNK) * P:(n % CHUNK + 1) * P]
        if isinstance(col, tuple):
            ws = width if isinstance(width, tuple) else (width,) * len(col)
            at = 0
            for c, k in zip(col, ws):
                dst[:, at:at + k] = w[row:row + P, c:c + k]
                at += k
        else:
            dst[:, 0:width] = w[row:row + P, col:col + width]

    par = np.zeros((P, NPAR), np.float32)

    def put(name, v):
        lo, hi = PO[name]
        par[:, lo:hi] = v

    def cols(v):
        return v.reshape(-1, P).T

    put("eps6", 1e-6)
    put("eps5", 1e-5)
    put("epsgn", 64e-5)
    cv = np.stack([cols(a["c"][0]), cols(a["c_ctx"])], -1)
    put("cvec", cv.reshape(P, -1))
    for l in range(2):
        put(f"ada_b{l}", cols(a["ada_b"][l]))
        put(f"n1g{l}", cols(a["norm1_g"][l]))
        put(f"n2g{l}", cols(a["norm2_g"][l]))
    put("final_g", cols(a["final_g"]))
    put("sgu_b", a["sgu_b"][0].reshape(1, -1))
    put("lqk", np.concatenate([a[n][0] for n in ("diff_lq1", "diff_lk1", "diff_lq2", "diff_lk2")])[None])
    put("subln", cols(a["diff_subln_g"][0]))
    put("odd_sink", a["odd_sink"][0][None])
    put("sgu_w", a["sgu_w"][0].transpose(2, 0, 1).reshape(P, -1))
    put("router_w", a["router_w_2"][0].reshape(KD, P, 8).transpose(1, 0, 2).reshape(P, -1))
    put("router_b", a["router_b_2"][0][None])
    for l in range(2):
        put(f"sinks_{l}", a["swa_sinks_2"][l][None])
        for n, k in (("mu", "rwkv_mu_2"), ("w0", "rwkv_w0_2"), ("a0", "rwkv_a0_2"), ("kk", "rwkv_k_k_2"),
                     ("ka", "rwkv_k_a_2"), ("rk", "rwkv_r_k_2"), ("gng", "rwkv_gn_g_2"), ("gnb", "rwkv_gn_b_2"),
                     ("gate_b", "gate_bias_2")):
            put(f"{n}_{l}", cols(a[k][l]))
        for i in range(2):
            put(f"ln{i + 1}g_{l}", cols(a["ln_g_2"][l, i]))
            put(f"ln{i + 1}b_{l}", cols(a["ln_b_2"][l, i]))
        lo, hi = PO[f"fbias_{l}"]
        par[0:4, lo:hi] = a["fox_f_bias_2"][l][:, None]
        put(f"wa_up_{l}", np.concatenate([a["rwkv_w_up_2"][l], a["rwkv_a_up_2"][l]], 0))
        put(f"g_up_{l}", a["rwkv_g_up_2"][l])

    xin = np.concatenate([a["x"][0], a["ctx"][0]], 0).T.reshape(KD, P, TT).transpose(1, 0, 2)
    arrays = {"stream": stream, "params": par, "consts": constants(), "xin": np.ascontiguousarray(xin)}
    nc = bacc.Bacc("TRN2", target_bir_lowering=False, num_devices=1)
    aps = [nc.dram_tensor(k, v.shape, F32, kind="ExternalInput").ap() for k, v in arrays.items()]
    out = nc.dram_tensor("out", (P, KD, T), F32, kind="ExternalOutput").ap()
    build(nc, *aps, out)
    r = run(nc, [arrays], core_ids=[0])
    y = r.results[0]["out"]
    return np.ascontiguousarray(y.transpose(2, 1, 0).reshape(1, T, D))
```

```python
from contextlib import ExitStack

import numpy as np

import concourse.bass as bass
from concourse import mybir

F32 = mybir.dt.float32
F32R = mybir.dt.float32r
U32 = mybir.dt.uint32
ALU = mybir.AluOpType
ACT = mybir.ActivationFunctionType
AX_X = mybir.AxisListType.X

P = 128
D = 1024
KD = D // P
T = 256
TC = 256
TT = T + TC
HD = 64
SCALE = HD ** -0.5
FH = 11
HID = 2 * FH * P
EXPERTS = 8
CHUNK = 4
RING = 11
SPLIT = 6
AHEAD = 4
BANKS = 6
NEG = -1e30
OUT_OF_LIST = -3e38
LAM_INIT = 0.8 - 0.6
BR_K = (4, 2, 2, 2)
UNITS_FFN = 2 * FH + KD
ALPHA = 4.0 ** 0.25
SCR = 23040

C_SWA, C_RWKV, C_FOX, C_DSA, C_GATE = 0, 768, 1792, 2564, 3272

PARAM_COLS = [
    ("eps6", 1), ("eps5", 1), ("epsgn", 1), ("cvec", 2 * KD),
    ("ada_b0", 48), ("ada_b1", 48), ("n1g0", KD), ("n1g1", KD), ("n2g0", KD), ("n2g1", KD), ("final_g", KD),
    ("sgu_b", 512), ("lqk", 256), ("subln", 1), ("odd_sink", 16), ("sgu_w", 512), ("router_w", 64), ("router_b", 8),
]
for _l in range(2):
    PARAM_COLS += [(f"{n}_{_l}", w) for n, w in (
        ("sinks", 8), ("mu", 8), ("w0", 2), ("a0", 2), ("kk", 2), ("ka", 2), ("rk", 2), ("gng", 2), ("gnb", 2),
        ("fbias", 1), ("gate_b", 32), ("ln1g", 8), ("ln1b", 8), ("ln2g", 8), ("ln2b", 8), ("wa_up", 256), ("g_up", 256))]

CONST_COLS = [
    ("ident", 128), ("mean_d", 128), ("mean_e", 128), ("blk64", 128), ("rot", 128), ("dup0", 128), ("dup1", 128),
    ("cos", 256), ("sin", 256), ("band", 1024), ("swa", 512), ("causal", 512), ("chunks", 512), ("sel8", 1024),
    ("pairmask", 512), ("inv0", 128), ("inv0t", 128), ("levels", 640), ("segs", 256), ("iota8", 8),
]


def offsets(cols):
    at, out = 0, {}
    for name, width in cols:
        out[name] = (at, at + width)
        at += width
    return out, at


PO, NPAR = offsets(PARAM_COLS)
CO, NCON = offsets(CONST_COLS)


def constants():
    c = np.zeros((P, NCON), np.float32)

    def put(name, value):
        a, b = CO[name]
        c[:value.shape[0], a:b] = value.reshape(value.shape[0], -1)

    i, j = np.arange(P)[:, None], np.arange(P)[None, :]
    put("ident", (i == j).astype(np.float32))
    put("mean_d", np.full((P, P), 1.0 / D, np.float32))
    put("mean_e", np.full((P, P), 1.0 / P, np.float32))
    put("blk64", (i // 64 == j // 64).astype(np.float32))
    half = j % 32 < 16
    put("rot", np.where(half & (i == j + 16), -1.0, np.where(~half & (i == j - 16), 1.0, 0.0)).astype(np.float32))
    put("dup0", ((i < 64) & (j % 64 == i)).astype(np.float32))
    put("dup1", ((i >= 64) & (j % 64 == i - 64)).astype(np.float32))
    t = np.arange(T)
    nf = HD // 4
    inv = np.float32(10000.0) ** (-np.arange(nf, dtype=np.float32) / np.float32(nf))
    ang = np.stack([(t // 64).astype(np.float32)[:, None] * inv, (t % 64).astype(np.float32)[:, None] * inv], 1)
    ang = np.broadcast_to(ang[:, :, None, :], (T, 2, 2, nf)).reshape(T, HD).T
    put("cos", np.tile(np.cos(ang), (2, 1)).astype(np.float32))
    put("sin", np.tile(np.sin(ang), (2, 1)).astype(np.float32))

    def mask(allowed, extra=0):
        m = np.zeros((P, 2, T + extra), np.float32)
        for q in range(2):
            m[:, q, :T] = np.where(allowed(q * P + i, np.arange(T)[None, :]), 0.0, NEG)
        return m

    put("band", mask(lambda q, k: np.abs(q - k) <= 128, TC))
    put("swa", mask(lambda q, k: (k // 64 <= q // 64) & (k // 64 >= q // 64 - 2)))
    put("causal", mask(lambda q, k: k <= q))
    put("chunks", mask(lambda q, k: k // 64 <= q // 64))
    put("sel8", np.broadcast_to((np.arange(8)[:, None] == np.arange(8)[None, :])[:, :, None], (8, 8, P)).astype(np.float32))
    same = i // 64 == j // 64
    strict, incl = (same & (i < j)), (same & (i <= j))
    put("pairmask", np.stack([strict, incl, strict, incl], 1).astype(np.float32))
    low = (i // 2 == j // 2) & (i > j)
    put("inv0", -low.astype(np.float32))
    put("inv0t", -low.T.astype(np.float32))
    lev = [((i // (2 * s) == j // (2 * s)) & (i // s < j // s)) for s in (2, 4, 8, 16, 32)]
    put("levels", np.stack(lev, 1).astype(np.float32))
    put("segs", np.broadcast_to((t % 64 != 0).astype(np.float32), (P, T)))
    put("iota8", np.broadcast_to(np.arange(8, dtype=np.float32), (P, 8)))
    return c


ADA_HALVES = [[0, 1]] + [[f + 1] for f in range(1, FH)]


PAIRS = [(i, j) for i in (0, 2, 3, 1) for j in range(KD)]
FILL_INDEX = (2, 3)
FILL_START, FILL_LOW, FILL_NORM, FILL_MATRIX, FILL_LEVEL = 2, 2, 2, 3, 1
FILLED = sum(FILL_INDEX) + FILL_START + FILL_LOW + FILL_NORM + FILL_MATRIX + 10 * FILL_LEVEL
assert FILLED == 3 * KD

def stream_plan():
    blocks, starts = [], []

    def pad():
        while len(blocks) % CHUNK:
            blocks.append(None)

    def tiles(name, idx, cols, k=KD, row=0, width=P):
        for c in cols:
            for kk in range(k):
                blocks.append((name, idx, row + kk * P, c, width))

    def wide(name, idx, col, n):
        for kk in range(KD):
            for c in range(n):
                blocks.append((name, idx, kk * P, col + c * P, P))

    def ada_rows(layer, group, k0, n):
        for kk in range(k0, k0 + n):
            for c in range(CHUNK):
                blocks.append(("ada_w", (layer,), kk * P, (CHUNK * group + c) * P, P))

    def ffn(w_up, w_gate_col, w_val, w_val_idx, w_val_col, w_down, idx, didx, row, ada=None):
        pad()
        starts.append(len(blocks) // CHUNK)
        for f in range(FH):
            tiles(w_up, idx, [w_gate_col + f * P])
            tiles(w_val, w_val_idx, [w_val_col + f * P])
            if ada is not None:
                for h in ADA_HALVES[f]:
                    ada_rows(1, 6 * ada + h // 2, h % 2 * (KD // 2), KD // 2)
        for j in range(KD):
            tiles(w_down, didx, [j * P], FH, row)

    for g in range(4):
        ada_rows(0, g, 0, KD)
    tiles("even_w_in", (0,), [j * P for j in (*range(4), *range(8, 16))])
    wide("even_w_in", (0,), 512, 4)
    wide("even_w_in", (0,), 2048, 4)
    for g in range(4, 12):
        ada_rows(0, g, 0, KD)
    tiles("even_w_out", (0,), [j * P for j in range(KD)])
    for half in range(2):
        ffn("ffn_w_in", half * FH * P, "ffn_w_in", (0,), HID + half * FH * P, "ffn_w_out", (0,), (0,), half * FH * P, half)
    tiles("odd_w_qkv", (0,), [j * P for j in range(10)])
    wide("odd_w_qkv", (0,), 1280, 2)
    tiles("odd_w_out", (0,), [j * P for j in range(KD)])
    for half in range(2):
        ffn("ffn_w_in", half * FH * P, "ffn_w_in", (1,), HID + half * FH * P, "ffn_w_out", (1,), (1,), half * FH * P)
    for l in range(2):
        w = "w_in_2"
        tiles(w, (l,), [C_SWA + j * P for j in range(5)] + [C_RWKV + j * P for j in range(8)]
              + [C_FOX + j * P for j in range(4)] + [C_DSA, C_DSA + P, C_DSA + 384, C_DSA + 512])
        for kk in range(KD):
            blocks.append((w, (l,), kk * P, (C_DSA + 256, C_DSA + 640), 64))
        tiles(w, (l,), [C_FOX + 768], width=4)
        tiles(w, (l,), [C_SWA + 640])
        for kk in range(KD):
            blocks.append((w, (l,), kk * P, (C_DSA + 320, C_DSA + 704), (64, 4)))
        wide(w, (l,), C_FOX + 512, 2)
        for i, j in PAIRS:
            tiles(w, (l,), [C_GATE + i * D + j * P])
            tiles("w_branch_2", (l,), [j * P], BR_K[i], sum(BR_K[:i]) * P)
        pad()
        tiles("w_out_2", (l,), [j * P for j in range(KD)])
        if l == 0:
            for half in range(2):
                c = half * FH * P
                ffn("ffn_w1_2", c, "ffn_w3_2", (0,), c, "ffn_w2_2", (0,), (0,), c)
        else:
            for e in range(EXPERTS):
                ffn("exp_w1_2", 0, "exp_w3_2", (0, e), 0, "exp_w2_2", (0, e), (0, e), 0)
    while len(blocks) % (CHUNK * RING):
        blocks.append(None)
    return blocks, starts


def build(nc, stream, params, consts, xin, out):
    rounds = stream.shape[0] // RING
    with ExitStack() as ctx:
        def sb(name, *shape, dt=F32):
            return ctx.enter_context(nc.sbuf_tensor(name, [P, *shape], dt))

        def sem(name):
            return ctx.enter_context(nc.semaphore(name))

        ring = sb("ring", RING, CHUNK * P)
        WH, WL = sb("WH", SPLIT, CHUNK * P, dt=F32R), sb("WL", SPLIT, CHUNK * P, dt=F32R)
        X = sb("X", KD, TT)
        par = sb("par", NPAR)
        con = sb("con", NCON)
        smalls = sb("smalls", 160)
        mod = sb("mod", 2, 48, 2)
        modg = sb("modg", 4, KD, 2)
        idx8 = sb("idx8", 2, 8, dt=U32)
        csH, csL = sb("csH", 2 * KD, dt=F32R), sb("csL", 2 * KD, dt=F32R)
        with ExitStack() as feed_forward:
            def ffb(name, *shape, dt=F32):
                return feed_forward.enter_context(nc.sbuf_tensor(name, [P, *shape], dt))

            AH, AL = ffb("AH", KD, TT, dt=F32R), ffb("AL", KD, TT, dt=F32R)
            HH, HL = ffb("HH", FH, TT, dt=F32R), ffb("HL", FH, TT, dt=F32R)
            SQF, RSF = ffb("SQF", KD, TT), ffb("RSF", TT)
            TMP = ffb("TMP", 2, TT)
            ROWF = ffb("ROWF", CHUNK * P)
        A = sb("A", KD, TT)
        S = sb("S", SCR)

        bank = [ctx.enter_context(nc.psum_tensor(f"bank{i}", [P, 512], F32)) for i in range(8)]
        NORM, ADA = bank[6], bank[7]
        ROWS = bank[6]
        MEAN = bank[7]

        def pr(name, a=0, b=None):
            lo, hi = PO[name]
            return par[:, lo + a:(hi if b is None else lo + b)]

        def cn(name, a=0, b=None):
            lo, hi = CO[name]
            return con[:, lo + a:(hi if b is None else lo + b)]

        def view(at, *shape):
            n = int(np.prod(shape))
            assert at + n <= SCR
            v = S[:, at:at + n]
            if len(shape) == 2:
                v = v.rearrange("p (a b) -> p a b", a=shape[0])
            if len(shape) == 3:
                v = v.rearrange("p (a b c) -> p a b c", a=shape[0], b=shape[1])
            return v

        def small(at, n):
            return smalls[:, at:at + n]

        def over(ap, n):
            return ap.unsqueeze(1).broadcast_to([P, n, ap.shape[1]])

        ident, sel8 = cn("ident"), cn("sel8").rearrange("p (e c) -> p e c", e=8)

        SQM = view(18432 - 4096, KD, TT)
        CW = X[:, :, T:TT]
        RSM = view(18432, TT)

        def SQN(ni):
            return SQF if ni % 2 and ni < 8 else SQM

        def RSN(ni):
            return RSF if ni % 2 and ni < 8 else RSM

        AT = 18432
        SM = view(AT, 2, 512)
        E = view(AT + 1024, 4, 512)
        ET = view(AT + 3072, 2, 512)
        mx, nm, sm, es, rc, r2 = (small(4 * n, 4) for n in range(6))
        nsink = small(24, 32)
        lam = small(60, 8)
        cs = small(70, 16)
        Q0, K0, U0, VG, VV = (view(2048 * n, 4, TT) for n in range(5))
        CAT0 = view(10240, KD, TT)
        VT = view(14336, 4, TT)
        ST6 = view(AT, 16, 6)
        MV2 = view(AT + 96, 16, 2)
        VRS = view(AT + 128, 16)
        RT1 = view(AT + 1024, 2, T)
        ROWM = view(AT + 4096, CHUNK * P)
        Q1, K1, KD1, V1 = view(0, KD, T), view(2048, 2, TT), view(3072, 4, TT), view(5120, 4, T)
        CAT1 = view(10240, KD, T)
        SQ_, SK, SKD = view(0, 4, T), view(1024, 1, T), view(1280, 2, T)
        FQ, FK, DQ, DQI = view(1792, 2, T), view(2304, 2, T), view(2816, 2, T), view(3328, 2, T)
        DKI, DKD, DKID, FC = view(3840, 1, T), view(4096, 1, T), view(4352, 1, T), view(4608, 4, T)
        SV, FV, DV = view(5632, 2, P), view(5888, 2, T), view(6400, 2, 68)
        RP = view(6656, KD, T)
        DSC, DWK, DMK, DT = view(8704, T), view(8960, T), view(9216, 2, T), view(9728, T)
        CAT2 = A[:, :, :].rearrange("p a b -> p (a b)")[:, 0:2560].rearrange("p (a b) -> p a b", a=10)
        W0 = 8704
        (SHD, LWV, AV, GV, CC, CX, KK, EC, EN, EX) = (view(W0 + 512 * n, 2, T) for n in range(10))
        DELTA = view(W0, KD, T)
        KNORM, RKK, BON = CX, SHD, view(W0 + 5120, 2, T)
        KR = view(W0 + 5632, 2, 2, T)
        BH, KH = view(W0 + 6656, 2, T), view(W0 + 7168, 2, T)
        LOW = view(W0 + 7680, 2, T)
        TOK = [view(W0 + 8192 + 512 * n, 2, T) for n in range(4)]
        MM = view(W0 + 10240, 8, 512)
        XX = view(0, 8, 256)
        LK = view(2048, 8, P)
        PP = view(3072, 8, P)
        MVS, U0N, GTN = view(4096, 8, 64), view(4608, 8, 64), view(5120, 4, P)
        SA = view(5632, 4, 64)
        STATE = view(5888, 5, P)
        YT = view(W0 + 5632, 2, T)
        YC, YS = view(W0 + 6656, 2, T), view(W0 + 7168, 2, T)
        ACC = X[:, :, T:TT]
        GP = A[:, :, :].rearrange("p a b -> p (a b)")[:, 2560:3584].rearrange("p (a b) -> p a b", a=4)
        GATE, PROD = GP[:, 0:2, :], GP[:, 2:4, :]
        LG, M8, EE = small(90, 16), small(106, 16), small(122, 8)
        IDXF, CWT = small(130, 4), view(W0, 2, 8)
        CWR, OH = view(W0 + 64, T), view(W0 + 320, 2, 8)

        w_loaded = [sem(f"w_loaded{i}") for i in range(RING)]
        w_taken = sem("w_taken")
        inputs_in = sem("inputs_in")
        gemm_done, gemm_free = sem("gemm_done"), sem("gemm_free")
        w_hi, split_begun = sem("w_hi"), sem("split_begun")
        h_hi, h_lo = sem("h_hi"), sem("h_lo")
        a_hi = sem("a_hi")
        act_tmp, cw_done = sem("act_tmp"), sem("cw_done")
        silu_c = sem("silu_c")
        ada_row, ada_copied = sem("ada_row"), sem("ada_copied")
        ada_done, mod_ready = sem("ada_done"), sem("mod_ready")
        n_sq, n_mm, n_root, n_x, n_a = sem("norm_sq"), sem("norm_mm"), sem("norm_root"), sem("norm_x"), sem("norm_a")
        n_mean, n_c = sem("norm_mean"), sem("norm_centred")
        dve_chain, act_chain = sem("dve_chain"), sem("act_chain")
        at_s, at_m, at_e, at_n = sem("att_scores"), sem("att_max"), sem("att_exp"), sem("att_normed")
        at_t, at_tv, at_o, at_out = sem("att_turned"), sem("att_turned_copy"), sem("att_pv"), sem("att_out")
        lam_sum, lam_exp = sem("lam_sum"), sem("lam_exp")
        gelu_v, v_var, v_root, v_normed = sem("gelu_v"), sem("v_var"), sem("v_root"), sem("v_normed")
        ready = sem("ready")
        diff_sq, diff_var, diff_root = sem("diff_sq"), sem("diff_var"), sem("diff_root")
        fox_pre, fox_e, fox_ln = sem("fox_pre"), sem("fox_exp"), sem("fox_log")
        rw_shift, rw_low, rw_pre, rw_sig = sem("rw_shift"), sem("rw_low"), sem("rw_pre"), sem("rw_sig")
        rw_c, rw_exp, rw_ks, rw_kroot = sem("rw_c"), sem("rw_exp"), sem("rw_ks"), sem("rw_kroot")
        rw_var, rw_vroot = sem("rw_var"), sem("rw_vroot")
        top_v, top_e = sem("top_v"), sem("top_e")
        out_done = sem("out_done")

        def keys(kap, n0, n1):
            return lambda base, h: kap(h)[base:base + HD, n0:n1]

        def unit(q, k, nk, mask, sink, vals, dst, last=True, bias=None):
            return dict(q=q, k=k, nk=nk, mask=mask, sink=sink, vals=vals, dst=dst, last=last, bias=bias)

        def units_even():
            us = []
            for half in range(2):
                k0 = half * T
                for h in range(4):
                    for qt in range(2):
                        q0 = half * T + qt * P
                        for s in range(2):
                            b = s * HD
                            us.append(unit(Q0[b:b + HD, h, q0:q0 + P], K0[b:b + HD, h, k0:TT], TT - k0, None, None,
                                           [VV[:, t, h * P:(h + 1) * P] for t in range(2 * half, 4)],
                                           CAT0[:, 4 + h, q0:q0 + P], last=s == 1))
            return us

        def units_odd():
            us = []
            for h in range(16):
                b, kv = (h % 2) * HD, h // 4
                for qt in range(2):
                    us.append(unit(Q1[b:b + HD, h // 2, qt * P:(qt + 1) * P], KD1[b:b + HD, kv, :], TT,
                                   cn("band", qt * TT, (qt + 1) * TT), h,
                                   [V1[:, t, kv * HD:(kv + 1) * HD] for t in range(4)],
                                   CAT1[b:b + HD, h // 2, qt * P:(qt + 1) * P]))
            return us

        def units_second(l):
            us = []
            for h in range(8):
                b, kv = (h % 2) * HD, h // 4
                for qt in range(2):
                    nk = (qt + 1) * P
                    us.append(unit(SQ_[b:b + HD, h // 2, qt * P:nk], SKD[b:b + HD, kv, 0:nk], nk,
                                   cn("swa", qt * T, qt * T + nk), h,
                                   [SV[:, t, kv * HD:(kv + 1) * HD] for t in range(qt + 1)],
                                   CAT2[b:b + HD, h // 2, qt * P:nk]))
            for h in range(4):
                b = (h % 2) * HD
                for qt in range(2):
                    nk = (qt + 1) * P
                    us.append(unit(FQ[b:b + HD, h // 2, qt * P:nk], FK[b:b + HD, h // 2, 0:nk], nk,
                                   cn("causal", qt * T, qt * T + nk), None,
                                   [FV[:, t, h * HD:(h + 1) * HD] for t in range(qt + 1)],
                                   CAT2[b:b + HD, 6 + h // 2, qt * P:nk], bias=(h, qt)))
            for h in range(4):
                b = (h % 2) * HD
                for qt in range(2):
                    nk = (qt + 1) * P
                    us.append(unit(DQ[b:b + HD, h // 2, qt * P:nk], DKD[b:b + HD, 0, 0:nk], nk,
                                   DMK[:, qt, 0:nk], None, [DV[:, t, 0:HD] for t in range(qt + 1)],
                                   CAT2[b:b + HD, 8 + h // 2, qt * P:nk]))
            return us

        def groups(us):
            g, out_ = 0, []
            for u in us:
                out_.append(g)
                g += u["last"]
            return out_, g

        def head_cols(m):
            h = 2 * (m % 2) + m // 4
            return slice(h * 64, (h + 1) * 64)

        block = ctx.enter_context(nc.Block())

        @block.sync
        def _(sp):
            sp.dma_start(par[:, :], params).then_inc(inputs_in, 16)
            for s in range(RING):
                sp.dma_start(ring[:, s, :], stream[s]).then_inc(w_loaded[s], 16)
                if s == 0:
                    sp.dma_start(X[:, :, :], xin).then_inc(inputs_in, 16)
                    sp.dma_start(con[:, :], consts).then_inc(inputs_in, 16)
            with sp.Fori(1, rounds) as r:
                for s in range(RING):
                    sp.wait_ge(w_taken, r * RING + (s - RING + 2))
                    sp.dma_start(ring[:, s, :], stream[r * RING + s]).then_inc(w_loaded[s], 16)
            sp.wait_ge(n_a, 8 * 9)
            sp.dma_start(out, X[:, :, 0:T]).then_inc(out_done, 16)
            sp.wait_ge(out_done, 16)

        @block.tensor
        def _(pe):
            st = dict(n=0, u=0, a=0, g=0, s=0, h=0, ada=0, p=0, free=False, i=None, ready=0)

            def val(x, per):
                return x if st["i"] is None else st["i"] * per + x

            def weight(n, signal=True):
                slot, c = (n // CHUNK) % RING, n % CHUNK
                if c == 0:
                    pe.wait_ge(w_loaded[slot], 16 * (n // CHUNK // RING + 1))
                    st["free"] = st["free"] or signal
                return ring[:, slot, c * P:(c + 1) * P]

            def mm(o, l, r, start, stop, end=False, sig=True):
                ins = pe.matmul(o, l, r, start=start, stop=stop)
                if end:
                    ins.then_inc(gemm_done, 1)
                elif st["free"] and sig:
                    ins.then_inc(w_taken, 1)
                    st["free"] = False
                return ins

            def unit_begin():
                u = st["u"]
                if u >= BANKS:
                    pe.wait_ge(gemm_free, val(u - BANKS + 1, UNITS_FFN))
                st["u"] += 1
                return bank[u % BANKS]

            def tile(rhs, k, tt, m=P):
                b = unit_begin()
                for kk in range(k):
                    w = weight(st["n"])
                    mm(b[0:m, 0:tt], w[:, 0:m], rhs(kk), kk == 0, kk == k - 1, kk == k - 1)
                    st["n"] += 1

            def split_tile(o, hi, lo, k):
                for kk in range(k):
                    n, s = st["n"], st["s"]
                    c = slice(n % CHUNK * P, (n % CHUNK + 1) * P)
                    first = n % CHUNK == 0
                    if first:
                        pe.wait_ge(w_taken, val(n // CHUNK + 1, PART_CHUNKS))
                    wh, wl = WH[:, s % SPLIT, c], WL[:, s % SPLIT, c]
                    ins = pe.matmul(o, wh, hi(kk), start=kk == 0, stop=False)
                    if first:
                        ins.then_inc(split_begun, 1)
                    pe.matmul(o, wh, lo(kk), start=False, stop=False)
                    ins = pe.matmul(o, wl, hi(kk), start=False, stop=kk == k - 1)
                    st["n"] += 1
                    st["s"] += n % CHUNK == CHUNK - 1
                ins.then_inc(gemm_done, 1)

            def tok_tiles(src, tiles, n):
                n0 = st["n"]
                for t in range(tiles):
                    b = unit_begin()
                    for kk in range(KD):
                        w = weight(n0 + kk * n, signal=t == tiles - 1)
                        slot, c = ((n0 + kk * n) // CHUNK) % RING, (n0 + kk * n) % CHUNK
                        w = ring[:, slot, c * P:(c + n) * P]
                        mm(b[:, 0:n * P], src(kk, t), w, kk == 0, kk == KD - 1, kk == KD - 1)
                st["n"] = n0 + KD * n

            def skip_to_chunk():
                st["n"] += -st["n"] % CHUNK

            def ada_rows(k0, n):
                for kk in range(k0, k0 + n):
                    weight(st["n"])
                    w = ring[:, (st["n"] // CHUNK) % RING, :]
                    ins = pe.matmul(ROWS[0:2, :], cs[:, 2 * kk:2 * kk + 2], w, start=kk == 0, stop=kk == KD - 1)
                    if kk < KD - 1:
                        ins.then_inc(w_taken, 1)
                        st["free"] = False
                    else:
                        ins.then_inc(ada_row, 1)
                    st["n"] += CHUNK

            def split_rows(k0, n):
                for kk in range(k0, k0 + n):
                    pe.wait_ge(w_taken, st["n"] // CHUNK + 1)
                    wh, wl = WH[:, st["s"] % SPLIT, :], WL[:, st["s"] % SPLIT, :]
                    ch, cl = csH[:, 2 * kk:2 * kk + 2], csL[:, 2 * kk:2 * kk + 2]
                    pe.matmul(ROWS[0:2, :], ch, wh, start=kk == 0, stop=False).then_inc(split_begun, 1)
                    pe.matmul(ROWS[0:2, :], cl, wh, start=False, stop=False)
                    ins = pe.matmul(ROWS[0:2, :], ch, wl, start=False, stop=kk == KD - 1)
                    if kk == KD - 1:
                        ins.then_inc(ada_row, 1)
                    st["n"] += CHUNK
                    st["s"] += 1

            def ada_turn(row, done=False):
                g = st["ada"]
                pe.wait_ge(ada_copied, g + 1)
                for c in range(CHUNK):
                    col = 2 * (CHUNK * (g % 12) + c)
                    ins = pe.transpose(ADA[:, col:col + 2], row[0:2, c * P:(c + 1) * P], ident[0:2, 0:2])
                    if c == 0 and st["free"]:
                        ins.then_inc(w_taken, 1)
                        st["free"] = False
                if done:
                    ins.then_inc(ada_done, 1)
                st["ada"] += 1

            def small_unit(pairs, tt, m=P):
                b = unit_begin()
                for j, (o, l, r, s, e) in enumerate(pairs(b)):
                    mm(o, l, r, s, e, j == len(pairs(b)) - 1)

            def dup_unit(lhs, rhs, tt):
                b = unit_begin()
                mm(b[:, 0:tt], lhs, rhs, True, True, True)

            def norm(ni, tt, layer_norm=False):
                SQ = SQN(ni)
                if layer_norm:
                    pe.wait_ge(gemm_free, st["u"])
                    for j in range(KD):
                        ins = pe.matmul(MEAN[:, 0:tt], cn("mean_d"), X[:, j, 0:tt], start=j == 0, stop=j == KD - 1)
                    ins.then_inc(n_mean, 1)
                for j in range(KD):
                    pe.wait_ge(n_sq, KD * ni + j + 1)
                    ins = pe.matmul(NORM[:, 0:tt], cn("mean_d"), SQ[:, j, 0:tt], start=j == 0, stop=j == KD - 1)
                ins.then_inc(n_mm, 1)

            def attention(us, extra=None):
                gs, ng = groups(us)
                a0, g0 = st["a"], st["g"]
                for s in range(len(us) + 3):
                    if s < len(us):
                        u = us[s]
                        if s >= 2:
                            pe.wait_ge(at_e, a0 + s - 1)
                        b = bank[s % 2]
                        ins = pe.matmul(b[:, 0:u["nk"]], u["q"], u["k"], start=True, stop=u["bias"] is None)
                        if u["bias"] is not None:
                            h, qt = u["bias"]
                            pe.matmul(b[:, 0:u["nk"]], sel8[0:4, h, :], FC[0:4, 1, 0:u["nk"]], start=False, stop=False)
                            for kt in range(qt + 1):
                                ins = pe.matmul(b[:, kt * P:(kt + 1) * P], FC[0:4, 0, qt * P:(qt + 1) * P],
                                                sel8[0:4, h, :], start=False, stop=kt == qt)
                        ins.then_inc(at_s, 1)
                    if extra is not None and s < len(us):
                        extra(s)
                    if 2 <= s < len(us) + 2 and us[s - 2]["last"]:
                        u, g = us[s - 2], gs[s - 2]
                        pe.wait_ge(at_n, a0 + s - 1)
                        if g >= 2:
                            pe.wait_ge(at_tv, g0 + g - 1)
                        for kt in range(u["nk"] // P):
                            ins = pe.transpose(bank[2 + g % 2][:, kt * P:(kt + 1) * P],
                                               E[:, (a0 + s - 2) % 4, kt * P:(kt + 1) * P], ident)
                        ins.then_inc(at_t, 1)
                    if s >= 3 and us[s - 3]["last"]:
                        u, g = us[s - 3], gs[s - 3]
                        pe.wait_ge(at_tv, g0 + g + 1)
                        if g >= 2:
                            pe.wait_ge(at_out, g0 + g - 1)
                        b, m = u["dst"].base_partition(), u["dst"].shape[0]
                        for kt, v in enumerate(u["vals"]):
                            ins = pe.matmul(bank[4 + g % 2][b:b + m, 0:P], v, ET[:, g % 2, kt * P:(kt + 1) * P],
                                            start=kt == 0, stop=kt == len(u["vals"]) - 1)
                        ins.then_inc(at_o, 1)
                st["a"] += len(us)
                st["g"] += ng
                pe.wait_ge(at_out, st["g"])

            def ready_wait():
                st["ready"] += 1
                pe.wait_ge(ready, st["ready"])

            def pairs(n):
                for i, j in PAIRS[st["p"]:st["p"] + n]:
                    tile(lambda kk: X[:, kk, 0:T], KD, T)
                    tile(lambda kk: CAT2[:, sum(BR_K[:i]) + kk, :], BR_K[i], T)
                st["p"] += n

            def ffn_part(tt, u0, ada=None):
                for f in range(FH):
                    for _ in range(2):
                        split_tile(unit_begin()[:, 0:tt], lambda kk: AH[:, kk, 0:tt], lambda kk: AL[:, kk, 0:tt], KD)
                    if ada is not None:
                        for h in ADA_HALVES[f]:
                            if h and h % 2 == 0:
                                ada_turn(ROWF)
                            split_rows(h % 2 * (KD // 2), KD // 2)
                for j in range(KD):
                    b = unit_begin()
                    if j == 0:
                        pe.wait_ge(h_lo, val(st["h"] + FH, FH))
                    split_tile(b[:, 0:tt], lambda kk: HH[:, kk, 0:tt], lambda kk: HL[:, kk, 0:tt], FH)
                    if ada is not None and j == 0:
                        ada_turn(ROWF, done=ada == 1)

            def ffn(count, tt):
                skip_to_chunk()
                n0, u0, s0 = st["n"], st["u"], st["s"]
                with pe.Fori(0, count) as i:
                    st["i"] = i
                    ffn_part(tt, u0)
                    assert st["n"] - n0 == PART_CHUNKS * CHUNK
                st["i"] = None
                st["n"], st["u"], st["s"] = n0 + count * PART_CHUNKS * CHUNK, u0 + count * UNITS_FFN, s0 + count * PART_CHUNKS
                st["h"] += count * FH

            pe.wait_ge(silu_c, 1)
            for g in range(4):
                ada_rows(0, KD)
                ada_turn(ROWM, done=g == 3)
            norm(0, TT)
            for j in range(12):
                if j == 0:
                    pe.wait_ge(n_a, 8)
                tile(lambda kk: A[:, kk, :], KD, TT)
            tok_tiles(lambda kk, t: A[:, kk, t * P:(t + 1) * P], 4, 4)
            tok_tiles(lambda kk, t: A[:, kk, t * P:(t + 1) * P], 4, 4)
            u_q = 4
            for j in range(8):
                t = (Q0 if j < 4 else K0)[:, j % 4, 0:T]
                pe.wait_ge(gemm_free, u_q + j + 1)
                dup_unit(cn("rot"), t, T)
            pe.wait_ge(v_normed, 1)
            for t in range(4):
                b = unit_begin()
                for g in range(4):
                    mm(b[:, g * P:(g + 1) * P], VG[:, t, g * P:(g + 1) * P], pr("sgu_w", g * P, (g + 1) * P),
                       True, True, g == 3)
            ready_wait()


            def ada_step(s):
                if s and s % 4 == 0:
                    ada_turn(ROWM)
                ada_rows(2 * (s % 4), 2)

            attention(units_even(), ada_step)
            ada_turn(ROWM, done=True)
            SQ = SQM
            for h in range(4):
                pe.wait_ge(diff_sq, h + 1)
                dup_unit(cn("mean_e"), SQ[:, h, :], TT)
            ready_wait()
            for j in range(KD):
                tile(lambda kk: CAT0[:, kk, :], KD, TT)
            norm(1, TT)
            ready_wait()
            skip_to_chunk()
            for part in range(2):
                ffn_part(TT, st["u"], ada=part)
                st["h"] += FH

            norm(2, TT)
            pe.wait_ge(n_a, 24)
            u_q = st["u"]
            for j in range(10):
                tt = T if j < 8 else TT
                tile(lambda kk: A[:, kk, 0:tt], KD, tt)
            tok_tiles(lambda kk, t: A[:, kk, t * P:(t + 1) * P], 4, 2)
            for j in range(10):
                t = Q1[:, j, :] if j < 8 else K1[:, j - 8, 0:T]
                pe.wait_ge(gemm_free, u_q + j + 1)
                dup_unit(cn("rot"), t, T)
            ready_wait()
            for kv in range(4):
                dup_unit(cn(f"dup{kv % 2}"), K1[:, kv // 2, :], TT)
            ready_wait()
            attention(units_odd())
            ready_wait()
            for j in range(KD):
                tile(lambda kk: CAT1[:, kk, :], KD, T)
            norm(3, T)
            ready_wait()
            ffn(2, T)
            norm(4, T)
            pe.wait_ge(n_a, 40)

            for l in range(2):
                for j in range(22):
                    tile(lambda kk: X[:, kk, 0:T], KD, T)
                tile(lambda kk: X[:, kk, 0:T], KD, T, m=4)
                tok_tiles(lambda kk, t: X[:, kk, t * P:(t + 1) * P], 2, 1)
                tok_tiles(lambda kk, t: X[:, kk, t * P:(t + 1) * P], 2, 1)
                tok_tiles(lambda kk, t: X[:, kk, t * P:(t + 1) * P], 2, 2)
                ready_wait()
                dup_unit(cn("dup0"), SK[:, 0, :], T)
                dup_unit(cn("dup1"), SK[:, 0, :], T)
                dup_unit(cn("dup0"), DKI[:, 0, :], T)
                dup_unit(cn("dup1"), DKI[:, 0, :], T)
                ready_wait()
                st["p"] = 0
                attention(units_second(l)[:16])
                for qt in range(2):
                    for h in range(4):
                        b = (h % 2) * HD
                        dup_unit(DQI[b:b + HD, h // 2, qt * P:(qt + 1) * P], DKID[b:b + HD, 0, :], T)
                    pairs(FILL_INDEX[qt])
                ready_wait()
                pe.wait_ge(gemm_free, st["u"])
                attention(units_second(l)[16:])

                pairs(FILL_START)
                pe.wait_ge(rw_low, l + 1)
                for j in range(2):
                    dup_unit(pr(f"wa_up_{l}", j * P, (j + 1) * P)[0:64], LOW[0:64, 0, :], T)
                for j in range(2):
                    dup_unit(pr(f"wa_up_{l}", j * P, (j + 1) * P)[64:128], RP[64:128, 6, :], T)
                for j in range(2):
                    dup_unit(pr(f"g_up_{l}", j * P, (j + 1) * P), LOW[:, 1, :], T)
                pairs(FILL_LOW)
                ready_wait()
                b = unit_begin()
                mm(b[:, :], cn("blk64"), KNORM[:, :, :].rearrange("p a b -> p (a b)"), True, True, True)
                b = unit_begin()
                mm(b[:, :], cn("blk64"), RKK[:, :, :].rearrange("p a b -> p (a b)"), True, True, True)
                pairs(FILL_NORM)
                ready_wait()
                for src in (lambda j: KR[:, j, 0, :], lambda j: BH[:, j, :], lambda j: KH[:, j, :], lambda j: RP[:, 4 + j, :]):
                    b = unit_begin()
                    for cp in range(2):
                        for j in range(2):
                            ins = pe.transpose(b[:, (2 * cp + j) * P:(2 * cp + j + 1) * P], src(j)[:, cp * P:(cp + 1) * P], ident)
                    ins.then_inc(gemm_done, 1)
                for m in range(8):
                    b0, cp, j = m // 4 * HD, m // 2 % 2, m % 2
                    tok = slice(cp * P, (cp + 1) * P)
                    b = unit_begin()
                    rhs = KR[b0:b0 + HD, j, :, tok]
                    mm(b[:, 0:256].rearrange("p (a b) -> p a b", a=2), BH[b0:b0 + HD, j, tok], rhs, True, True)
                    mm(b[:, 256:512].rearrange("p (a b) -> p a b", a=2), KH[b0:b0 + HD, j, tok], rhs, True, True, True)
                for par in range(2):
                    b = unit_begin()
                    for h in range(4):
                        b0, cp, j = par * HD, h // 2, h % 2
                        tok = slice(cp * P, (cp + 1) * P)
                        mm(b[:, h * P:(h + 1) * P], KR[b0:b0 + HD, j, 0, tok], BH[b0:b0 + HD, j, tok], True, True, h == 3)
                pairs(FILL_MATRIX)
                for lev in range(5):
                    ready_wait()
                    for q in range(2):
                        b = unit_begin()
                        for h in range(4):
                            m = 4 * q + h
                            mm(b[:, h * P:(h + 1) * P], LK[:, m, :], XX[:, m, 0:P], True, True, h == 3)
                    pairs(FILL_LEVEL)
                    ready_wait()
                    for q in range(4):
                        b = unit_begin()
                        for h in range(2):
                            m = 2 * q + h
                            mm(b[:, 2 * h * P:(2 * h + 1) * P], XX[:, m, P:2 * P], PP[:, m, :], True, True)
                            mm(b[:, (2 * h + 1) * P:(2 * h + 2) * P], PP[:, m, :], XX[:, m, P:2 * P], True, True, h == 1)
                    pairs(FILL_LEVEL)
                ready_wait()
                b = unit_begin()
                for m in range(8):
                    mm(b[:, m * 64:(m + 1) * 64], MM[:, m, 256:384], TOK[3][:, m // 2 % 2, head_cols(m)],
                       True, True, m == 7)
                b = unit_begin()
                for m in range(8):
                    b0, cp, j = m // 4 * HD, m // 2 % 2, m % 2
                    mm(b[b0:b0 + HD, (2 * cp + j) * P:(2 * cp + j + 1) * P], TOK[0][:, cp, head_cols(m)],
                       XX[:, m, P:2 * P], True, True, m == 7)
                ready_wait()
                b = unit_begin()
                for m in range(8):
                    mm(b[:, m * 64:(m + 1) * 64], XX[:, m, P:2 * P], MVS[:, m, :], True, True, m == 7)
                ready_wait()
                for c in range(4):
                    cp, rb = c // 2, (c % 2) * 64
                    if c:
                        ready_wait()
                    for par in range(2):
                        b, b0 = unit_begin(), par * HD
                        for j in range(2):
                            mm(b[rb:rb + 64, j * 64:(j + 1) * 64], GTN[b0:b0 + HD, 2 * cp + j, rb:rb + 64],
                               STATE[b0:b0 + HD, c, j * 64:(j + 1) * 64], True, True, j == 1)
                    ready_wait()
                    b = unit_begin()
                    for n in range(4):
                        b0, j = n // 2 * HD, n % 2
                        o, hc = b[b0:b0 + HD, j * 64:(j + 1) * 64], head_cols(4 * (n // 2) + j)
                        mm(o, TOK[1][rb:rb + 64, cp, hc], SA[rb:rb + 64, n, :], True, False)
                        mm(o, TOK[2][rb:rb + 64, cp, hc], TOK[3][rb:rb + 64, cp, hc], False, True, n == 3)
                    b = unit_begin()
                    for n in range(4):
                        b0, j = n // 2 * HD, n % 2
                        mm(b[b0:b0 + HD, j * 64:(j + 1) * 64], STATE[b0:b0 + HD, c, j * 64:(j + 1) * 64],
                           KR[b0:b0 + HD, j, 1, c * 64:(c + 1) * 64], True, True, n == 3)
                    b = unit_begin()
                    for n in range(4):
                        b0, j = n // 2 * HD, n % 2
                        m = 4 * (n // 2) + 2 * cp + j
                        o = b[b0:b0 + HD, j * 64:(j + 1) * 64]
                        mm(o, SA[rb:rb + 64, n, :], MM[rb:rb + 64, m, 128 + rb:192 + rb], True, False)
                        mm(o, TOK[3][rb:rb + 64, cp, head_cols(m)], MM[rb:rb + 64, m, 384 + rb:448 + rb],
                           False, True, n == 3)
                ready_wait()
                dup_unit(cn("blk64"), YT[:, :, :].rearrange("p a b -> p (a b)"), 512)
                ready_wait()
                dup_unit(cn("blk64"), YS[:, :, :].rearrange("p a b -> p (a b)"), 512)
                ready_wait()

                pairs(KD)
                skip_to_chunk()
                ready_wait()
                for j in range(KD):
                    tile(lambda kk: ACC[:, kk, :], KD, T)
                ready_wait()
                norm(5 + 2 * l, T, layer_norm=True)
                pe.wait_ge(n_a, 8 * (6 + 2 * l))
                if l == 1:
                    rw = pr("router_w").rearrange("p (k e) -> p k e", k=KD)
                    for t in range(2):
                        b = unit_begin()
                        for kk in range(KD):
                            mm(b[:, 0:8], X[:, kk, t * P:(t + 1) * P], rw[:, kk, :], kk == 0, kk == KD - 1, kk == KD - 1)
                    ready_wait()
                    b = unit_begin()
                    for t in range(2):
                        ins = pe.transpose(b[0:8, t * P:(t + 1) * P], CWT[:, t, :], ident)
                    ins.then_inc(gemm_done, 1)
                    ready_wait()
                    for e in range(EXPERTS):
                        dup_unit(sel8[0:8, e, :], CWR[0:8, :], T)
                    ready_wait()
                ready_wait()
                ffn(2 if l == 0 else EXPERTS, T)
                norm(6 + 2 * l, T, layer_norm=True)
                if l == 0:
                    pe.wait_ge(n_a, 8 * 7)

        @block.scalar
        def _(act):
            st = dict(u=0, a=0, g=0, tmp=0, s=0, h=0, ada=0, p=0, used=[0, 0], i=None)
            SQ = SQM

            def f(o, i, fn, **kw):
                return nc.scalar.activation(o, i, fn, **kw)

            def copy_rows(row):
                act.wait_ge(ada_row, st["ada"] + 1)
                f(row[0:2, :], ROWS[0:2, :], ACT.Copy).then_inc(ada_copied, 1)
                st["ada"] += 1

            def norm(ni, tt, src, dst, scale, shift, eps, split=False, rows=0):
                SQ, RS = SQN(ni), RSN(ni)
                for j in range(KD):
                    if ni >= 5:
                        act.wait_ge(n_c, KD * (ni - 5) + j + 1)
                    f(SQ[:, j, 0:tt], src[:, j, 0:tt], ACT.Square).then_inc(n_sq, 1)
                for _ in range(rows):
                    copy_rows(ROWM)
                act.wait_ge(n_mm, ni + 1)
                f(RS[:, 0:tt], NORM[:, 0:tt], ACT.Sqrt, bias=eps).then_inc(n_root, 1)
                for j in range(KD):
                    act.wait_ge(n_x, KD * ni + j + 1)
                    for s in range(tt // T):
                        d = dst[:, j, s * T:(s + 1) * T]
                        if split:
                            ins = f(AH[:, j, s * T:(s + 1) * T], SQ[:, j, s * T:(s + 1) * T], ACT.Identity,
                                    scale=scale(j, s), bias=shift(j, s))
                        elif shift is None:
                            ins = f(d, d, ACT.Copy, scale=scale(j, s))
                        else:
                            ins = f(d, d, ACT.Identity, scale=scale(j, s), bias=shift(j, s))
                    ins.then_inc(n_a, 1)

            def attention(us, rows=False):
                gs, ng = groups(us)
                a0, g0 = st["a"], st["g"]
                for s in range(len(us) + 2):
                    if s < len(us):
                        u, a = us[s], a0 + s
                        act.wait_ge(at_m, a + 1)
                        if s >= 4:
                            if us[s - 4]["last"]:
                                act.wait_ge(at_t, g0 + gs[s - 4] + 1)
                            else:
                                act.wait_ge(at_n, a - 2)
                        src = bank[s % 2][:, 0:u["nk"]] if u["mask"] is None else SM[:, a % 2, 0:u["nk"]]
                        c = slice(a % 4, a % 4 + 1)
                        ins = f(E[:, a % 4, 0:u["nk"]], src, ACT.Exp, bias=nm[:, c], scale=SCALE, accum_out=sm[:, c])
                        if u["sink"] is not None:
                            ins = f(es[:, c], SINK(u["sink"]), ACT.Exp, bias=nm[:, c])
                        ins.then_inc(at_e, 1)
                    if s >= 2 and us[s - 2]["last"]:
                        u, g = us[s - 2], gs[s - 2]
                        act.wait_ge(at_t, g0 + g + 1)
                        if g >= 2:
                            act.wait_ge(at_o, g0 + g - 1)
                        f(ET[:, g % 2, 0:u["nk"]], bank[2 + g % 2][:, 0:u["nk"]], ACT.Copy).then_inc(at_tv, 1)
                    if rows and 1 <= s <= len(us) and s % 4 == 0:
                        copy_rows(ROWM)
                st["a"] += len(us)
                st["g"] += ng

            def val(x, per):
                return x if st["i"] is None else st["i"] * per + x

            def gates(l, n):
                for i, j in PAIRS[st["p"]:st["p"] + n]:
                    c = st["u"]
                    act.wait_ge(gemm_done, c + 1)
                    if st["p"] >= 2:
                        act.wait_ge(gemm_free, st["used"][st["p"] % 2])
                    f(GATE[:, st["p"] % 2, :], bank[c % BANKS][:, 0:T], ACT.Sigmoid,
                      bias=pr(f"gate_b_{l}", i * KD + j, i * KD + j + 1)).then_inc(act_tmp, 1)
                    st["u"] += 2
                    st["used"][st["p"] % 2] = st["u"]
                    st["tmp"] += 1
                    st["p"] += 1

            def high_parts(c0, upto):
                while st["c"] < upto:
                    c, s = c0 + st["c"], st["s"] + st["c"]
                    act.wait_ge(w_loaded[c % RING], val(16 * (c // RING + 1), 16 * PART_CHUNKS // RING))
                    if s >= SPLIT:
                        act.wait_ge(split_begun, val(s - SPLIT + 2, PART_CHUNKS))
                    f(WH[:, s % SPLIT, :], ring[:, c % RING, :], ACT.Copy).then_inc(w_hi, 1)
                    st["c"] += 1

            def ffn_part(c0, tt, ada):
                u0 = st["u"]
                st["c"] = 0
                for q in range(FH):
                    u = u0 + 2 * q
                    high_parts(c0, gate_chunks(q, ada) + AHEAD)
                    if ada and q and ADA_HALVES[q - 1][-1] % 2:
                        copy_rows(ROWF)
                    act.wait_ge(gemm_done, val(u + 1, UNITS_FFN))
                    if st["h"] + q >= 2:
                        act.wait_ge(h_lo, val(st["h"] + q - 1, FH))
                    f(TMP[:, q % 2, 0:tt], bank[u % BANKS][:, 0:tt], ACT.Silu).then_inc(act_tmp, 1)
                    high_parts(c0, gate_chunks(q, ada) + 2 + AHEAD)
                    act.wait_ge(gemm_free, val(u + 2, UNITS_FFN))
                    f(HH[:, q, 0:tt], TMP[:, q % 2, 0:tt], ACT.Copy).then_inc(h_hi, 1)
                if ada:
                    high_parts(c0, gate_chunks(FH, ada) - 2 + AHEAD)
                    copy_rows(ROWF)
                high_parts(c0, part_chunks(ada))

            def ffn(k, count, tt, ada=False):
                c0, u0 = FFN_START[k], st["u"]
                if ada:
                    for part in range(count):
                        ffn_part(FFN_START[k + part], tt, True)
                        st["u"] += UNITS_FFN
                        st["s"] += part_chunks(True)
                        st["h"] += FH
                        st["tmp"] += FH
                    return
                with act.Fori(0, count) as i:
                    st["i"] = i
                    ffn_part(c0, tt, False)
                st["i"] = None
                st["u"] = u0 + count * UNITS_FFN
                st["s"] += count * PART_CHUNKS
                st["h"] += count * FH
                st["tmp"] += count * FH

            act.wait_ge(inputs_in, 48)
            f(cs, pr("cvec"), ACT.Silu).then_inc(silu_c, 1)
            act.wait_ge(silu_c, 1)
            f(csH[:, :], cs, ACT.Copy).then_inc(a_hi, 1)
            norm_mod = lambda l, n: (lambda j, s: modg[:, 2 * l + n, j, s:s + 1])
            norm_sh = lambda l, n: (lambda j, s: mod[:, l, 24 * n + j, s:s + 1])
            norm(0, TT, X, A, norm_mod(0, 0), norm_sh(0, 0), pr("eps6"), rows=4)
            for j in range(4):
                act.wait_ge(gemm_free, j + 1)
                f(U0[:, j, :], U0[:, j, :], ACT.Gelu)
            for t in range(4):
                act.wait_ge(gemm_free, 12 + t + 1)
                f(VT[:, t, :], VT[:, t, :], ACT.Gelu).then_inc(gelu_v, 1)
            act.wait_ge(v_var, 1)
            f(VRS, VRS, ACT.Sqrt, bias=pr("eps6")).then_inc(v_root, 1)
            act.wait_ge(lam_sum, 1)
            f(lam[:, 2:4], lam[:, 0:2], ACT.Exp).then_inc(lam_exp, 1)
            st["u"] = 20
            attention(units_even(), rows=True)
            for h in range(4):
                act.wait_ge(at_out, 8 + 2 * (h + 1))
                f(SQ[:, h, :], CAT0[:, 4 + h, :], ACT.Square).then_inc(diff_sq, 1)
            act.wait_ge(diff_var, 1)
            f(SQ[:, 4:8, :], SQ[:, 4:8, :], ACT.Sqrt, bias=pr("eps6")).then_inc(diff_root, 1)
            act.wait_ge(gemm_free, 20 + 8 + 4 + 4 + 8)
            norm(1, TT, X, A, norm_mod(0, 1), norm_sh(0, 1), pr("eps6"), split=True)
            st["u"] = 44
            ffn(0, 2, TT, ada=True)
            act.wait_ge(gemm_free, st["u"])
            act.wait_ge(mod_ready, 1)
            norm(2, TT, X, A, norm_mod(1, 0), norm_sh(1, 0), pr("eps6"))
            st["u"] += 10 + 4 + 10 + 4
            SINK = lambda h: pr("odd_sink", h, h + 1)
            attention(units_odd())
            st["u"] += KD
            act.wait_ge(gemm_free, st["u"])
            norm(3, T, X, A, norm_mod(1, 1), norm_sh(1, 1), pr("eps6"), split=True)
            ffn(2, 2, T)
            act.wait_ge(gemm_free, st["u"])
            norm(4, T, X, X, lambda j, s: pr("final_g", j, j + 1), None, pr("eps6"))

            for l in range(2):
                SINK = lambda h: pr(f"sinks_{l}", h, h + 1)
                act.wait_ge(fox_pre, l + 1)
                f(FC[0:4, 3, :], FC[0:4, 2, :], ACT.Exp).then_inc(fox_e, 1)
                act.wait_ge(fox_e, l + 1)
                f(FC[0:4, 3, :], FC[0:4, 3, :], ACT.Ln, bias=1.0).then_inc(fox_ln, 1)
                st["p"], st["u"] = 0, UB[l]["index"]
                attention(units_second(l)[:16])
                for qt in range(2):
                    st["u"] += 4
                    gates(l, FILL_INDEX[qt])
                attention(units_second(l)[16:])
                act.wait_ge(rw_shift, l + 1)
                f(LOW[0:64, 0, :], RP[0:64, 6, :], ACT.Tanh)
                f(LOW[:, 1, :], RP[:, 7, :], ACT.Sigmoid).then_inc(rw_low, 1)
                gates(l, FILL_START)
                st["u"] += 6
                act.wait_ge(rw_sig, l + 1)
                f(LWV, LWV, ACT.Sigmoid)
                f(AV, AV, ACT.Sigmoid).then_inc(rw_pre, 1)
                act.wait_ge(rw_c, l + 1)
                f(EC, CC, ACT.Exp)
                f(EN, CC, ACT.Exp, scale=-1.0)
                f(EX, EX, ACT.Exp).then_inc(rw_exp, 1)
                gates(l, FILL_LOW)
                st["u"] += 2
                act.wait_ge(rw_ks, l + 1)
                f(KNORM, KNORM, ACT.Sqrt).then_inc(rw_kroot, 1)
                gates(l, FILL_NORM)
                st["u"] += 4 + 8 + 2
                gates(l, FILL_MATRIX)
                for lev in range(5):
                    st["u"] += 2
                    gates(l, FILL_LEVEL)
                    st["u"] += 4
                    gates(l, FILL_LEVEL)
                act.wait_ge(rw_var, l + 1)
                f(YS, YS, ACT.Sqrt, bias=pr("epsgn")).then_inc(rw_vroot, 1)
                st["u"] = UB[l]["merge"]
                gates(l, KD)
                norm(5 + 2 * l, T, X, X, lambda j, s: pr(f"ln1g_{l}", j, j + 1),
                     lambda j, s: pr(f"ln1b_{l}", j, j + 1), pr("eps5"))
                for j in range(KD):
                    act.wait_ge(n_a, KD * (5 + 2 * l) + j + 1)
                    f(AH[:, j, 0:T], X[:, j, 0:T], ACT.Copy).then_inc(a_hi, 1)
                if l == 1:
                    act.wait_ge(top_v, 1)
                    f(EE[:, 0:2], EE[:, 0:2], ACT.Exp).then_inc(top_e, 1)
                st["u"] = UB[l]["ffn"]
                ffn(4 + 2 * l, 2 if l == 0 else EXPERTS, T)
                norm(6 + 2 * l, T, X, X, lambda j, s: pr(f"ln2g_{l}", j, j + 1),
                     lambda j, s: pr(f"ln2b_{l}", j, j + 1), pr("eps5"))

        @block.vector
        def _(dve):
            V = nc.vector
            st = dict(u=0, a=0, g=0, tmp=0, chain=0, s=0, h=0, p=0, i=None)
            SQ = SQM

            def link(ins):
                st["chain"] += 1
                ins.then_inc(dve_chain, 1)
                dve.wait_ge(dve_chain, st["chain"])

            def take():
                dve.wait_ge(gemm_done, st["u"] + 1)
                st["u"] += 1
                return bank[(st["u"] - 1) % BANKS]

            def free(ins):
                ins.then_inc(gemm_free, 1)

            def settled_but_last():
                dve.wait_ge(gemm_free, st["u"] - 1)

            def settled():
                dve.wait_ge(gemm_free, st["u"])

            marks = {}

            def mark(semaphore):
                n, slot = marks.get(semaphore.name, (0, len(marks)))
                if n:
                    dve.wait_ge(semaphore, n)
                marks[semaphore.name] = (n + 1, slot)
                V.memset(small(140 + slot, 1), 0.0).then_inc(semaphore, 1)

            def go():
                mark(ready)

            def copy_units(dsts, m=P):
                for d in dsts:
                    free(V.tensor_copy(d, take()[0:d.shape[0], 0:d.shape[1]]))

            def norm(ni, tt, src, dst, split=None):
                SQ, RS = SQN(ni), RSN(ni)
                dst = SQ if split else dst
                if ni >= 5:
                    dve.wait_ge(n_mean, ni - 4)
                    for j in range(KD):
                        V.tensor_tensor(src[:, j, 0:tt], src[:, j, 0:tt], MEAN[:, 0:tt], ALU.subtract).then_inc(n_c, 1)
                dve.wait_ge(n_root, ni + 1)
                link(V.reciprocal(RS[:, 0:tt], RS[:, 0:tt]))
                if ni >= 5:
                    dve.wait_ge(n_c, KD * (ni - 4))
                for j in range(KD):
                    V.tensor_tensor(dst[:, j, 0:tt], src[:, j, 0:tt], RS[:, 0:tt], ALU.mult).then_inc(n_x, 1)
                if split:
                    scale, shift = split
                    dve.wait_ge(n_x, KD * (ni + 1))
                    for j in range(KD):
                        for s in range(tt // T):
                            ins = V.tensor_scalar(TMP[:, j % 2, s * T:(s + 1) * T], SQ[:, j, s * T:(s + 1) * T],
                                                  scale(j, s), shift(j, s), ALU.mult, ALU.add)
                        link(ins)
                        dve.wait_ge(n_a, KD * ni + j + 1)
                        ins = V.tensor_tensor(AL[:, j, 0:tt], TMP[:, j % 2, 0:tt], AH[:, j, 0:tt].bitcast(F32), ALU.subtract)
                        link(ins)
                    go()

            def rope(q, j):
                b = take()[:, 0:T]
                dve.wait_ge(gemm_free, st["u"] - 1)
                link(V.tensor_tensor(RT1[:, 0, :], b, cn("sin"), ALU.mult))
                link(V.tensor_tensor(RT1[:, 1, :], q, cn("cos"), ALU.mult))
                free(V.tensor_tensor(q, RT1[:, 0, :], RT1[:, 1, :], ALU.add))

            def attention(us, diff=False):
                gs, ng = groups(us)
                a0, g0 = st["a"], st["g"]
                for s in range(len(us) + 4):
                    if s < len(us):
                        u, a = us[s], a0 + s
                        c = slice(a % 4, a % 4 + 1)
                        b = bank[s % 2][:, 0:u["nk"]]
                        dve.wait_ge(at_s, a + 1)
                        if s >= 2:
                            dve.wait_ge(at_e, a - 1)
                        if u["mask"] is not None:
                            link(V.tensor_tensor_reduce(SM[:, a % 2, 0:u["nk"]], b, u["mask"], 1.0, OUT_OF_LIST,
                                                        ALU.add, ALU.max, mx[:, c]))
                        else:
                            link(V.reduce_max(mx[:, c], b, AX_X))
                        if u["sink"] is not None:
                            V.tensor_scalar(nm[:, c], mx[:, c], -SCALE, nsink[:, u["sink"]:u["sink"] + 1],
                                            ALU.mult, ALU.min).then_inc(at_m, 1)
                        else:
                            V.tensor_scalar(nm[:, c], mx[:, c], -SCALE, None, ALU.mult).then_inc(at_m, 1)
                    if 1 <= s <= len(us):
                        u, a = us[s - 1], a0 + s - 1
                        c = slice(a % 4, a % 4 + 1)
                        e = E[:, a % 4, 0:u["nk"]]
                        dve.wait_ge(at_e, a + 1)
                        if u["sink"] is not None:
                            link(V.tensor_tensor(sm[:, c], sm[:, c], es[:, c], ALU.add))
                        link(V.reciprocal(rc[:, c], sm[:, c]))
                        if not diff or not u["last"]:
                            V.tensor_scalar(e, e, rc[:, c], None, ALU.mult).then_inc(at_n, 1)
                        else:
                            link(V.tensor_tensor(r2[:, c], rc[:, c], lam[:, 4:5], ALU.mult))
                            dve.wait_ge(at_n, a)
                            V.scalar_tensor_tensor(e, e, r2[:, c], E[:, (a - 1) % 4, 0:u["nk"]],
                                                   ALU.mult, ALU.add).then_inc(at_n, 1)
                    if s >= 4 and us[s - 4]["last"]:
                        u, g = us[s - 4], gs[s - 4]
                        b0, m = u["dst"].base_partition(), u["dst"].shape[0]
                        dve.wait_ge(at_o, g0 + g + 1)
                        V.tensor_copy(u["dst"], bank[4 + g % 2][b0:b0 + m, 0:P]).then_inc(at_out, 1)
                st["a"] += len(us)
                st["g"] += ng

            def val(x, per):
                return x if st["i"] is None else st["i"] * per + x

            def pairs(n):
                for i, j in PAIRS[st["p"]:st["p"] + n]:
                    k = st["p"] % 2
                    st["u"] += 1
                    b = take()[:, 0:T]
                    st["tmp"] += 1
                    dve.wait_ge(act_tmp, st["tmp"])
                    if i == 0:
                        for s in range(2):
                            c = slice(s * P, (s + 1) * P)
                            free(V.tensor_tensor(ACC[:, j, c], b[:, c], GATE[:, k, c], ALU.mult))
                    else:
                        free(V.tensor_tensor(PROD[:, k, :], b, GATE[:, k, :], ALU.mult))
                        dve.wait_ge(gemm_free, st["u"] - 1)
                        free(V.tensor_tensor(ACC[:, j, :], ACC[:, j, :], PROD[:, k, :], ALU.add))
                    st["p"] += 1

            def low_parts(c0, upto):
                while st["c"] < upto:
                    c, s = c0 + st["c"], st["s"] + st["c"]
                    dve.wait_ge(w_hi, val(s + 1, PART_CHUNKS))
                    V.tensor_tensor(WL[:, s % SPLIT, :], ring[:, c % RING, :], WH[:, s % SPLIT, :].bitcast(F32),
                                    ALU.subtract).then_inc(w_taken, 1)
                    st["c"] += 1

            def hidden_low(q, tt):
                dve.wait_ge(h_hi, val(st["h"] + q + 1, FH))
                V.tensor_tensor(HL[:, q, 0:tt], TMP[:, q % 2, 0:tt], HH[:, q, 0:tt].bitcast(F32), ALU.subtract).then_inc(h_lo, 1)

            def ffn_part(c0, tt, gate, ada, experts):
                u0, h = st["u"], tt // 2
                st["c"] = 0
                for q in range(FH):
                    u = u0 + 2 * q + 1
                    low_parts(c0, gate_chunks(q, ada) + 2 + AHEAD)
                    dve.wait_ge(gemm_done, val(u + 1, UNITS_FFN))
                    dve.wait_ge(act_tmp, val(st["tmp"] + q + 1, FH))
                    if experts:
                        V.tensor_tensor(TMP[:, q % 2, 0:T], TMP[:, q % 2, 0:T], CW[:, st["i"], :], ALU.mult).then_inc(cw_done, 1)
                        dve.wait_ge(cw_done, val(q + 1, FH))
                    for s in range(2):
                        free(V.tensor_tensor(TMP[:, q % 2, s * h:(s + 1) * h], TMP[:, q % 2, s * h:(s + 1) * h],
                                             bank[u % BANKS][:, s * h:(s + 1) * h], ALU.mult))
                    if q:
                        hidden_low(q - 1, tt)
                hidden_low(FH - 1, tt)
                for j in range(KD):
                    u = u0 + 2 * FH + j
                    low_parts(c0, min(part_chunks(ada), gate_chunks(FH, ada) - 2 + -(-FH * (j + 1) // CHUNK) + AHEAD))
                    dve.wait_ge(gemm_done, val(u + 1, UNITS_FFN))
                    dve.wait_ge(gemm_free, val(u - UNITS_FFN + 1, UNITS_FFN))
                    residual(j, bank[u % BANKS], tt, gate)

            def ffn(k, count, tt, gate, ada=False, experts=False):
                c0, u0 = FFN_START[k], st["u"]
                dve.wait_ge(gemm_done, u0)
                if ada:
                    for part in range(count):
                        ffn_part(FFN_START[k + part], tt, gate, True, False)
                        st["u"] += UNITS_FFN
                        st["s"] += part_chunks(True)
                        st["h"] += FH
                        st["tmp"] += FH
                    return
                with dve.Fori(0, count) as i:
                    st["i"] = i
                    ffn_part(c0, tt, gate, False, experts)
                st["i"] = None
                st["u"] = u0 + count * UNITS_FFN
                st["s"] += count * PART_CHUNKS
                st["h"] += count * FH
                st["tmp"] += count * FH

            def residual(j, b, tt, gate):
                for s in range(tt // T):
                    cols = slice(s * T, (s + 1) * T)
                    if gate is None:
                        ins = V.tensor_tensor(X[:, j, cols], X[:, j, cols], b[:, cols], ALU.add)
                    else:
                        ins = V.scalar_tensor_tensor(X[:, j, cols], b[:, cols], gate(j, s), X[:, j, cols],
                                                     ALU.mult, ALU.add)
                free(ins)

            def modulation(l, lo, hi):
                n = 2 * (hi - lo)
                src = ADA[:, 2 * lo:2 * hi].rearrange("p (j s) -> p j s", s=2)
                bias = pr(f"ada_b{l}", lo, hi).unsqueeze(2).broadcast_to([P, hi - lo, 2])
                link(V.tensor_tensor(mod[:, l, lo:hi, :], src, bias, ALU.add))

            def gains(l, n, name):
                g = pr(f"{name}{l}").unsqueeze(2).broadcast_to([P, KD, 2])
                return V.scalar_tensor_tensor(modg[:, 2 * l + n, :, :], mod[:, l, 24 * n + 8:24 * n + 16, :], 1.0, g,
                                              ALU.add, ALU.mult)

            dve.wait_ge(a_hi, 1)
            link(V.tensor_tensor(csL[:, :], cs, csH[:, :].bitcast(F32), ALU.subtract))
            dve.wait_ge(ada_done, 1)
            modulation(0, 0, 16)
            link(gains(0, 0, "n1g"))
            norm(0, TT, X, A)
            copy_units([U0[:, j, :] for j in range(4)] + [Q0[:, j, :] for j in range(4)] + [K0[:, j, :] for j in range(4)])
            copy_units([VT[:, t, :] for t in range(4)] + [VV[:, t, :] for t in range(4)])
            settled()
            for j in range(8):
                rope((Q0 if j < 4 else K0)[:, j % 4, 0:T], j)
            settled()
            dve.wait_ge(gelu_v, 4)
            for t in range(4):
                for g in range(4):
                    V.bn_stats(ST6[:, 4 * t + g, :], VT[:, t, g * P:(g + 1) * P])
            link(V.memset(small(159, 1), 0.0))
            for n in range(16):
                ins = V.bn_aggr(MV2[:, n, :], ST6[:, n, :])
            link(ins)
            V.tensor_copy(VRS, MV2[:, :, 1]).then_inc(v_var, 1)
            ll = pr("lqk").rearrange("p (a b) -> p a b", a=4)
            V.tensor_tensor_reduce(SQ[:, 7, 0:64], ll[:, 0, :], ll[:, 1, :], 1.0, 0.0, ALU.mult, ALU.add, lam[:, 0:1])
            V.tensor_tensor_reduce(SQ[:, 7, 64:128], ll[:, 2, :], ll[:, 3, :], 1.0, 0.0, ALU.mult, ALU.add,
                                   lam[:, 1:2]).then_inc(lam_sum, 1)
            dve.wait_ge(v_root, 1)
            link(V.reciprocal(VRS, VRS))
            for t in range(4):
                for g in range(4):
                    n = 4 * t + g
                    ins = V.tensor_scalar(VG[:, t, g * P:(g + 1) * P], VT[:, t, g * P:(g + 1) * P], MV2[:, n, 0:1],
                                          VRS[:, n:n + 1], ALU.subtract, ALU.mult)
            ins.then_inc(v_normed, 1)
            dve.wait_ge(lam_exp, 1)
            link(V.tensor_tensor(lam[:, 5:6], lam[:, 3:4], lam[:, 2:3], ALU.subtract))
            link(V.tensor_scalar(lam[:, 4:5], lam[:, 5:6], -LAM_INIT, None, ALU.add))
            link(V.tensor_scalar(lam[:, 6:7], pr("subln"), 1.0 - LAM_INIT, None, ALU.mult))
            sgub = pr("sgu_b").rearrange("p (g c) -> p g c", g=4)
            for t in range(4):
                b = take()[:, :].rearrange("p (g c) -> p g c", g=4)
                link(V.tensor_tensor(CAT0[:, 0:4, t * P:(t + 1) * P], b, sgub, ALU.add))
                free(V.tensor_tensor(CAT0[:, 0:4, t * P:(t + 1) * P], CAT0[:, 0:4, t * P:(t + 1) * P],
                                     U0[:, :, t * P:(t + 1) * P], ALU.mult))
            settled()
            go()
            attention(units_even(), diff=True)
            dve.wait_ge(ada_done, 2)
            modulation(0, 16, 48)
            link(gains(0, 1, "n2g"))
            copy_units([SQ[:, 4 + h, :] for h in range(4)])
            settled()
            mark(diff_var)
            dve.wait_ge(diff_root, 1)
            link(V.reciprocal(SQ[:, 4:8, :], SQ[:, 4:8, :]))
            link(V.scalar_tensor_tensor(CAT0[:, 4:8, :], CAT0[:, 4:8, :], lam[:, 6:7], SQ[:, 4:8, :], ALU.mult, ALU.mult))
            go()
            for j in range(KD):
                residual(j, take(), TT, lambda j, s: mod[:, 0, 16 + j, s:s + 1])
            settled()
            norm(1, TT, X, A, (lambda j, s: modg[:, 1, j, s:s + 1], lambda j, s: mod[:, 0, 24 + j, s:s + 1]))
            ffn(0, 2, TT, lambda j, s: mod[:, 0, 40 + j, s:s + 1], ada=True)
            dve.wait_ge(ada_done, 3)
            modulation(1, 0, 48)
            link(gains(1, 0, "n1g"))
            gains(1, 1, "n2g").then_inc(mod_ready, 1)

            settled()
            norm(2, TT, X, A)
            copy_units([Q1[:, j, :] for j in range(8)] + [K1[:, j, :] for j in range(2)] + [V1[:, t, :] for t in range(4)])
            link(V.tensor_scalar(nsink[:, 0:16], pr("odd_sink"), -1.0, None, ALU.mult))
            settled()
            for j in range(10):
                rope(Q1[:, j, :] if j < 8 else K1[:, j - 8, 0:T], j)
            settled()
            go()
            copy_units([KD1[:, kv, :] for kv in range(4)])
            settled()
            go()
            attention(units_odd())
            go()
            for j in range(KD):
                residual(j, take(), T, lambda j, s: mod[:, 1, 16 + j, s:s + 1])
            settled()
            norm(3, T, X, A, (lambda j, s: modg[:, 3, j, s:s + 1], lambda j, s: mod[:, 1, 24 + j, s:s + 1]))
            ffn(2, 2, T, lambda j, s: mod[:, 1, 40 + j, s:s + 1])
            settled()
            norm(4, T, X, X)

            for l in range(2):
                copy_units([SQ_[:, j, :] for j in range(4)] + [SK[:, 0, :]] + [RP[:, j, :] for j in range(8)]
                           + [FQ[:, j, :] for j in range(2)] + [FK[:, j, :] for j in range(2)]
                           + [DQ[:, j, :] for j in range(2)] + [DQI[:, j, :] for j in range(2)] + [DKI[:, 0, :]])
                free(V.tensor_scalar(FC[0:4, 1, :], take()[0:4, 0:T], pr(f"fbias_{l}")[0:4], None, ALU.add))
                copy_units([SV[:, t, :] for t in range(2)] + [DV[:, t, :] for t in range(2)] + [FV[:, t, :] for t in range(2)])
                link(V.tensor_scalar(nsink[:, 0:8], pr(f"sinks_{l}"), -1.0, None, ALU.mult))
                settled()
                go()
                link(V.tensor_scalar(FC[0:4, 0, :], FC[0:4, 1, :], -1.0, None, ALU.mult))
                V.tensor_tensor(FC[0:4, 2, :], FC[0:4, 0, :], FC[0:4, 1, :], ALU.min).then_inc(fox_pre, 1)
                copy_units([SKD[:, 0, :], SKD[:, 1, :], DKD[:, 0, :], DKID[:, 0, :]])
                settled()
                go()
                st["p"] = 0
                attention(units_second(l)[:16])
                assert st["u"] == UB[l]["index"]
                dve.wait_ge(fox_ln, l + 1)
                link(V.tensor_scalar(FC[0:4, 1, :], FC[0:4, 1, :], 0.0, None, ALU.min))
                link(V.tensor_tensor(FC[0:4, 1, :], FC[0:4, 1, :], FC[0:4, 3, :], ALU.subtract))
                link(V.memset(FC[0:4, 3, :], 1.0))
                link(V.tensor_tensor_scan(FC[0:4, 2, :], FC[0:4, 3, :], FC[0:4, 1, :], 0.0, ALU.mult, ALU.add))
                V.tensor_scalar(FC[0:4, 0, :], FC[0:4, 2, :], 1.0 / SCALE, None, ALU.mult)
                link(V.tensor_scalar(FC[0:4, 1, :], FC[0:4, 2, :], -1.0 / SCALE, None, ALU.mult))
                for qt in range(2):
                    for h in range(4):
                        b = take()[:, 0:T]
                        w = DV[:, qt, HD + h:HD + h + 1]
                        if h == 0:
                            ins = V.tensor_scalar(DSC, b, 0.0, w, ALU.max, ALU.mult)
                            free(ins)
                        else:
                            free(V.tensor_scalar(DT, b, 0.0, w, ALU.max, ALU.mult))
                            settled()
                            link(V.tensor_tensor(DSC, DSC, DT, ALU.add))
                    link(V.tensor_tensor(DSC, DSC, cn("chunks", qt * T, (qt + 1) * T), ALU.add))
                    src = DSC
                    for r in range(8):
                        link(V.max(M8[:, 0:8], src))
                        link(V.match_replace(DWK, M8[:, 0:8], src, OUT_OF_LIST))
                        src = DWK
                    link(V.tensor_scalar(DMK[:, qt, :], DWK, OUT_OF_LIST / 2, NEG, ALU.is_gt, ALU.mult))
                    if qt:
                        go()
                    pairs(FILL_INDEX[qt])
                attention(units_second(l)[16:])

                dve.wait_ge(at_out, st["g"])
                V.tensor_tensor(DELTA[:, :, 1:T], RP[:, :, 0:T - 1], RP[:, :, 1:T], ALU.subtract)
                link(V.tensor_scalar(DELTA[:, :, 0:1], RP[:, :, 0:1], -1.0, None, ALU.mult))
                for j in range(KD):
                    ins = V.scalar_tensor_tensor(RP[:, j, :], DELTA[:, j, :], pr(f"mu_{l}", j, j + 1), RP[:, j, :],
                                                 ALU.mult, ALU.add)
                link(ins)
                mark(rw_shift)
                pairs(FILL_START)
                for j in range(2):
                    free(V.tensor_scalar(LWV[:, j, :], take()[:, 0:T], pr(f"w0_{l}", j, j + 1), None, ALU.add))
                for j in range(2):
                    free(V.tensor_scalar(AV[:, j, :], take()[:, 0:T], pr(f"a0_{l}", j, j + 1), None, ALU.add))
                copy_units([GV[:, j, :] for j in range(2)])
                settled()
                mark(rw_sig)
                dve.wait_ge(rw_pre, l + 1)
                link(V.tensor_scalar(LWV, LWV, -float(np.exp(-0.5)), None, ALU.mult))
                for j in range(2):
                    ins = V.tensor_tensor_scan(CC[:, j, :], cn("segs"), LWV[:, j, :], 0.0, ALU.mult, ALU.add)
                link(ins)
                V.tensor_tensor(EX, CC, LWV, ALU.subtract).then_inc(rw_c, 1)
                for j in range(2):
                    ins = V.tensor_scalar(KK[:, j, :], RP[:, 2 + j, :], pr(f"kk_{l}", j, j + 1), None, ALU.mult)
                link(ins)
                V.tensor_tensor(KNORM, KK, KK, ALU.mult)
                for j in range(2):
                    ins = V.tensor_scalar(BON[:, j, :], AV[:, j, :], -1.0, pr(f"ka_{l}", j, j + 1), ALU.add, ALU.mult)
                link(ins)
                link(V.scalar_tensor_tensor(RP[:, 2:4, :], BON, 1.0, RP[:, 2:4, :], ALU.add, ALU.mult))
                for j in range(2):
                    ins = V.scalar_tensor_tensor(RKK[:, j, :], RP[:, j, :], pr(f"rk_{l}", j, j + 1), RP[:, 2 + j, :],
                                                 ALU.mult, ALU.mult)
                link(ins)
                go()
                pairs(FILL_LOW)
                b = take()
                kn = KNORM[:, :, :].rearrange("p a b -> p (a b)")
                free(V.tensor_scalar(kn, b[:, :], 1e-12, None, ALU.add))
                settled()
                mark(rw_ks)
                b = take()
                free(V.tensor_tensor(BON, b[:, :].rearrange("p (a b) -> p a b", a=2), RP[:, 4:6, :], ALU.mult))
                dve.wait_ge(rw_kroot, l + 1)
                link(V.reciprocal(KNORM, KNORM))
                link(V.tensor_tensor(KK, KK, KNORM, ALU.mult))
                dve.wait_ge(rw_exp, l + 1)
                V.tensor_tensor(KR[:, :, 0, :], KK, EX, ALU.mult)
                V.tensor_tensor(KR[:, :, 1, :], RP[:, 0:2, :], EC, ALU.mult)
                V.tensor_tensor(KH, RP[:, 2:4, :], EN, ALU.mult)
                link(V.tensor_tensor(BH, KK, AV, ALU.mult))
                link(V.tensor_tensor(BH, BH, EN, ALU.mult))
                go()
                pairs(FILL_NORM)
                for n in range(4):
                    free(V.tensor_copy(TOK[n][:, :, :].rearrange("p a b -> p (a b)"), take()[:, :]))
                for m in range(8):
                    free(V.tensor_tensor(MM[:, m, :], take()[:, :], cn("pairmask"), ALU.mult))
                for cp in range(2):
                    b = take()[:, :].rearrange("p (m c) -> p m c", m=4)
                    free(V.tensor_tensor(XX[:, 4 * cp:4 * cp + 4, 0:P], b, over(cn("inv0"), 4), ALU.mult))
                settled()
                link(V.tensor_tensor(XX[:, :, P:2 * P], MM[:, :, 0:P], over(cn("inv0t"), 8), ALU.mult))
                xx = XX[:, :, :].rearrange("p m (a c) -> p (m a) c", a=2)
                link(V.tensor_tensor(xx, xx, over(ident, 16), ALU.add))
                for lev in range(5):
                    link(V.tensor_tensor(LK, MM[:, :, 0:P], over(cn("levels", lev * P, (lev + 1) * P), 8), ALU.mult))
                    go()
                    pairs(FILL_LEVEL if lev else FILL_MATRIX)
                    for q in range(2):
                        free(V.tensor_copy(PP[:, 4 * q:4 * q + 4, :].rearrange("p a b -> p (a b)"), take()[:, :]))
                    settled()
                    go()
                    pairs(FILL_LEVEL)
                    for q in range(4):
                        x2 = XX[:, 2 * q:2 * q + 2, :].rearrange("p a b -> p (a b)")
                        free(V.tensor_tensor(x2, x2, take()[:, :], ALU.subtract))
                    settled()
                go()
                pairs(FILL_LEVEL)
                free(V.tensor_copy(MVS[:, :, :].rearrange("p a b -> p (a b)"), take()[:, :]))
                free(V.tensor_scalar(GTN[:, :, :].rearrange("p a b -> p (a b)"), take()[:, :], -1.0, None, ALU.mult))
                settled()
                go()
                free(V.tensor_scalar(U0N[:, :, :].rearrange("p a b -> p (a b)"), take()[:, :], -1.0, None, ALU.mult))
                link(V.memset(STATE[:, 0, :], 0.0))
                settled()
                go()
                for c in range(4):
                    cp, rb = c // 2, (c % 2) * 64
                    for par in range(2):
                        b = take()[rb:rb + 64, 0:P].rearrange("p (a b) -> p a b", a=2)
                        m = 4 * par + 2 * cp
                        free(V.tensor_tensor(SA[rb:rb + 64, 2 * par:2 * par + 2, :], b, U0N[rb:rb + 64, m:m + 2, :], ALU.add))
                    settled()
                    go()
                    b = take()
                    if c < 3:
                        link(V.tensor_tensor(STATE[:, 4, :], STATE[:, c, :], b[:, 0:P], ALU.add))
                        for j in range(2):
                            ins = V.tensor_scalar(STATE[:, c + 1, j * 64:(j + 1) * 64], STATE[:, 4, j * 64:(j + 1) * 64],
                                                  EC[:, j, c * 64 + 63:c * 64 + 64], None, ALU.mult)
                        link(ins)
                    free(V.tensor_copy(small(158, 1), b[:, 0:1]))
                    if c < 3:
                        go()
                    yc = YC[:, :, c * 64:(c + 1) * 64]
                    for part in range(2):
                        b = take()[:, 0:P].rearrange("p (a b) -> p a b", a=2)
                        if part:
                            settled_but_last()
                        free(V.tensor_tensor(yc, yc, b, ALU.add) if part else V.tensor_copy(yc, b))
                    settled()
                link(V.tensor_copy(YT, YC))
                go()
                b = take()[:, :].rearrange("p (a b) -> p a b", a=2)
                link(V.scalar_tensor_tensor(YC, b, -1.0 / HD, YT, ALU.mult, ALU.add))
                free(V.tensor_tensor(YS, YC, YC, ALU.mult))
                settled()
                go()
                b = take()[:, :].rearrange("p (a b) -> p a b", a=2)
                free(V.tensor_scalar(YS, b, 1.0 / HD, None, ALU.mult))
                settled()
                mark(rw_var)
                dve.wait_ge(rw_vroot, l + 1)
                link(V.reciprocal(YS, YS))
                link(V.tensor_tensor(YC, YC, YS, ALU.mult))
                for j in range(2):
                    ins = V.tensor_scalar(YC[:, j, :], YC[:, j, :], pr(f"gng_{l}", j, j + 1), pr(f"gnb_{l}", j, j + 1),
                                          ALU.mult, ALU.add)
                link(ins)
                link(V.tensor_tensor(YC, YC, BON, ALU.add))
                link(V.tensor_tensor(CAT2[:, 4:6, :], YC, GV, ALU.mult))
                go()

                assert st["u"] == UB[l]["merge"], (st["u"], UB)
                pairs(KD)
                settled()
                for j in range(KD):
                    ins = V.tensor_scalar(X[:, j, 0:T], X[:, j, 0:T], ALPHA, None, ALU.mult)
                link(ins)
                go()
                for j in range(KD):
                    residual(j, take(), T, None)
                settled()
                go()
                norm(5 + 2 * l, T, X, X)
                dve.wait_ge(n_a, 8 * (6 + 2 * l))
                if l == 1:
                    for t in range(2):
                        free(V.tensor_tensor(LG[:, 8 * t:8 * t + 8], take()[:, 0:8], pr("router_b"), ALU.add))
                    settled()
                    for t in range(2):
                        lg, m8 = LG[:, 8 * t:8 * t + 8], M8[:, 8 * t:8 * t + 8]
                        link(V.max(m8, lg))
                        link(V.max_index(idx8[:, t, :], m8, lg))
                        V.tensor_copy(IDXF[:, 2 * t:2 * t + 2], idx8[:, t, 0:2])
                        link(V.tensor_tensor(EE[:, t:t + 1], m8[:, 1:2], m8[:, 0:1], ALU.subtract))
                    mark(top_v)
                    dve.wait_ge(top_e, 1)
                    link(V.tensor_scalar(EE[:, 2:4], EE[:, 0:2], 1.0, None, ALU.add))
                    link(V.reciprocal(EE[:, 4:6], EE[:, 2:4]))
                    link(V.tensor_tensor(EE[:, 6:8], EE[:, 4:6], EE[:, 0:2], ALU.mult))
                    for t in range(2):
                        V.tensor_scalar(OH[:, 0, :], cn("iota8"), IDXF[:, 2 * t:2 * t + 1], EE[:, 4 + t:5 + t],
                                        ALU.is_equal, ALU.mult)
                        link(V.tensor_scalar(OH[:, 1, :], cn("iota8"), IDXF[:, 2 * t + 1:2 * t + 2], EE[:, 6 + t:7 + t],
                                             ALU.is_equal, ALU.mult))
                        link(V.tensor_tensor(CWT[:, t, :], OH[:, 0, :], OH[:, 1, :], ALU.add))
                    go()
                    copy_units([CWR[0:8, :]])
                    settled()
                    go()
                    copy_units([CW[:, e, :] for e in range(EXPERTS)])
                    settled()
                    go()
                for j in range(KD):
                    dve.wait_ge(a_hi, 1 + KD * l + j + 1)
                    link(V.tensor_tensor(AL[:, j, 0:T], X[:, j, 0:T], AH[:, j, 0:T].bitcast(F32), ALU.subtract))
                for j in range(KD):
                    ins = V.tensor_scalar(X[:, j, 0:T], X[:, j, 0:T], ALPHA, None, ALU.mult)
                link(ins)
                go()
                assert st["u"] == UB[l]["ffn"], (st["u"], UB)
                if l == 1:
                    assert st["tmp"] == UB["tmp_experts"], (st, UB)
                ffn(4 + 2 * l, 2 if l == 0 else EXPERTS, T, None, experts=l == 1)
                settled()
                norm(6 + 2 * l, T, X, X)
                if l == 0:
                    dve.wait_ge(n_a, 8 * 7)


def _unit_bases():
    u = 20 + 8 + 4 + 4 + KD + 2 * UNITS_FFN
    u += 10 + 4 + 10 + 4 + KD + 2 * UNITS_FFN
    out = {}
    for l in range(2):
        u += 23 + 6 + 4
        out[l] = {"index": u}
        u += 8 + 2 * FILLED
        u += 6 + 2 + 4 + 8 + 2 + 5 * 6 + 3 + 20 + 2
        out[l]["merge"] = u
        u += 2 * KD + KD
        if l:
            u += 2 + 1 + EXPERTS
        out[l]["ffn"] = u
        u += (2 if l == 0 else EXPERTS) * UNITS_FFN
    out["tmp_experts"] = 2 * FH * 3 + 2 * 4 * KD
    return out


def gate_chunks(q, ada):
    return 2 * 2 * q + 2 + (KD // 2 * sum(len(x) for x in ADA_HALVES[:q]) if ada else 0)


def part_chunks(ada):
    return gate_chunks(FH, ada) - 2 + FH * KD // CHUNK


UB = _unit_bases()
PART_CHUNKS = part_chunks(False)
FFN_START = stream_plan()[1]


def kernel(**inputs):
    import concourse.bacc as bacc
    from concourse.bass_utils import run_bass_kernel_spmd as run

    a = {k: np.asarray(v) for k, v in inputs.items()}
    plan, _ = stream_plan()
    chunks = len(plan) // CHUNK
    stream = np.zeros((chunks, P, CHUNK * P), np.float32)
    for n, blk in enumerate(plan):
        if blk is None:
            continue
        name, idx, row, col, width = blk
        w = a[name][idx]
        dst = stream[n // CHUNK, :, (n % CHUNK) * P:(n % CHUNK + 1) * P]
        if isinstance(col, tuple):
            ws = width if isinstance(width, tuple) else (width,) * len(col)
            at = 0
            for c, k in zip(col, ws):
                dst[:, at:at + k] = w[row:row + P, c:c + k]
                at += k
        else:
            dst[:, 0:width] = w[row:row + P, col:col + width]

    par = np.zeros((P, NPAR), np.float32)

    def put(name, v):
        lo, hi = PO[name]
        par[:, lo:hi] = v

    def cols(v):
        return v.reshape(-1, P).T

    put("eps6", 1e-6)
    put("eps5", 1e-5)
    put("epsgn", 64e-5)
    cv = np.stack([cols(a["c"][0]), cols(a["c_ctx"])], -1)
    put("cvec", cv.reshape(P, -1))
    for l in range(2):
        put(f"ada_b{l}", cols(a["ada_b"][l]))
        put(f"n1g{l}", cols(a["norm1_g"][l]))
        put(f"n2g{l}", cols(a["norm2_g"][l]))
    put("final_g", cols(a["final_g"]))
    put("sgu_b", a["sgu_b"][0].reshape(1, -1))
    put("lqk", np.concatenate([a[n][0] for n in ("diff_lq1", "diff_lk1", "diff_lq2", "diff_lk2")])[None])
    put("subln", cols(a["diff_subln_g"][0]))
    put("odd_sink", a["odd_sink"][0][None])
    put("sgu_w", a["sgu_w"][0].transpose(2, 0, 1).reshape(P, -1))
    put("router_w", a["router_w_2"][0].reshape(KD, P, 8).transpose(1, 0, 2).reshape(P, -1))
    put("router_b", a["router_b_2"][0][None])
    for l in range(2):
        put(f"sinks_{l}", a["swa_sinks_2"][l][None])
        for n, k in (("mu", "rwkv_mu_2"), ("w0", "rwkv_w0_2"), ("a0", "rwkv_a0_2"), ("kk", "rwkv_k_k_2"),
                     ("ka", "rwkv_k_a_2"), ("rk", "rwkv_r_k_2"), ("gng", "rwkv_gn_g_2"), ("gnb", "rwkv_gn_b_2"),
                     ("gate_b", "gate_bias_2")):
            put(f"{n}_{l}", cols(a[k][l]))
        for i in range(2):
            put(f"ln{i + 1}g_{l}", cols(a["ln_g_2"][l, i]))
            put(f"ln{i + 1}b_{l}", cols(a["ln_b_2"][l, i]))
        lo, hi = PO[f"fbias_{l}"]
        par[0:4, lo:hi] = a["fox_f_bias_2"][l][:, None]
        put(f"wa_up_{l}", np.concatenate([a["rwkv_w_up_2"][l], a["rwkv_a_up_2"][l]], 0))
        put(f"g_up_{l}", a["rwkv_g_up_2"][l])

    xin = np.concatenate([a["x"][0], a["ctx"][0]], 0).T.reshape(KD, P, TT).transpose(1, 0, 2)
    arrays = {"stream": stream, "params": par, "consts": constants(), "xin": np.ascontiguousarray(xin)}
    nc = bacc.Bacc("TRN2", target_bir_lowering=False, num_devices=1)
    aps = [nc.dram_tensor(k, v.shape, F32, kind="ExternalInput").ap() for k, v in arrays.items()]
    out = nc.dram_tensor("out", (P, KD, T), F32, kind="ExternalOutput").ap()
    build(nc, *aps, out)
    r = run(nc, [arrays], core_ids=[0])
    y = r.results[0]["out"]
    return np.ascontiguousarray(y.transpose(2, 1, 0).reshape(1, T, D))
```

```python
from contextlib import ExitStack

import numpy as np

import concourse.bass as bass
from concourse import mybir

F32 = mybir.dt.float32
F32R = mybir.dt.float32r
U32 = mybir.dt.uint32
ALU = mybir.AluOpType
ACT = mybir.ActivationFunctionType
AX_X = mybir.AxisListType.X

P = 128
D = 1024
KD = D // P
T = 256
TC = 256
TT = T + TC
HD = 64
SCALE = HD ** -0.5
FH = 11
HID = 2 * FH * P
EXPERTS = 8
CHUNK = 4
RING = 11
SPLIT = 6
AHEAD = 4
BANKS = 6
NEG = -1e30
OUT_OF_LIST = -3e38
LAM_INIT = 0.8 - 0.6
BR_K = (4, 2, 2, 2)
UNITS_FFN = 2 * FH + KD
ALPHA = 4.0 ** 0.25
SCR = 23040

C_SWA, C_RWKV, C_FOX, C_DSA, C_GATE = 0, 768, 1792, 2564, 3272

PARAM_COLS = [
    ("eps6", 1), ("eps5", 1), ("epsgn", 1), ("cvec", 2 * KD),
    ("ada_b0", 48), ("ada_b1", 48), ("n1g0", KD), ("n1g1", KD), ("n2g0", KD), ("n2g1", KD), ("final_g", KD),
    ("sgu_b", 512), ("lqk", 256), ("subln", 1), ("odd_sink", 16), ("sgu_w", 512), ("router_w", 64), ("router_b", 8),
]
for _l in range(2):
    PARAM_COLS += [(f"{n}_{_l}", w) for n, w in (
        ("sinks", 8), ("mu", 8), ("w0", 2), ("a0", 2), ("kk", 2), ("ka", 2), ("rk", 2), ("gng", 2), ("gnb", 2),
        ("fbias", 1), ("gate_b", 32), ("ln1g", 8), ("ln1b", 8), ("ln2g", 8), ("ln2b", 8), ("wa_up", 256), ("g_up", 256))]

CONST_COLS = [
    ("ident", 128), ("mean_d", 128), ("mean_e", 128), ("blk64", 128), ("rot", 128), ("dup0", 128), ("dup1", 128),
    ("cos", 256), ("sin", 256), ("band", 1024), ("swa", 512), ("causal", 512), ("chunks", 512), ("sel8", 1024),
    ("pairmask", 512), ("inv0", 128), ("inv0t", 128), ("levels", 640), ("segs", 256), ("iota8", 8),
]


def offsets(cols):
    at, out = 0, {}
    for name, width in cols:
        out[name] = (at, at + width)
        at += width
    return out, at


PO, NPAR = offsets(PARAM_COLS)
CO, NCON = offsets(CONST_COLS)
FIRST_PAR, FIRST_CON = PO["final_g"][0], CO["mean_e"][0]


def constants():
    c = np.zeros((P, NCON), np.float32)

    def put(name, value):
        a, b = CO[name]
        c[:value.shape[0], a:b] = value.reshape(value.shape[0], -1)

    i, j = np.arange(P)[:, None], np.arange(P)[None, :]
    put("ident", (i == j).astype(np.float32))
    put("mean_d", np.full((P, P), 1.0 / D, np.float32))
    put("mean_e", np.full((P, P), 1.0 / P, np.float32))
    put("blk64", (i // 64 == j // 64).astype(np.float32))
    half = j % 32 < 16
    put("rot", np.where(half & (i == j + 16), -1.0, np.where(~half & (i == j - 16), 1.0, 0.0)).astype(np.float32))
    put("dup0", ((i < 64) & (j % 64 == i)).astype(np.float32))
    put("dup1", ((i >= 64) & (j % 64 == i - 64)).astype(np.float32))
    t = np.arange(T)
    nf = HD // 4
    inv = np.float32(10000.0) ** (-np.arange(nf, dtype=np.float32) / np.float32(nf))
    ang = np.stack([(t // 64).astype(np.float32)[:, None] * inv, (t % 64).astype(np.float32)[:, None] * inv], 1)
    ang = np.broadcast_to(ang[:, :, None, :], (T, 2, 2, nf)).reshape(T, HD).T
    put("cos", np.tile(np.cos(ang), (2, 1)).astype(np.float32))
    put("sin", np.tile(np.sin(ang), (2, 1)).astype(np.float32))

    def mask(allowed, extra=0):
        m = np.zeros((P, 2, T + extra), np.float32)
        for q in range(2):
            m[:, q, :T] = np.where(allowed(q * P + i, np.arange(T)[None, :]), 0.0, NEG)
        return m

    put("band", mask(lambda q, k: np.abs(q - k) <= 128, TC))
    put("swa", mask(lambda q, k: (k // 64 <= q // 64) & (k // 64 >= q // 64 - 2)))
    put("causal", mask(lambda q, k: k <= q))
    put("chunks", mask(lambda q, k: k // 64 <= q // 64))
    put("sel8", np.broadcast_to((np.arange(8)[:, None] == np.arange(8)[None, :])[:, :, None], (8, 8, P)).astype(np.float32))
    same = i // 64 == j // 64
    strict, incl = (same & (i < j)), (same & (i <= j))
    put("pairmask", np.stack([strict, incl, strict, incl], 1).astype(np.float32))
    low = (i // 2 == j // 2) & (i > j)
    put("inv0", -low.astype(np.float32))
    put("inv0t", -low.T.astype(np.float32))
    lev = [((i // (2 * s) == j // (2 * s)) & (i // s < j // s)) for s in (2, 4, 8, 16, 32)]
    put("levels", np.stack(lev, 1).astype(np.float32))
    put("segs", np.broadcast_to((t % 64 != 0).astype(np.float32), (P, T)))
    put("iota8", np.broadcast_to(np.arange(8, dtype=np.float32), (P, 8)))
    return c


ADA_HALVES = [[0, 1]] + [[f + 1] for f in range(1, FH)]


PAIRS = [(i, j) for i in (0, 2, 3, 1) for j in range(KD)]
FILL_INDEX = (2, 3)
FILL_START, FILL_LOW, FILL_NORM, FILL_MATRIX, FILL_LEVEL = 2, 2, 2, 3, 1
FILLED = sum(FILL_INDEX) + FILL_START + FILL_LOW + FILL_NORM + FILL_MATRIX + 10 * FILL_LEVEL
assert FILLED == 3 * KD

def stream_plan():
    blocks, starts, projections = [], [], []

    def pad():
        while len(blocks) % CHUNK:
            blocks.append(None)

    def tiles(name, idx, cols, k=KD, row=0, width=P):
        for c in cols:
            for kk in range(k):
                blocks.append((name, idx, row + kk * P, c, width))

    def wide(name, idx, col, n):
        for kk in range(KD):
            for c in range(n):
                blocks.append((name, idx, kk * P, col + c * P, P))

    def ada_rows(layer, group, k0, n):
        for kk in range(k0, k0 + n):
            for c in range(CHUNK):
                blocks.append(("ada_w", (layer,), kk * P, (CHUNK * group + c) * P, P))

    def ffn(w_up, w_gate_col, w_val, w_val_idx, w_val_col, w_down, idx, didx, row, ada=None):
        pad()
        starts.append(len(blocks) // CHUNK)
        for f in range(FH):
            tiles(w_up, idx, [w_gate_col + f * P])
            tiles(w_val, w_val_idx, [w_val_col + f * P])
            if ada is not None:
                for h in ADA_HALVES[f]:
                    ada_rows(1, 6 * ada + h // 2, h % 2 * (KD // 2), KD // 2)
        for j in range(KD):
            tiles(w_down, didx, [j * P], FH, row)

    for g in range(4):
        ada_rows(0, g, 0, KD)
    projections.append(len(blocks) // CHUNK)
    tiles("even_w_in", (0,), [j * P for j in (*range(8, 16), *range(4))])
    wide("even_w_in", (0,), 512, 4)
    wide("even_w_in", (0,), 2048, 4)
    for g in range(4, 12):
        ada_rows(0, g, 0, KD)
    projections.append(len(blocks) // CHUNK)
    tiles("even_w_out", (0,), [j * P for j in range(KD)])
    for half in range(2):
        ffn("ffn_w_in", half * FH * P, "ffn_w_in", (0,), HID + half * FH * P, "ffn_w_out", (0,), (0,), half * FH * P, half)
    projections.append(len(blocks) // CHUNK)
    tiles("odd_w_qkv", (0,), [j * P for j in (8, 9, *range(8))])
    wide("odd_w_qkv", (0,), 1280, 2)
    projections.append(len(blocks) // CHUNK)
    tiles("odd_w_out", (0,), [j * P for j in range(KD)])
    for half in range(2):
        ffn("ffn_w_in", half * FH * P, "ffn_w_in", (1,), HID + half * FH * P, "ffn_w_out", (1,), (1,), half * FH * P)
    for l in range(2):
        w = "w_in_2"
        projections.append(len(blocks) // CHUNK)
        tiles(w, (l,), [C_SWA + j * P for j in range(5)] + [C_RWKV + j * P for j in range(8)]
              + [C_FOX + j * P for j in range(4)] + [C_DSA, C_DSA + P, C_DSA + 384, C_DSA + 512])
        for kk in range(KD):
            blocks.append((w, (l,), kk * P, (C_DSA + 256, C_DSA + 640), 64))
        tiles(w, (l,), [C_FOX + 768], width=4)
        tiles(w, (l,), [C_SWA + 640])
        for kk in range(KD):
            blocks.append((w, (l,), kk * P, (C_DSA + 320, C_DSA + 704), (64, 4)))
        wide(w, (l,), C_FOX + 512, 2)
        for i, j in PAIRS:
            tiles(w, (l,), [C_GATE + i * D + j * P])
            tiles("w_branch_2", (l,), [j * P], BR_K[i], sum(BR_K[:i]) * P)
        pad()
        projections.append(len(blocks) // CHUNK)
        tiles("w_out_2", (l,), [j * P for j in range(KD)])
        if l == 0:
            for half in range(2):
                c = half * FH * P
                ffn("ffn_w1_2", c, "ffn_w3_2", (0,), c, "ffn_w2_2", (0,), (0,), c)
        else:
            for e in range(EXPERTS):
                ffn("exp_w1_2", 0, "exp_w3_2", (0, e), 0, "exp_w2_2", (0, e), (0, e), 0)
    while len(blocks) % (CHUNK * RING):
        blocks.append(None)
    return blocks, starts, projections


def build(nc, stream, params, consts, xin, out):
    rounds = stream.shape[0] // RING
    with ExitStack() as ctx:
        def sb(name, *shape, dt=F32):
            return ctx.enter_context(nc.sbuf_tensor(name, [P, *shape], dt))

        def sem(name):
            return ctx.enter_context(nc.semaphore(name))

        ring = sb("ring", RING, CHUNK * P)
        WH, WL = sb("WH", SPLIT, CHUNK * P, dt=F32R), sb("WL", SPLIT, CHUNK * P, dt=F32R)
        X = sb("X", KD, TT)
        par = sb("par", NPAR)
        con = sb("con", NCON)
        smalls = sb("smalls", 160)
        mod = sb("mod", 2, 48, 2)
        modg = sb("modg", 4, KD, 2)
        idx8 = sb("idx8", 2, 8, dt=U32)
        csH, csL = sb("csH", 2 * KD, dt=F32R), sb("csL", 2 * KD, dt=F32R)
        with ExitStack() as feed_forward:
            def ffb(name, *shape, dt=F32):
                return feed_forward.enter_context(nc.sbuf_tensor(name, [P, *shape], dt))

            AH, AL = ffb("AH", KD, TT, dt=F32R), ffb("AL", KD, TT, dt=F32R)
            HH, HL = ffb("HH", FH, TT, dt=F32R), ffb("HL", FH, TT, dt=F32R)
            SQF, RSF = ffb("SQF", KD, TT), ffb("RSF", TT)
            TMP = ffb("TMP", 2, TT)
            ROWF = ffb("ROWF", CHUNK * P)
        with ExitStack() as projecting:
            PH = projecting.enter_context(nc.sbuf_tensor("PH", [P, KD, TT], F32R))
            projecting.enter_context(nc.sbuf_tensor("gap0", [P, 4096], F32))
            CL = projecting.enter_context(nc.sbuf_tensor("CL", [P, KD, TT], F32R))
            projecting.enter_context(nc.sbuf_tensor("gap1", [P, 2048], F32))
            PL = projecting.enter_context(nc.sbuf_tensor("PL", [P, KD, TT], F32R))
        A = sb("A", KD, TT)
        S = sb("S", SCR)

        bank = [ctx.enter_context(nc.psum_tensor(f"bank{i}", [P, 512], F32)) for i in range(8)]
        NORM, ADA = bank[6], bank[7]
        ROWS = bank[6]

        def DIFF(n):
            return bank[7][:, 96:96 + T] if n < 6 else bank[n - 6][:, 0:T]

        MEAN = bank[7]

        def pr(name, a=0, b=None):
            lo, hi = PO[name]
            return par[:, lo + a:(hi if b is None else lo + b)]

        def cn(name, a=0, b=None):
            lo, hi = CO[name]
            return con[:, lo + a:(hi if b is None else lo + b)]

        def view(at, *shape):
            n = int(np.prod(shape))
            assert at + n <= SCR
            v = S[:, at:at + n]
            if len(shape) == 2:
                v = v.rearrange("p (a b) -> p a b", a=shape[0])
            if len(shape) == 3:
                v = v.rearrange("p (a b c) -> p a b c", a=shape[0], b=shape[1])
            return v

        def small(at, n):
            return smalls[:, at:at + n]

        def over(ap, n):
            return ap.unsqueeze(1).broadcast_to([P, n, ap.shape[1]])

        ident, sel8 = cn("ident"), cn("sel8").rearrange("p (e c) -> p e c", e=8)

        SQM = view(18432 - 4096, KD, TT)
        CW = X[:, :, T:TT]
        RSM = view(18432, TT)

        def SQN(ni):
            return SQF if ni % 2 and ni < 8 else SQM

        def RSN(ni):
            return RSF if ni % 2 and ni < 8 else RSM

        AT = 18432
        SM = view(AT, 2, 512)
        E = view(AT + 1024, 4, 512)
        ET = view(AT + 3072, 2, 512)
        mx, nm, sm, es, rc, r2 = (small(4 * n, 4) for n in range(6))
        nsink = small(24, 32)
        lam = small(60, 8)
        cs = small(70, 16)
        Q0, K0, U0, VG, VV = (view(2048 * n, 4, TT) for n in range(5))
        CAT0 = view(10240, KD, TT)
        VT = view(14336, 4, TT)
        ST6 = view(AT, 16, 6)
        MV2 = view(AT + 96, 16, 2)
        VRS = view(AT + 128, 16)
        RT1 = view(AT + 1024, 2, T)
        ROWM = view(AT + 4096, CHUNK * P)
        Q1, K1, KD1, V1 = view(0, KD, T), view(2048, 2, TT), view(3072, 4, TT), view(5120, 4, T)
        CAT1 = view(10240, KD, T)

        def kq_tile(j):
            return K1[:, j, :] if j < 2 else Q1[:, j - 2, :]

        SQ_, SK, SKD = view(0, 4, T), view(1024, 1, T), view(1280, 2, T)
        FQ, FK, DQ, DQI = view(1792, 2, T), view(2304, 2, T), view(2816, 2, T), view(3328, 2, T)
        DKI, DKD, DKID, FC = view(3840, 1, T), view(4096, 1, T), view(4352, 1, T), view(4608, 4, T)
        SV, FV, DV = view(5632, 2, P), view(5888, 2, T), view(6400, 2, 68)
        RP = view(6656, KD, T)
        DSC, DWK, DMK, DT = view(8704, T), view(8960, T), view(9216, 2, T), view(9728, T)
        CAT2 = A[:, :, :].rearrange("p a b -> p (a b)")[:, 0:2560].rearrange("p (a b) -> p a b", a=10)
        W0 = 8704
        (SHD, LWV, AV, GV, CC, CX, KK, EC, EN, EX) = (view(W0 + 512 * n, 2, T) for n in range(10))
        DELTA = view(W0, KD, T)
        KNORM, RKK, BON = CX, SHD, view(W0 + 5120, 2, T)
        KR = view(W0 + 5632, 2, 2, T)
        BH, KH = view(W0 + 6656, 2, T), view(W0 + 7168, 2, T)
        LOW = view(W0 + 7680, 2, T)
        TOK = [view(W0 + 8192 + 512 * n, 2, T) for n in range(4)]
        MM = view(W0 + 10240, 8, 512)
        XX = view(0, 8, 256)
        LK = view(2048, 8, P)
        PP = view(3072, 8, P)
        MVS, U0N, GTN = view(4096, 8, 64), view(4608, 8, 64), view(5120, 4, P)
        SA = view(5632, 4, 64)
        STATE = view(5888, 5, P)
        YT = view(W0 + 5632, 2, T)
        YC, YS = view(W0 + 6656, 2, T), view(W0 + 7168, 2, T)
        ACC = X[:, :, T:TT]
        GP = A[:, :, :].rearrange("p a b -> p (a b)")[:, 2560:3584].rearrange("p (a b) -> p a b", a=4)
        GATE, PROD = GP[:, 0:2, :], GP[:, 2:4, :]
        LG, M8, EE = small(90, 16), small(106, 16), small(122, 8)
        IDXF, CWT = small(130, 4), view(W0, 2, 8)
        CWR, OH = view(W0 + 64, T), view(W0 + 320, 2, 8)

        w_loaded = [sem(f"w_loaded{i}") for i in range(RING)]
        w_taken = sem("w_taken")
        cond_in, first_in, x_in, tables_in = sem("cond_in"), sem("first_in"), sem("x_in"), sem("tables_in")
        a_lo = sem("a_lo")
        gemm_done, gemm_free = sem("gemm_done"), sem("gemm_free")
        w_hi, split_begun = sem("w_hi"), sem("split_begun")
        h_hi, h_lo = sem("h_hi"), sem("h_lo")
        a_hi = sem("a_hi")
        act_tmp, cw_done = sem("act_tmp"), sem("cw_done")
        silu_c = sem("silu_c")
        ada_row, ada_copied = sem("ada_row"), sem("ada_copied")
        ada_done, mod_ready = sem("ada_done"), sem("mod_ready")
        n_sq, n_mm, n_root, n_x, n_a = sem("norm_sq"), sem("norm_mm"), sem("norm_root"), sem("norm_x"), sem("norm_a")
        n_mean, n_c = sem("norm_mean"), sem("norm_centred")
        dve_chain, act_chain = sem("dve_chain"), sem("act_chain")
        at_s, at_m, at_e, at_n = sem("att_scores"), sem("att_max"), sem("att_exp"), sem("att_normed")
        at_t, at_tv, at_o, at_out = sem("att_turned"), sem("att_turned_copy"), sem("att_pv"), sem("att_out")
        lam_sum, lam_exp = sem("lam_sum"), sem("lam_exp")
        gelu_v, v_var, v_root, v_normed = sem("gelu_v"), sem("v_var"), sem("v_root"), sem("v_normed")
        ready = sem("ready")
        diff_sq, diff_mean, diff_root = sem("diff_sq"), sem("diff_mean"), sem("diff_root")
        diff_normed = sem("diff_normed")
        fox_pre, fox_e, fox_ln = sem("fox_pre"), sem("fox_exp"), sem("fox_log")
        rw_shift, rw_low, rw_pre, rw_sig = sem("rw_shift"), sem("rw_low"), sem("rw_pre"), sem("rw_sig")
        rw_c, rw_exp, rw_ks, rw_kroot = sem("rw_c"), sem("rw_exp"), sem("rw_ks"), sem("rw_kroot")
        rw_var, rw_vroot = sem("rw_var"), sem("rw_vroot")
        top_v, top_e = sem("top_v"), sem("top_e")
        out_done = sem("out_done")

        def keys(kap, n0, n1):
            return lambda base, h: kap(h)[base:base + HD, n0:n1]

        def unit(q, k, nk, mask, sink, vals, dst, last=True, bias=None):
            return dict(q=q, k=k, nk=nk, mask=mask, sink=sink, vals=vals, dst=dst, last=last, bias=bias)

        def units_even():
            us = []
            for h in range(4):
                for half in range(2):
                    k0 = half * T
                    for qt in range(2):
                        q0 = half * T + qt * P
                        for s in range(2):
                            b = s * HD
                            us.append(unit(Q0[b:b + HD, h, q0:q0 + P], K0[b:b + HD, h, k0:TT], TT - k0, None, None,
                                           [VV[:, t, h * P:(h + 1) * P] for t in range(2 * half, 4)],
                                           CAT0[:, 4 + h, q0:q0 + P], last=s == 1))
            return us

        def units_odd():
            us = []
            for h in range(16):
                b, kv = (h % 2) * HD, h // 4
                for qt in range(2):
                    us.append(unit(Q1[b:b + HD, h // 2, qt * P:(qt + 1) * P], KD1[b:b + HD, kv, :], TT,
                                   cn("band", qt * TT, (qt + 1) * TT), h,
                                   [V1[:, t, kv * HD:(kv + 1) * HD] for t in range(4)],
                                   CAT1[b:b + HD, h // 2, qt * P:(qt + 1) * P]))
            return us

        def units_second(l):
            us = []
            for h in range(8):
                b, kv = (h % 2) * HD, h // 4
                for qt in range(2):
                    nk = (qt + 1) * P
                    us.append(unit(SQ_[b:b + HD, h // 2, qt * P:nk], SKD[b:b + HD, kv, 0:nk], nk,
                                   cn("swa", qt * T, qt * T + nk), h,
                                   [SV[:, t, kv * HD:(kv + 1) * HD] for t in range(qt + 1)],
                                   CAT2[b:b + HD, h // 2, qt * P:nk]))
            for h in range(4):
                b = (h % 2) * HD
                for qt in range(2):
                    nk = (qt + 1) * P
                    us.append(unit(FQ[b:b + HD, h // 2, qt * P:nk], FK[b:b + HD, h // 2, 0:nk], nk,
                                   cn("causal", qt * T, qt * T + nk), None,
                                   [FV[:, t, h * HD:(h + 1) * HD] for t in range(qt + 1)],
                                   CAT2[b:b + HD, 6 + h // 2, qt * P:nk], bias=(h, qt)))
            for h in range(4):
                b = (h % 2) * HD
                for qt in range(2):
                    nk = (qt + 1) * P
                    us.append(unit(DQ[b:b + HD, h // 2, qt * P:nk], DKD[b:b + HD, 0, 0:nk], nk,
                                   DMK[:, qt, 0:nk], None, [DV[:, t, 0:HD] for t in range(qt + 1)],
                                   CAT2[b:b + HD, 8 + h // 2, qt * P:nk]))
            return us

        def groups(us):
            g, out_ = 0, []
            for u in us:
                out_.append(g)
                g += u["last"]
            return out_, g

        def head_cols(m):
            h = 2 * (m % 2) + m // 4
            return slice(h * 64, (h + 1) * 64)

        block = ctx.enter_context(nc.Block())

        @block.sync
        def _(sp):
            first_par, first_con = slice(0, FIRST_PAR), slice(0, FIRST_CON)
            sp.dma_start(par[:, first_par], params[:, first_par]).then_inc(cond_in, 16)
            for s in range(RING):
                sp.dma_start(ring[:, s, :], stream[s]).then_inc(w_loaded[s], 16)
                if s == 0:
                    sp.dma_start(con[:, first_con], consts[:, first_con]).then_inc(first_in, 16)
                if s == 7:
                    sp.dma_start(X[:, :, :], xin).then_inc(x_in, 16)
            for n in range(RING, 3 * RING):
                sp.wait_ge(w_taken, n - RING + 2)
                sp.dma_start(ring[:, n % RING, :], stream[n]).then_inc(w_loaded[n % RING], 16)
            sp.dma_start(par[:, FIRST_PAR:], params[:, FIRST_PAR:]).then_inc(tables_in, 16)
            sp.dma_start(con[:, FIRST_CON:], consts[:, FIRST_CON:]).then_inc(tables_in, 16)
            with sp.Fori(3, rounds) as r:
                for s in range(RING):
                    sp.wait_ge(w_taken, r * RING + (s - RING + 2))
                    sp.dma_start(ring[:, s, :], stream[r * RING + s]).then_inc(w_loaded[s], 16)
            sp.wait_ge(n_a, 8 * 9)
            sp.dma_start(out, X[:, :, 0:T]).then_inc(out_done, 16)
            sp.wait_ge(out_done, 16)

        @block.tensor
        def _(pe):
            st = dict(n=0, u=0, a=0, g=0, s=0, h=0, ada=0, p=0, alo=0, free=False, i=None, ready=0)

            def val(x, per):
                return x if st["i"] is None else st["i"] * per + x

            def weight(n, signal=True):
                slot, c = (n // CHUNK) % RING, n % CHUNK
                if c == 0:
                    pe.wait_ge(w_loaded[slot], 16 * (n // CHUNK // RING + 1))
                    st["free"] = st["free"] or signal
                return ring[:, slot, c * P:(c + 1) * P]

            def mm(o, l, r, start, stop, end=False, sig=True):
                ins = pe.matmul(o, l, r, start=start, stop=stop)
                if end:
                    ins.then_inc(gemm_done, 1)
                elif st["free"] and sig:
                    ins.then_inc(w_taken, 1)
                    st["free"] = False
                return ins

            def unit_begin():
                u = st["u"]
                if u >= BANKS:
                    pe.wait_ge(gemm_free, val(u - BANKS + 1, UNITS_FFN))
                st["u"] += 1
                return bank[u % BANKS]

            def tile(rhs, k, tt, m=P):
                b = unit_begin()
                for kk in range(k):
                    w = weight(st["n"])
                    mm(b[0:m, 0:tt], w[:, 0:m], rhs(kk), kk == 0, kk == k - 1, kk == k - 1)
                    st["n"] += 1

            def split_tile(o, hi, lo, k, fresh=False):
                for kk in range(k):
                    if fresh:
                        pe.wait_ge(a_lo, st["alo"] + kk + 1)
                    n, s = st["n"], st["s"]
                    c = slice(n % CHUNK * P, (n % CHUNK + 1) * P)
                    first = n % CHUNK == 0
                    if first:
                        pe.wait_ge(w_taken, val(n // CHUNK + 1, PART_CHUNKS))
                    wh, wl = (W[:, s % SPLIT, c][:, 0:o.shape[0]] for W in (WH, WL))
                    ins = pe.matmul(o, wh, hi(kk), start=kk == 0, stop=False)
                    if first:
                        ins.then_inc(split_begun, 1)
                    pe.matmul(o, wh, lo(kk), start=False, stop=False)
                    ins = pe.matmul(o, wl, hi(kk), start=False, stop=kk == k - 1)
                    st["n"] += 1
                    st["s"] += n % CHUNK == CHUNK - 1
                ins.then_inc(gemm_done, 1)

            def projection(tt, m=P, fresh=False):
                split_tile(unit_begin()[0:m, 0:tt], lambda kk: PH[:, kk, 0:tt], lambda kk: PL[:, kk, 0:tt], KD, fresh)
                if fresh:
                    st["alo"] += KD

            def out_projection(high):
                for j in range(KD):
                    split_tile(unit_begin()[:, 0:T], lambda kk: high[:, kk, 0:T], lambda kk: CL[:, kk, 0:T], KD, j == 0)
                st["alo"] += KD

            def split_tok_tiles(tiles, n):
                units = [unit_begin()[:, 0:n * P] for _ in range(tiles)]
                for kk in range(KD):
                    at, s = st["n"] % CHUNK * P, st["s"]
                    first = at == 0
                    if first:
                        pe.wait_ge(w_taken, st["n"] // CHUNK + 1)
                    wh, wl = (W[:, s % SPLIT, at:at + n * P] for W in (WH, WL))
                    for t, o in enumerate(units):
                        tok = slice(t * P, (t + 1) * P)
                        ins = pe.matmul(o, PH[:, kk, tok], wh, start=kk == 0, stop=False)
                        if first and t == 0:
                            ins.then_inc(split_begun, 1)
                        pe.matmul(o, PL[:, kk, tok], wh, start=False, stop=False)
                        ins = pe.matmul(o, PH[:, kk, tok], wl, start=False, stop=kk == KD - 1)
                        if kk == KD - 1:
                            ins.then_inc(gemm_done, 1)
                    st["n"] += n
                    st["s"] += st["n"] % CHUNK == 0

            def skip_to_chunk():
                st["n"] += -st["n"] % CHUNK

            def ada_rows(k0, n):
                for kk in range(k0, k0 + n):
                    weight(st["n"])
                    w = ring[:, (st["n"] // CHUNK) % RING, :]
                    ins = pe.matmul(ROWS[0:2, :], cs[:, 2 * kk:2 * kk + 2], w, start=kk == 0, stop=kk == KD - 1)
                    if kk < KD - 1:
                        ins.then_inc(w_taken, 1)
                        st["free"] = False
                    else:
                        ins.then_inc(ada_row, 1)
                    st["n"] += CHUNK

            def split_rows(k0, n):
                for kk in range(k0, k0 + n):
                    pe.wait_ge(w_taken, st["n"] // CHUNK + 1)
                    wh, wl = WH[:, st["s"] % SPLIT, :], WL[:, st["s"] % SPLIT, :]
                    ch, cl = csH[:, 2 * kk:2 * kk + 2], csL[:, 2 * kk:2 * kk + 2]
                    pe.matmul(ROWS[0:2, :], ch, wh, start=kk == 0, stop=False).then_inc(split_begun, 1)
                    pe.matmul(ROWS[0:2, :], cl, wh, start=False, stop=False)
                    ins = pe.matmul(ROWS[0:2, :], ch, wl, start=False, stop=kk == KD - 1)
                    if kk == KD - 1:
                        ins.then_inc(ada_row, 1)
                    st["n"] += CHUNK
                    st["s"] += 1

            def ada_turn(row, done=False):
                g = st["ada"]
                pe.wait_ge(ada_copied, g + 1)
                for c in range(CHUNK):
                    col = 2 * (CHUNK * (g % 12) + c)
                    ins = pe.transpose(ADA[:, col:col + 2], row[0:2, c * P:(c + 1) * P], ident[0:2, 0:2])
                    if c == 0 and st["free"]:
                        ins.then_inc(w_taken, 1)
                        st["free"] = False
                if done:
                    ins.then_inc(ada_done, 1)
                st["ada"] += 1

            def small_unit(pairs, tt, m=P):
                b = unit_begin()
                for j, (o, l, r, s, e) in enumerate(pairs(b)):
                    mm(o, l, r, s, e, j == len(pairs(b)) - 1)

            def dup_unit(lhs, rhs, tt):
                b = unit_begin()
                mm(b[:, 0:tt], lhs, rhs, True, True, True)

            def norm(ni, tt, layer_norm=False):
                SQ = SQN(ni)
                if layer_norm:
                    pe.wait_ge(gemm_free, st["u"])
                    for j in range(KD):
                        ins = pe.matmul(MEAN[:, 0:tt], cn("mean_d"), X[:, j, 0:tt], start=j == 0, stop=j == KD - 1)
                    ins.then_inc(n_mean, 1)
                for j in range(KD):
                    pe.wait_ge(n_sq, KD * ni + j + 1)
                    ins = pe.matmul(NORM[:, 0:tt], cn("mean_d"), SQ[:, j, 0:tt], start=j == 0, stop=j == KD - 1)
                ins.then_inc(n_mm, 1)

            def attention(us, extra=None):
                gs, ng = groups(us)
                a0, g0 = st["a"], st["g"]
                for s in range(len(us) + 3):
                    if s < len(us):
                        u = us[s]
                        if s >= 2:
                            pe.wait_ge(at_e, a0 + s - 1)
                        b = bank[s % 2]
                        ins = pe.matmul(b[:, 0:u["nk"]], u["q"], u["k"], start=True, stop=u["bias"] is None)
                        if u["bias"] is not None:
                            h, qt = u["bias"]
                            pe.matmul(b[:, 0:u["nk"]], sel8[0:4, h, :], FC[0:4, 1, 0:u["nk"]], start=False, stop=False)
                            for kt in range(qt + 1):
                                ins = pe.matmul(b[:, kt * P:(kt + 1) * P], FC[0:4, 0, qt * P:(qt + 1) * P],
                                                sel8[0:4, h, :], start=False, stop=kt == qt)
                        ins.then_inc(at_s, 1)
                    if extra is not None and s < len(us):
                        extra(s)
                    if 2 <= s < len(us) + 2 and us[s - 2]["last"]:
                        u, g = us[s - 2], gs[s - 2]
                        pe.wait_ge(at_n, a0 + s - 1)
                        if g >= 2:
                            pe.wait_ge(at_tv, g0 + g - 1)
                        for kt in range(u["nk"] // P):
                            ins = pe.transpose(bank[2 + g % 2][:, kt * P:(kt + 1) * P],
                                               E[:, (a0 + s - 2) % 4, kt * P:(kt + 1) * P], ident)
                        ins.then_inc(at_t, 1)
                    if s >= 3 and us[s - 3]["last"]:
                        u, g = us[s - 3], gs[s - 3]
                        pe.wait_ge(at_tv, g0 + g + 1)
                        if g >= 2:
                            pe.wait_ge(at_out, g0 + g - 1)
                        b, m = u["dst"].base_partition(), u["dst"].shape[0]
                        for kt, v in enumerate(u["vals"]):
                            ins = pe.matmul(bank[4 + g % 2][b:b + m, 0:P], v, ET[:, g % 2, kt * P:(kt + 1) * P],
                                            start=kt == 0, stop=kt == len(u["vals"]) - 1)
                        ins.then_inc(at_o, 1)
                st["a"] += len(us)
                st["g"] += ng
                pe.wait_ge(at_out, st["g"])

            def ready_wait():
                st["ready"] += 1
                pe.wait_ge(ready, st["ready"])

            def pairs(n):
                for i, j in PAIRS[st["p"]:st["p"] + n]:
                    tile(lambda kk: X[:, kk, 0:T], KD, T)
                    tile(lambda kk: CAT2[:, sum(BR_K[:i]) + kk, :], BR_K[i], T)
                st["p"] += n

            def ffn_part(tt, u0, ada=None):
                for f in range(FH):
                    for half in range(2):
                        split_tile(unit_begin()[:, 0:tt], lambda kk: AH[:, kk, 0:tt], lambda kk: AL[:, kk, 0:tt], KD,
                                   fresh=ada == 0 and f == half == 0)
                    if ada is not None:
                        for h in ADA_HALVES[f]:
                            if h and h % 2 == 0:
                                ada_turn(ROWF)
                            split_rows(h % 2 * (KD // 2), KD // 2)
                for j in range(KD):
                    b = unit_begin()
                    if j == 0:
                        pe.wait_ge(h_lo, val(st["h"] + FH, FH))
                    split_tile(b[:, 0:tt], lambda kk: HH[:, kk, 0:tt], lambda kk: HL[:, kk, 0:tt], FH)
                    if ada is not None and j == 0:
                        ada_turn(ROWF, done=ada == 1)

            def ffn(count, tt):
                skip_to_chunk()
                n0, u0, s0 = st["n"], st["u"], st["s"]
                with pe.Fori(0, count) as i:
                    st["i"] = i
                    ffn_part(tt, u0)
                    assert st["n"] - n0 == PART_CHUNKS * CHUNK
                st["i"] = None
                st["n"], st["u"], st["s"] = n0 + count * PART_CHUNKS * CHUNK, u0 + count * UNITS_FFN, s0 + count * PART_CHUNKS
                st["h"] += count * FH

            pe.wait_ge(silu_c, 1)
            pe.wait_ge(first_in, 16)
            for g in range(4):
                ada_rows(0, KD)
                ada_turn(ROWM, done=g == 3)
            norm(0, TT)
            pe.wait_ge(tables_in, 32)
            for j in range(12):
                projection(TT, fresh=j == 0)
                if 0 <= j - 2 < 8:
                    pe.wait_ge(gemm_free, tile_unit(j - 2) + 1)
                    dup_unit(cn("rot"), (Q0 if j - 2 < 4 else K0)[:, (j - 2) % 4, 0:T], T)
            split_tok_tiles(4, 4)
            split_tok_tiles(4, 4)
            pe.wait_ge(v_normed, 1)
            for t in range(4):
                b = unit_begin()
                for g in range(4):
                    mm(b[:, g * P:(g + 1) * P], VG[:, t, g * P:(g + 1) * P], pr("sgu_w", g * P, (g + 1) * P),
                       True, True, g == 3)
            ready_wait()

            def ada_step(s):
                if s and s % 4 == 0:
                    ada_turn(ROWM)
                ada_rows(2 * (s % 4), 2)
                if s % 4 == 1 and s >= 9:
                    diff_square_mean((s - 9) // 4)

            def diff_square_mean(n):
                pe.wait_ge(diff_sq, n + 1)
                if 0 < n < 6:
                    pe.wait_ge(diff_root, n)
                pe.matmul(DIFF(n), cn("mean_e"), SQM[:, n // 2, n % 2 * T:(n % 2 + 1) * T],
                          start=True, stop=True).then_inc(diff_mean, 1)

            attention(units_even(), ada_step)
            ada_turn(ROWM, done=True)
            for n in (6, 7):
                diff_square_mean(n)
            ready_wait()
            for j in range(KD):
                split_tile(unit_begin()[:, :], lambda kk: PH[:, kk, :], lambda kk: CL[:, kk, :], KD)
            norm(1, TT)
            skip_to_chunk()
            for part in range(2):
                ffn_part(TT, st["u"], ada=part)
                st["h"] += FH
                if part == 0:
                    st["alo"] += KD

            norm(2, TT)
            u_q = st["u"]
            for j in range(12):
                if j < 10:
                    projection(TT if j < 2 else T, fresh=j == 0)
                if j >= 2:
                    pe.wait_ge(gemm_free, u_q + tile_unit(j - 2) + 1)
                    dup_unit(cn("rot"), kq_tile(j - 2)[:, 0:T], T)
            split_tok_tiles(4, 2)
            ready_wait()
            for kv in range(4):
                dup_unit(cn(f"dup{kv % 2}"), K1[:, kv // 2, :], TT)
            ready_wait()
            attention(units_odd())
            out_projection(PH)
            norm(3, T)
            ready_wait()
            st["alo"] += KD
            ffn(2, T)
            norm(4, T)

            for l in range(2):
                for j in range(22):
                    projection(T, fresh=j == 0)
                projection(T, m=4)
                split_tok_tiles(2, 1)
                split_tok_tiles(2, 1)
                split_tok_tiles(2, 2)
                ready_wait()
                dup_unit(cn("dup0"), SK[:, 0, :], T)
                dup_unit(cn("dup1"), SK[:, 0, :], T)
                dup_unit(cn("dup0"), DKI[:, 0, :], T)
                dup_unit(cn("dup1"), DKI[:, 0, :], T)
                ready_wait()
                st["p"] = 0
                attention(units_second(l)[:16])
                for qt in range(2):
                    for h in range(4):
                        b = (h % 2) * HD
                        dup_unit(DQI[b:b + HD, h // 2, qt * P:(qt + 1) * P], DKID[b:b + HD, 0, :], T)
                    pairs(FILL_INDEX[qt])
                ready_wait()
                pe.wait_ge(gemm_free, st["u"])
                attention(units_second(l)[16:])

                pairs(FILL_START)
                pe.wait_ge(rw_low, l + 1)
                for j in range(2):
                    dup_unit(pr(f"wa_up_{l}", j * P, (j + 1) * P)[0:64], LOW[0:64, 0, :], T)
                for j in range(2):
                    dup_unit(pr(f"wa_up_{l}", j * P, (j + 1) * P)[64:128], RP[64:128, 6, :], T)
                for j in range(2):
                    dup_unit(pr(f"g_up_{l}", j * P, (j + 1) * P), LOW[:, 1, :], T)
                pairs(FILL_LOW)
                ready_wait()
                b = unit_begin()
                mm(b[:, :], cn("blk64"), KNORM[:, :, :].rearrange("p a b -> p (a b)"), True, True, True)
                b = unit_begin()
                mm(b[:, :], cn("blk64"), RKK[:, :, :].rearrange("p a b -> p (a b)"), True, True, True)
                pairs(FILL_NORM)
                ready_wait()
                for src in (lambda j: KR[:, j, 0, :], lambda j: BH[:, j, :], lambda j: KH[:, j, :], lambda j: RP[:, 4 + j, :]):
                    b = unit_begin()
                    for cp in range(2):
                        for j in range(2):
                            ins = pe.transpose(b[:, (2 * cp + j) * P:(2 * cp + j + 1) * P], src(j)[:, cp * P:(cp + 1) * P], ident)
                    ins.then_inc(gemm_done, 1)
                for m in range(8):
                    b0, cp, j = m // 4 * HD, m // 2 % 2, m % 2
                    tok = slice(cp * P, (cp + 1) * P)
                    b = unit_begin()
                    rhs = KR[b0:b0 + HD, j, :, tok]
                    mm(b[:, 0:256].rearrange("p (a b) -> p a b", a=2), BH[b0:b0 + HD, j, tok], rhs, True, True)
                    mm(b[:, 256:512].rearrange("p (a b) -> p a b", a=2), KH[b0:b0 + HD, j, tok], rhs, True, True, True)
                for par in range(2):
                    b = unit_begin()
                    for h in range(4):
                        b0, cp, j = par * HD, h // 2, h % 2
                        tok = slice(cp * P, (cp + 1) * P)
                        mm(b[:, h * P:(h + 1) * P], KR[b0:b0 + HD, j, 0, tok], BH[b0:b0 + HD, j, tok], True, True, h == 3)
                pairs(FILL_MATRIX)
                for lev in range(5):
                    ready_wait()
                    for q in range(2):
                        b = unit_begin()
                        for h in range(4):
                            m = 4 * q + h
                            mm(b[:, h * P:(h + 1) * P], LK[:, m, :], XX[:, m, 0:P], True, True, h == 3)
                    pairs(FILL_LEVEL)
                    ready_wait()
                    for q in range(4):
                        b = unit_begin()
                        for h in range(2):
                            m = 2 * q + h
                            mm(b[:, 2 * h * P:(2 * h + 1) * P], XX[:, m, P:2 * P], PP[:, m, :], True, True)
                            mm(b[:, (2 * h + 1) * P:(2 * h + 2) * P], PP[:, m, :], XX[:, m, P:2 * P], True, True, h == 1)
                    pairs(FILL_LEVEL)
                ready_wait()
                b = unit_begin()
                for m in range(8):
                    mm(b[:, m * 64:(m + 1) * 64], MM[:, m, 256:384], TOK[3][:, m // 2 % 2, head_cols(m)],
                       True, True, m == 7)
                b = unit_begin()
                for m in range(8):
                    b0, cp, j = m // 4 * HD, m // 2 % 2, m % 2
                    mm(b[b0:b0 + HD, (2 * cp + j) * P:(2 * cp + j + 1) * P], TOK[0][:, cp, head_cols(m)],
                       XX[:, m, P:2 * P], True, True, m == 7)
                ready_wait()
                b = unit_begin()
                for m in range(8):
                    mm(b[:, m * 64:(m + 1) * 64], XX[:, m, P:2 * P], MVS[:, m, :], True, True, m == 7)
                ready_wait()
                for c in range(4):
                    cp, rb = c // 2, (c % 2) * 64
                    if c:
                        ready_wait()
                    for par in range(2):
                        b, b0 = unit_begin(), par * HD
                        for j in range(2):
                            mm(b[rb:rb + 64, j * 64:(j + 1) * 64], GTN[b0:b0 + HD, 2 * cp + j, rb:rb + 64],
                               STATE[b0:b0 + HD, c, j * 64:(j + 1) * 64], True, True, j == 1)
                    ready_wait()
                    b = unit_begin()
                    for n in range(4):
                        b0, j = n // 2 * HD, n % 2
                        o, hc = b[b0:b0 + HD, j * 64:(j + 1) * 64], head_cols(4 * (n // 2) + j)
                        mm(o, TOK[1][rb:rb + 64, cp, hc], SA[rb:rb + 64, n, :], True, False)
                        mm(o, TOK[2][rb:rb + 64, cp, hc], TOK[3][rb:rb + 64, cp, hc], False, True, n == 3)
                    b = unit_begin()
                    for n in range(4):
                        b0, j = n // 2 * HD, n % 2
                        mm(b[b0:b0 + HD, j * 64:(j + 1) * 64], STATE[b0:b0 + HD, c, j * 64:(j + 1) * 64],
                           KR[b0:b0 + HD, j, 1, c * 64:(c + 1) * 64], True, True, n == 3)
                    b = unit_begin()
                    for n in range(4):
                        b0, j = n // 2 * HD, n % 2
                        m = 4 * (n // 2) + 2 * cp + j
                        o = b[b0:b0 + HD, j * 64:(j + 1) * 64]
                        mm(o, SA[rb:rb + 64, n, :], MM[rb:rb + 64, m, 128 + rb:192 + rb], True, False)
                        mm(o, TOK[3][rb:rb + 64, cp, head_cols(m)], MM[rb:rb + 64, m, 384 + rb:448 + rb],
                           False, True, n == 3)
                ready_wait()
                dup_unit(cn("blk64"), YT[:, :, :].rearrange("p a b -> p (a b)"), 512)
                ready_wait()
                dup_unit(cn("blk64"), YS[:, :, :].rearrange("p a b -> p (a b)"), 512)
                ready_wait()

                pairs(KD)
                skip_to_chunk()
                out_projection(PL)
                ready_wait()
                norm(5 + 2 * l, T, layer_norm=True)
                pe.wait_ge(n_a, 8 * (6 + 2 * l))
                if l == 1:
                    rw = pr("router_w").rearrange("p (k e) -> p k e", k=KD)
                    for t in range(2):
                        b = unit_begin()
                        for kk in range(KD):
                            mm(b[:, 0:8], X[:, kk, t * P:(t + 1) * P], rw[:, kk, :], kk == 0, kk == KD - 1, kk == KD - 1)
                    ready_wait()
                    b = unit_begin()
                    for t in range(2):
                        ins = pe.transpose(b[0:8, t * P:(t + 1) * P], CWT[:, t, :], ident)
                    ins.then_inc(gemm_done, 1)
                    ready_wait()
                    for e in range(EXPERTS):
                        dup_unit(sel8[0:8, e, :], CWR[0:8, :], T)
                    ready_wait()
                ready_wait()
                st["alo"] += KD
                ffn(2 if l == 0 else EXPERTS, T)
                norm(6 + 2 * l, T, layer_norm=True)

        @block.scalar
        def _(act):
            st = dict(u=0, a=0, g=0, tmp=0, s=0, h=0, ada=0, p=0, used=[0, 0], i=None)
            SQ = SQM

            def f(o, i, fn, **kw):
                return nc.scalar.activation(o, i, fn, **kw)

            def copy_rows(row):
                act.wait_ge(ada_row, st["ada"] + 1)
                f(row[0:2, :], ROWS[0:2, :], ACT.Copy).then_inc(ada_copied, 1)
                st["ada"] += 1

            def norm(ni, tt, src, dst, scale, shift, eps, split=False, rows=0, ahead=None):
                SQ, RS = SQN(ni), RSN(ni)
                for j in range(KD):
                    if ni >= 5:
                        act.wait_ge(n_c, KD * (ni - 5) + j + 1)
                    f(SQ[:, j, 0:tt], src[:, j, 0:tt], ACT.Square).then_inc(n_sq, 1)
                for _ in range(rows):
                    copy_rows(ROWM)
                if ahead is not None:
                    st["c"] = 0
                    high_parts(ahead, AHEAD)
                act.wait_ge(n_mm, ni + 1)
                f(RS[:, 0:tt], NORM[:, 0:tt], ACT.Sqrt, bias=eps).then_inc(n_root, 1)
                for j in range(KD):
                    act.wait_ge(n_x, KD * ni + j + 1)
                    for s in range(tt // T):
                        d = dst[:, j, s * T:(s + 1) * T]
                        if split:
                            ins = f(split[:, j, s * T:(s + 1) * T], SQ[:, j, s * T:(s + 1) * T], ACT.Identity,
                                    bias=shift(j, s))
                        elif shift is None:
                            ins = f(d, d, ACT.Copy, scale=scale(j, s))
                        else:
                            ins = f(d, d, ACT.Identity, scale=scale(j, s), bias=shift(j, s))
                    ins.then_inc(n_a, 1)

            def attention(us, rows=False):
                gs, ng = groups(us)
                a0, g0 = st["a"], st["g"]
                for s in range(len(us) + 2):
                    if s < len(us):
                        u, a = us[s], a0 + s
                        act.wait_ge(at_m, a + 1)
                        if s >= 4:
                            if us[s - 4]["last"]:
                                act.wait_ge(at_t, g0 + gs[s - 4] + 1)
                            else:
                                act.wait_ge(at_n, a - 2)
                        src = bank[s % 2][:, 0:u["nk"]] if u["mask"] is None else SM[:, a % 2, 0:u["nk"]]
                        c = slice(a % 4, a % 4 + 1)
                        ins = f(E[:, a % 4, 0:u["nk"]], src, ACT.Exp, bias=nm[:, c], scale=SCALE, accum_out=sm[:, c])
                        if u["sink"] is not None:
                            ins = f(es[:, c], SINK(u["sink"]), ACT.Exp, bias=nm[:, c])
                        ins.then_inc(at_e, 1)
                    if s >= 2 and us[s - 2]["last"]:
                        u, g = us[s - 2], gs[s - 2]
                        act.wait_ge(at_t, g0 + g + 1)
                        if g >= 2:
                            act.wait_ge(at_o, g0 + g - 1)
                        f(ET[:, g % 2, 0:u["nk"]], bank[2 + g % 2][:, 0:u["nk"]], ACT.Copy).then_inc(at_tv, 1)
                    if rows and 1 <= s <= len(us) and s % 4 == 0:
                        copy_rows(ROWM)
                    if rows and s < len(us):
                        if s == 3:
                            f(PH[:, 0:4, :], CAT0[:, 0:4, :], ACT.Copy).then_inc(a_hi, 1)
                        if s % 4 == 0 and s >= 8:
                            diff_square((s - 8) // 4)
                        if s % 4 == 2 and s >= 10:
                            diff_sqrt((s - 10) // 4)
                        if s % 4 == 0 and s >= 12:
                            diff_high((s - 12) // 4)
                st["a"] += len(us)
                st["g"] += ng

            def diff_part(n):
                return n // 2, slice(n % 2 * T, (n % 2 + 1) * T)

            def diff_square(n):
                h, cols = diff_part(n)
                act.wait_ge(at_out, 2 * (n + 1))
                f(SQM[:, h, cols], CAT0[:, 4 + h, cols], ACT.Square).then_inc(diff_sq, 1)

            def diff_sqrt(n):
                h, cols = diff_part(n)
                act.wait_ge(diff_mean, n + 1)
                f(SQM[:, 4 + h, cols], DIFF(n), ACT.Sqrt, bias=pr("eps6")).then_inc(diff_root, 1)

            def diff_high(n):
                h, cols = diff_part(n)
                act.wait_ge(diff_normed, n + 1)
                f(PH[:, 4 + h, cols], CAT0[:, 4 + h, cols], ACT.Copy).then_inc(a_hi, 1)

            def val(x, per):
                return x if st["i"] is None else st["i"] * per + x

            def gates(l, n):
                for i, j in PAIRS[st["p"]:st["p"] + n]:
                    c = st["u"]
                    act.wait_ge(gemm_done, c + 1)
                    if st["p"] >= 2:
                        act.wait_ge(gemm_free, st["used"][st["p"] % 2])
                    f(GATE[:, st["p"] % 2, :], bank[c % BANKS][:, 0:T], ACT.Sigmoid,
                      bias=pr(f"gate_b_{l}", i * KD + j, i * KD + j + 1)).then_inc(act_tmp, 1)
                    st["u"] += 2
                    st["used"][st["p"] % 2] = st["u"]
                    st["tmp"] += 1
                    st["p"] += 1

            def high_parts(c0, upto):
                while st["c"] < upto:
                    c, s = c0 + st["c"], st["s"] + st["c"]
                    act.wait_ge(w_loaded[c % RING], val(16 * (c // RING + 1), 16 * PART_CHUNKS // RING))
                    if s >= SPLIT:
                        act.wait_ge(split_begun, val(s - SPLIT + 2, PART_CHUNKS))
                    f(WH[:, s % SPLIT, :], ring[:, c % RING, :], ACT.Copy).then_inc(w_hi, 1)
                    st["c"] += 1

            def ffn_part(c0, tt, ada, kept=False):
                u0 = st["u"]
                if not kept:
                    st["c"] = 0
                for q in range(FH):
                    u = u0 + 2 * q
                    high_parts(c0, gate_chunks(q, ada) + AHEAD)
                    if ada and q and ADA_HALVES[q - 1][-1] % 2:
                        copy_rows(ROWF)
                    act.wait_ge(gemm_done, val(u + 1, UNITS_FFN))
                    if st["h"] + q >= 2:
                        act.wait_ge(h_lo, val(st["h"] + q - 1, FH))
                    f(TMP[:, q % 2, 0:tt], bank[u % BANKS][:, 0:tt], ACT.Silu).then_inc(act_tmp, 1)
                    high_parts(c0, gate_chunks(q, ada) + 2 + AHEAD)
                    act.wait_ge(gemm_free, val(u + 2, UNITS_FFN))
                    f(HH[:, q, 0:tt], TMP[:, q % 2, 0:tt], ACT.Copy).then_inc(h_hi, 1)
                if ada:
                    high_parts(c0, gate_chunks(FH, ada) - 2 + AHEAD)
                    copy_rows(ROWF)
                high_parts(c0, part_chunks(ada))

            def ffn(k, count, tt, ada=False):
                c0, u0 = FFN_START[k], st["u"]
                if ada:
                    for part in range(count):
                        ffn_part(FFN_START[k + part], tt, True, kept=part == 0)
                        st["u"] += UNITS_FFN
                        st["s"] += part_chunks(True)
                        st["h"] += FH
                        st["tmp"] += FH
                    return
                with act.Fori(0, count) as i:
                    st["i"] = i
                    ffn_part(c0, tt, False)
                st["i"] = None
                st["u"] = u0 + count * UNITS_FFN
                st["s"] += count * PART_CHUNKS
                st["h"] += count * FH
                st["tmp"] += count * FH

            act.wait_ge(cond_in, 16)
            f(cs, pr("cvec"), ACT.Silu).then_inc(silu_c, 1)
            act.wait_ge(silu_c, 1)
            f(csH[:, :], cs, ACT.Copy).then_inc(a_hi, 1)
            norm_mod = lambda l, n: (lambda j, s: modg[:, 2 * l + n, j, s:s + 1])
            norm_sh = lambda l, n: (lambda j, s: mod[:, l, 24 * n + j, s:s + 1])
            act.wait_ge(x_in, 16)
            norm(0, TT, X, A, None, norm_sh(0, 0), pr("eps6"), split=PH, rows=4, ahead=PROJ_START[0])
            high_parts(PROJ_START[0], 30)
            for j in range(4):
                act.wait_ge(gemm_free, tile_unit(8 + j) + 1)
                f(U0[:, j, :], U0[:, j, :], ACT.Gelu)
            high_parts(PROJ_START[0], 36)
            for t in range(4):
                act.wait_ge(gemm_free, 20 + t + 1)
                f(VT[:, t, :], VT[:, t, :], ACT.Gelu).then_inc(gelu_v, 1)
            high_parts(PROJ_START[0], 40)
            st["s"] += 40
            act.wait_ge(v_var, 1)
            f(VRS, VRS, ACT.Sqrt, bias=pr("eps6")).then_inc(v_root, 1)
            act.wait_ge(lam_sum, 1)
            f(lam[:, 2:4], lam[:, 0:2], ACT.Exp).then_inc(lam_exp, 1)
            st["u"] = 20
            attention(units_even(), rows=True)
            st["c"] = 0
            high_parts(PROJ_START[1], AHEAD)
            for n in (6, 7):
                diff_square(n)
                diff_sqrt(n)
                diff_high(n - 1)
            diff_high(7)
            high_parts(PROJ_START[1], 16)
            st["s"] += 16
            act.wait_ge(gemm_free, 20 + 8 + 4 + 8)
            norm(1, TT, X, A, None, norm_sh(0, 1), pr("eps6"), split=AH, ahead=FFN_START[0])
            st["u"] = 40
            ffn(0, 2, TT, ada=True)
            act.wait_ge(gemm_free, st["u"])
            act.wait_ge(mod_ready, 1)
            norm(2, TT, X, A, None, norm_sh(1, 0), pr("eps6"), split=PH, ahead=PROJ_START[2])
            high_parts(PROJ_START[2], 24)
            st["s"] += 24
            st["u"] += 10 + 4 + 10 + 4
            SINK = lambda h: pr("odd_sink", h, h + 1)
            st["c"] = 0
            high_parts(PROJ_START[3], AHEAD)
            attention(units_odd())
            for j in range(KD):
                act.wait_ge(at_out, 16 + 4 * (j + 1))
                f(PH[:, j, 0:T], CAT1[:, j, :], ACT.Copy).then_inc(a_hi, 1)
            high_parts(PROJ_START[3], 16)
            st["s"] += 16
            st["u"] += KD
            act.wait_ge(gemm_free, st["u"])
            norm(3, T, X, A, None, norm_sh(1, 1), pr("eps6"), split=AH)
            ffn(2, 2, T)
            act.wait_ge(gemm_free, st["u"])
            norm(4, T, X, X, lambda j, s: pr("final_g", j, j + 1), None, pr("eps6"), ahead=PROJ_START[4])

            for l in range(2):
                for j in range(KD):
                    act.wait_ge(n_a, KD * (4 + 2 * l) + j + 1)
                    f(PH[:, j, 0:T], X[:, j, 0:T], ACT.Copy).then_inc(a_hi, 1)
                high_parts(PROJ_START[4 + 2 * l], 54)
                st["s"] += 54
                SINK = lambda h: pr(f"sinks_{l}", h, h + 1)
                act.wait_ge(fox_pre, l + 1)
                f(FC[0:4, 3, :], FC[0:4, 2, :], ACT.Exp).then_inc(fox_e, 1)
                act.wait_ge(fox_e, l + 1)
                f(FC[0:4, 3, :], FC[0:4, 3, :], ACT.Ln, bias=1.0).then_inc(fox_ln, 1)
                st["p"], st["u"] = 0, UB[l]["index"]
                attention(units_second(l)[:16])
                for qt in range(2):
                    st["u"] += 4
                    gates(l, FILL_INDEX[qt])
                attention(units_second(l)[16:])
                act.wait_ge(rw_shift, l + 1)
                f(LOW[0:64, 0, :], RP[0:64, 6, :], ACT.Tanh)
                f(LOW[:, 1, :], RP[:, 7, :], ACT.Sigmoid).then_inc(rw_low, 1)
                gates(l, FILL_START)
                st["u"] += 6
                act.wait_ge(rw_sig, l + 1)
                f(LWV, LWV, ACT.Sigmoid)
                f(AV, AV, ACT.Sigmoid).then_inc(rw_pre, 1)
                act.wait_ge(rw_c, l + 1)
                f(EC, CC, ACT.Exp)
                f(EN, CC, ACT.Exp, scale=-1.0)
                f(EX, EX, ACT.Exp).then_inc(rw_exp, 1)
                gates(l, FILL_LOW)
                st["u"] += 2
                act.wait_ge(rw_ks, l + 1)
                f(KNORM, KNORM, ACT.Sqrt).then_inc(rw_kroot, 1)
                gates(l, FILL_NORM)
                st["u"] += 4 + 8 + 2
                gates(l, FILL_MATRIX)
                for lev in range(5):
                    st["u"] += 2
                    gates(l, FILL_LEVEL)
                    st["u"] += 4
                    gates(l, FILL_LEVEL)
                act.wait_ge(rw_var, l + 1)
                f(YS, YS, ACT.Sqrt, bias=pr("epsgn")).then_inc(rw_vroot, 1)
                st["u"] = UB[l]["merge"]
                for j in range(KD):
                    gates(l, 1)
                    if j >= 2:
                        f(PL[:, j - 2, 0:T], ACC[:, j - 2, :], ACT.Copy).then_inc(a_hi, 1)
                act.wait_ge(gemm_free, st["u"])
                for j in (KD - 2, KD - 1):
                    f(PL[:, j, 0:T], ACC[:, j, :], ACT.Copy).then_inc(a_hi, 1)
                st["c"] = 0
                high_parts(PROJ_START[5 + 2 * l], 16)
                st["s"] += 16
                norm(5 + 2 * l, T, X, X, lambda j, s: pr(f"ln1g_{l}", j, j + 1),
                     lambda j, s: pr(f"ln1b_{l}", j, j + 1), pr("eps5"))
                for j in range(KD):
                    act.wait_ge(n_a, KD * (5 + 2 * l) + j + 1)
                    f(AH[:, j, 0:T], X[:, j, 0:T], ACT.Copy).then_inc(a_hi, 1)
                if l == 1:
                    act.wait_ge(top_v, 1)
                    f(EE[:, 0:2], EE[:, 0:2], ACT.Exp).then_inc(top_e, 1)
                st["u"] = UB[l]["ffn"]
                ffn(4 + 2 * l, 2 if l == 0 else EXPERTS, T)
                norm(6 + 2 * l, T, X, X, lambda j, s: pr(f"ln2g_{l}", j, j + 1),
                     lambda j, s: pr(f"ln2b_{l}", j, j + 1), pr("eps5"), ahead=PROJ_START[6] if l == 0 else None)

        @block.vector
        def _(dve):
            V = nc.vector
            st = dict(u=0, a=0, g=0, tmp=0, chain=0, s=0, h=0, p=0, i=None)
            SQ = SQM

            def link(ins):
                st["chain"] += 1
                ins.then_inc(dve_chain, 1)
                dve.wait_ge(dve_chain, st["chain"])

            def take():
                dve.wait_ge(gemm_done, st["u"] + 1)
                st["u"] += 1
                return bank[(st["u"] - 1) % BANKS]

            def free(ins):
                ins.then_inc(gemm_free, 1)

            def settled_but_last():
                dve.wait_ge(gemm_free, st["u"] - 1)

            def settled():
                dve.wait_ge(gemm_free, st["u"])

            marks = {}

            def mark(semaphore):
                n, slot = marks.get(semaphore.name, (0, len(marks)))
                if n:
                    dve.wait_ge(semaphore, n)
                marks[semaphore.name] = (n + 1, slot)
                V.memset(small(140 + slot, 1), 0.0).then_inc(semaphore, 1)

            def go():
                mark(ready)

            def copy_units(dsts, m=P):
                for d in dsts:
                    free(V.tensor_copy(d, take()[0:d.shape[0], 0:d.shape[1]]))

            def norm(ni, tt, src, dst, split=None, ahead=None):
                SQ, RS = SQN(ni), RSN(ni)
                if ni >= 5:
                    dve.wait_ge(n_mean, ni - 4)
                    for j in range(KD):
                        V.tensor_tensor(src[:, j, 0:tt], src[:, j, 0:tt], MEAN[:, 0:tt], ALU.subtract).then_inc(n_c, 1)
                if ahead is not None:
                    st["c"] = 0
                    low_parts(ahead, AHEAD)
                dve.wait_ge(n_root, ni + 1)
                link(V.reciprocal(RS[:, 0:tt], RS[:, 0:tt]))
                if ni >= 5:
                    dve.wait_ge(n_c, KD * (ni - 4))
                for j in range(KD):
                    if split:
                        for s in range(tt // T):
                            cols = slice(s * T, (s + 1) * T)
                            ins = V.scalar_tensor_tensor(SQ[:, j, cols], src[:, j, cols], split[0](j, s), RS[:, cols],
                                                         ALU.mult, ALU.mult)
                    else:
                        ins = V.tensor_tensor(dst[:, j, 0:tt], src[:, j, 0:tt], RS[:, 0:tt], ALU.mult)
                    ins.then_inc(n_x, 1)
                if split:
                    gain, shift, high, low = split
                    for j in range(KD):
                        dve.wait_ge(n_a, KD * ni + j + 1)
                        for s in range(tt // T):
                            cols = slice(s * T, (s + 1) * T)
                            ins = V.scalar_tensor_tensor(low[:, j, cols], SQ[:, j, cols], shift(j, s),
                                                         high[:, j, cols].bitcast(F32), ALU.add, ALU.subtract)
                        ins.then_inc(a_lo, 1)

            def projections(k, outs):
                c0, end, total = PROJ_START[k], 0, sum(x[1] for x in outs)
                for d, chunks, put in outs:
                    end += chunks
                    low_parts(c0, min(total, end + AHEAD))
                    b = take()[0:d.shape[0], 0:d.shape[1]]
                    free(V.tensor_copy(d, b) if put is None else put(d, b))
                st["s"] += total

            def input_low(high, low, src, n0):
                for j in range(KD):
                    dve.wait_ge(a_hi, n0 + j + 1)
                    V.tensor_tensor(low[:, j, 0:T], src[:, j, 0:T], high[:, j, 0:T].bitcast(F32),
                                    ALU.subtract).then_inc(a_lo, 1)

            def tok(dsts, chunks):
                return [(d, chunks if i == 0 else 0, None) for i, d in enumerate(dsts)]

            def rope(q, j):
                b = take()[:, 0:T]
                dve.wait_ge(gemm_free, st["u"] - 1)
                link(V.tensor_tensor(RT1[:, 0, :], b, cn("sin"), ALU.mult))
                link(V.tensor_tensor(RT1[:, 1, :], q, cn("cos"), ALU.mult))
                free(V.tensor_tensor(q, RT1[:, 0, :], RT1[:, 1, :], ALU.add))

            def diff_norm(n):
                h, cols = n // 2, slice(n % 2 * T, (n % 2 + 1) * T)
                dve.wait_ge(diff_root, n + 1)
                link(V.reciprocal(SQM[:, 4 + h, cols], SQM[:, 4 + h, cols]))
                V.scalar_tensor_tensor(CAT0[:, 4 + h, cols], CAT0[:, 4 + h, cols], lam[:, 6:7], SQM[:, 4 + h, cols],
                                       ALU.mult, ALU.mult).then_inc(diff_normed, 1)

            def diff_low(n):
                h, cols = n // 2, slice(n % 2 * T, (n % 2 + 1) * T)
                dve.wait_ge(a_hi, 2 + n + 1)
                V.tensor_tensor(CL[:, 4 + h, cols], CAT0[:, 4 + h, cols], PH[:, 4 + h, cols].bitcast(F32), ALU.subtract)

            def attention(us, diff=False):
                gs, ng = groups(us)
                a0, g0 = st["a"], st["g"]
                for s in range(len(us) + 4):
                    if diff and s < len(us):
                        if s == 6:
                            dve.wait_ge(a_hi, 2)
                            V.tensor_tensor(CL[:, 0:4, :], CAT0[:, 0:4, :], PH[:, 0:4, :].bitcast(F32), ALU.subtract)
                        if s % 4 == 3 and s >= 11:
                            diff_norm((s - 11) // 4)
                        if s % 4 == 1 and s >= 13:
                            diff_low((s - 13) // 4)
                    if s < len(us):
                        u, a = us[s], a0 + s
                        c = slice(a % 4, a % 4 + 1)
                        b = bank[s % 2][:, 0:u["nk"]]
                        dve.wait_ge(at_s, a + 1)
                        if s >= 2:
                            dve.wait_ge(at_e, a - 1)
                        if u["mask"] is not None:
                            link(V.tensor_tensor_reduce(SM[:, a % 2, 0:u["nk"]], b, u["mask"], 1.0, OUT_OF_LIST,
                                                        ALU.add, ALU.max, mx[:, c]))
                        else:
                            link(V.reduce_max(mx[:, c], b, AX_X))
                        if u["sink"] is not None:
                            V.tensor_scalar(nm[:, c], mx[:, c], -SCALE, nsink[:, u["sink"]:u["sink"] + 1],
                                            ALU.mult, ALU.min).then_inc(at_m, 1)
                        else:
                            V.tensor_scalar(nm[:, c], mx[:, c], -SCALE, None, ALU.mult).then_inc(at_m, 1)
                    if 1 <= s <= len(us):
                        u, a = us[s - 1], a0 + s - 1
                        c = slice(a % 4, a % 4 + 1)
                        e = E[:, a % 4, 0:u["nk"]]
                        dve.wait_ge(at_e, a + 1)
                        if u["sink"] is not None:
                            link(V.tensor_tensor(sm[:, c], sm[:, c], es[:, c], ALU.add))
                        link(V.reciprocal(rc[:, c], sm[:, c]))
                        if not diff or not u["last"]:
                            V.tensor_scalar(e, e, rc[:, c], None, ALU.mult).then_inc(at_n, 1)
                        else:
                            link(V.tensor_tensor(r2[:, c], rc[:, c], lam[:, 4:5], ALU.mult))
                            dve.wait_ge(at_n, a)
                            V.scalar_tensor_tensor(e, e, r2[:, c], E[:, (a - 1) % 4, 0:u["nk"]],
                                                   ALU.mult, ALU.add).then_inc(at_n, 1)
                    if s >= 4 and us[s - 4]["last"]:
                        u, g = us[s - 4], gs[s - 4]
                        b0, m = u["dst"].base_partition(), u["dst"].shape[0]
                        dve.wait_ge(at_o, g0 + g + 1)
                        V.tensor_copy(u["dst"], bank[4 + g % 2][b0:b0 + m, 0:P]).then_inc(at_out, 1)
                st["a"] += len(us)
                st["g"] += ng

            def val(x, per):
                return x if st["i"] is None else st["i"] * per + x

            def pairs(n):
                for i, j in PAIRS[st["p"]:st["p"] + n]:
                    k = st["p"] % 2
                    st["u"] += 1
                    b = take()[:, 0:T]
                    st["tmp"] += 1
                    dve.wait_ge(act_tmp, st["tmp"])
                    if i == 0:
                        for s in range(2):
                            c = slice(s * P, (s + 1) * P)
                            free(V.tensor_tensor(ACC[:, j, c], b[:, c], GATE[:, k, c], ALU.mult))
                    else:
                        free(V.tensor_tensor(PROD[:, k, :], b, GATE[:, k, :], ALU.mult))
                        dve.wait_ge(gemm_free, st["u"] - 1)
                        free(V.tensor_tensor(ACC[:, j, :], ACC[:, j, :], PROD[:, k, :], ALU.add))
                    st["p"] += 1

            def low_parts(c0, upto):
                while st["c"] < upto:
                    c, s = c0 + st["c"], st["s"] + st["c"]
                    dve.wait_ge(w_hi, val(s + 1, PART_CHUNKS))
                    V.tensor_tensor(WL[:, s % SPLIT, :], ring[:, c % RING, :], WH[:, s % SPLIT, :].bitcast(F32),
                                    ALU.subtract).then_inc(w_taken, 1)
                    st["c"] += 1

            def hidden_low(q, tt):
                dve.wait_ge(h_hi, val(st["h"] + q + 1, FH))
                V.tensor_tensor(HL[:, q, 0:tt], TMP[:, q % 2, 0:tt], HH[:, q, 0:tt].bitcast(F32), ALU.subtract).then_inc(h_lo, 1)

            def ffn_part(c0, tt, gate, ada, experts, kept=False):
                u0, h = st["u"], tt // 2
                if not kept:
                    st["c"] = 0
                for q in range(FH):
                    u = u0 + 2 * q + 1
                    low_parts(c0, gate_chunks(q, ada) + 2 + AHEAD)
                    dve.wait_ge(gemm_done, val(u + 1, UNITS_FFN))
                    dve.wait_ge(act_tmp, val(st["tmp"] + q + 1, FH))
                    if experts:
                        V.tensor_tensor(TMP[:, q % 2, 0:T], TMP[:, q % 2, 0:T], CW[:, st["i"], :], ALU.mult).then_inc(cw_done, 1)
                        dve.wait_ge(cw_done, val(q + 1, FH))
                    for s in range(2):
                        free(V.tensor_tensor(TMP[:, q % 2, s * h:(s + 1) * h], TMP[:, q % 2, s * h:(s + 1) * h],
                                             bank[u % BANKS][:, s * h:(s + 1) * h], ALU.mult))
                    if q:
                        hidden_low(q - 1, tt)
                hidden_low(FH - 1, tt)
                for j in range(KD):
                    u = u0 + 2 * FH + j
                    low_parts(c0, min(part_chunks(ada), gate_chunks(FH, ada) - 2 + -(-FH * (j + 1) // CHUNK) + AHEAD))
                    dve.wait_ge(gemm_done, val(u + 1, UNITS_FFN))
                    dve.wait_ge(gemm_free, val(u - UNITS_FFN + 1, UNITS_FFN))
                    residual(j, bank[u % BANKS], tt, gate)

            def ffn(k, count, tt, gate, ada=False, experts=False):
                c0, u0 = FFN_START[k], st["u"]
                dve.wait_ge(gemm_done, u0)
                if ada:
                    for part in range(count):
                        ffn_part(FFN_START[k + part], tt, gate, True, False, kept=part == 0)
                        st["u"] += UNITS_FFN
                        st["s"] += part_chunks(True)
                        st["h"] += FH
                        st["tmp"] += FH
                    return
                with dve.Fori(0, count) as i:
                    st["i"] = i
                    ffn_part(c0, tt, gate, False, experts)
                st["i"] = None
                st["u"] = u0 + count * UNITS_FFN
                st["s"] += count * PART_CHUNKS
                st["h"] += count * FH
                st["tmp"] += count * FH

            def residual(j, b, tt, gate):
                free(residual_parts(j, b, tt, gate))

            def residual_parts(j, b, tt, gate):
                for s in range(tt // T):
                    cols = slice(s * T, (s + 1) * T)
                    if gate is None:
                        ins = V.tensor_tensor(X[:, j, cols], X[:, j, cols], b[:, cols], ALU.add)
                    else:
                        ins = V.scalar_tensor_tensor(X[:, j, cols], b[:, cols], gate(j, s), X[:, j, cols],
                                                     ALU.mult, ALU.add)
                return ins

            def modulation(l, lo, hi):
                n = 2 * (hi - lo)
                src = ADA[:, 2 * lo:2 * hi].rearrange("p (j s) -> p j s", s=2)
                bias = pr(f"ada_b{l}", lo, hi).unsqueeze(2).broadcast_to([P, hi - lo, 2])
                link(V.tensor_tensor(mod[:, l, lo:hi, :], src, bias, ALU.add))

            def gains(l, n, name):
                g = pr(f"{name}{l}").unsqueeze(2).broadcast_to([P, KD, 2])
                return V.scalar_tensor_tensor(modg[:, 2 * l + n, :, :], mod[:, l, 24 * n + 8:24 * n + 16, :], 1.0, g,
                                              ALU.add, ALU.mult)

            dve.wait_ge(a_hi, 1)
            link(V.tensor_tensor(csL[:, :], cs, csH[:, :].bitcast(F32), ALU.subtract))
            dve.wait_ge(ada_done, 1)
            modulation(0, 0, 16)
            link(gains(0, 0, "n1g"))
            norm(0, TT, X, A, (lambda j, s: modg[:, 0, j, s:s + 1], lambda j, s: mod[:, 0, j, s:s + 1], PH, PL),
                 ahead=PROJ_START[0])
            dve.wait_ge(tables_in, 32)
            for j in range(12):
                low_parts(PROJ_START[0], 2 * (j + 1) + AHEAD)
                copy_units([(Q0, K0, U0)[j // 4][:, j % 4, :]])
                if 0 <= j - 2 < 8:
                    rope((Q0 if j - 2 < 4 else K0)[:, (j - 2) % 4, 0:T], j - 2)
            low_parts(PROJ_START[0], 32 + AHEAD)
            copy_units([VT[:, t, :] for t in range(4)])
            settled()
            dve.wait_ge(gelu_v, 4)
            for t in range(4):
                for g in range(4):
                    V.bn_stats(ST6[:, 4 * t + g, :], VT[:, t, g * P:(g + 1) * P])
            link(V.memset(small(159, 1), 0.0))
            low_parts(PROJ_START[0], 38)
            for n in range(16):
                ins = V.bn_aggr(MV2[:, n, :], ST6[:, n, :])
            link(ins)
            V.tensor_copy(VRS, MV2[:, :, 1]).then_inc(v_var, 1)
            low_parts(PROJ_START[0], 40)
            st["s"] += 40
            ll = pr("lqk").rearrange("p (a b) -> p a b", a=4)
            V.tensor_tensor_reduce(SQ[:, 7, 0:64], ll[:, 0, :], ll[:, 1, :], 1.0, 0.0, ALU.mult, ALU.add, lam[:, 0:1])
            V.tensor_tensor_reduce(SQ[:, 7, 64:128], ll[:, 2, :], ll[:, 3, :], 1.0, 0.0, ALU.mult, ALU.add,
                                   lam[:, 1:2]).then_inc(lam_sum, 1)
            dve.wait_ge(v_root, 1)
            link(V.reciprocal(VRS, VRS))
            for t in range(4):
                for g in range(4):
                    n = 4 * t + g
                    ins = V.tensor_scalar(VG[:, t, g * P:(g + 1) * P], VT[:, t, g * P:(g + 1) * P], MV2[:, n, 0:1],
                                          VRS[:, n:n + 1], ALU.subtract, ALU.mult)
            ins.then_inc(v_normed, 1)
            dve.wait_ge(lam_exp, 1)
            link(V.tensor_tensor(lam[:, 5:6], lam[:, 3:4], lam[:, 2:3], ALU.subtract))
            link(V.tensor_scalar(lam[:, 4:5], lam[:, 5:6], -LAM_INIT, None, ALU.add))
            link(V.tensor_scalar(lam[:, 6:7], pr("subln"), 1.0 - LAM_INIT, None, ALU.mult))
            copy_units([VV[:, t, :] for t in range(4)])
            sgub = pr("sgu_b").rearrange("p (g c) -> p g c", g=4)
            for t in range(4):
                b = take()[:, :].rearrange("p (g c) -> p g c", g=4)
                link(V.tensor_tensor(CAT0[:, 0:4, t * P:(t + 1) * P], b, sgub, ALU.add))
                free(V.tensor_tensor(CAT0[:, 0:4, t * P:(t + 1) * P], CAT0[:, 0:4, t * P:(t + 1) * P],
                                     U0[:, :, t * P:(t + 1) * P], ALU.mult))
            settled()
            go()
            attention(units_even(), diff=True)
            dve.wait_ge(ada_done, 2)
            modulation(0, 16, 48)
            link(gains(0, 1, "n2g"))
            st["c"] = 0
            low_parts(PROJ_START[1], AHEAD)
            diff_low(5)
            diff_norm(6)
            diff_low(6)
            diff_norm(7)
            diff_low(7)
            go()
            projections(1, [(X[:, j, :], 2, lambda d, b, j=j: residual_parts(j, b, TT, lambda j, s: mod[:, 0, 16 + j, s:s + 1]))
                            for j in range(KD)])
            settled()
            norm(1, TT, X, A, (lambda j, s: modg[:, 1, j, s:s + 1], lambda j, s: mod[:, 0, 24 + j, s:s + 1], AH, AL),
                 ahead=FFN_START[0])
            ffn(0, 2, TT, lambda j, s: mod[:, 0, 40 + j, s:s + 1], ada=True)
            dve.wait_ge(ada_done, 3)
            modulation(1, 0, 48)
            link(gains(1, 0, "n1g"))
            gains(1, 1, "n2g").then_inc(mod_ready, 1)

            settled()
            norm(2, TT, X, A, (lambda j, s: modg[:, 2, j, s:s + 1], lambda j, s: mod[:, 1, j, s:s + 1], PH, PL),
                 ahead=PROJ_START[2])
            link(V.tensor_scalar(nsink[:, 0:16], pr("odd_sink"), -1.0, None, ALU.mult))
            for j in range(12):
                if j < 10:
                    low_parts(PROJ_START[2], min(24, 2 * (j + 1) + AHEAD))
                    copy_units([kq_tile(j)])
                if j >= 2:
                    rope(kq_tile(j - 2)[:, 0:T], j - 2)
            st["s"] += 24
            settled()
            go()
            copy_units([V1[:, t, :] for t in range(4)])
            copy_units([KD1[:, kv, :] for kv in range(4)])
            settled()
            go()
            st["c"] = 0
            low_parts(PROJ_START[3], AHEAD)
            attention(units_odd())
            input_low(PH, CL, CAT1, 10)
            projections(3, [(X[:, j, 0:T], 2, lambda d, b, j=j: residual_parts(j, b, T, lambda j, s: mod[:, 1, 16 + j, s:s + 1]))
                            for j in range(KD)])
            settled()
            norm(3, T, X, A, (lambda j, s: modg[:, 3, j, s:s + 1], lambda j, s: mod[:, 1, 24 + j, s:s + 1], AH, AL))
            go()
            ffn(2, 2, T, lambda j, s: mod[:, 1, 40 + j, s:s + 1])
            settled()
            norm(4, T, X, X, ahead=PROJ_START[4])

            for l in range(2):
                input_low(PH, PL, X, 18 + 3 * KD * l)
                tiles_ = [SQ_[:, j, :] for j in range(4)] + [SK[:, 0, :]] + [RP[:, j, :] for j in range(8)]
                tiles_ += [x[:, j, :] for x in (FQ, FK, DQ, DQI) for j in range(2)] + [DKI[:, 0, :]]
                projections(4 + 2 * l, [(d, 2, None) for d in tiles_]
                            + [(FC[0:4, 1, :], 2, lambda d, b: V.tensor_scalar(d, b, pr(f"fbias_{l}")[0:4], None, ALU.add))]
                            + tok([SV[:, t, :] for t in range(2)], 2) + tok([DV[:, t, :] for t in range(2)], 2)
                            + tok([FV[:, t, :] for t in range(2)], 4))
                link(V.tensor_scalar(nsink[:, 0:8], pr(f"sinks_{l}"), -1.0, None, ALU.mult))
                settled()
                go()
                link(V.tensor_scalar(FC[0:4, 0, :], FC[0:4, 1, :], -1.0, None, ALU.mult))
                V.tensor_tensor(FC[0:4, 2, :], FC[0:4, 0, :], FC[0:4, 1, :], ALU.min).then_inc(fox_pre, 1)
                copy_units([SKD[:, 0, :], SKD[:, 1, :], DKD[:, 0, :], DKID[:, 0, :]])
                settled()
                go()
                st["p"] = 0
                attention(units_second(l)[:16])
                assert st["u"] == UB[l]["index"]
                dve.wait_ge(fox_ln, l + 1)
                link(V.tensor_scalar(FC[0:4, 1, :], FC[0:4, 1, :], 0.0, None, ALU.min))
                link(V.tensor_tensor(FC[0:4, 1, :], FC[0:4, 1, :], FC[0:4, 3, :], ALU.subtract))
                link(V.memset(FC[0:4, 3, :], 1.0))
                link(V.tensor_tensor_scan(FC[0:4, 2, :], FC[0:4, 3, :], FC[0:4, 1, :], 0.0, ALU.mult, ALU.add))
                V.tensor_scalar(FC[0:4, 0, :], FC[0:4, 2, :], 1.0 / SCALE, None, ALU.mult)
                link(V.tensor_scalar(FC[0:4, 1, :], FC[0:4, 2, :], -1.0 / SCALE, None, ALU.mult))
                for qt in range(2):
                    for h in range(4):
                        b = take()[:, 0:T]
                        w = DV[:, qt, HD + h:HD + h + 1]
                        if h == 0:
                            ins = V.tensor_scalar(DSC, b, 0.0, w, ALU.max, ALU.mult)
                            free(ins)
                        else:
                            free(V.tensor_scalar(DT, b, 0.0, w, ALU.max, ALU.mult))
                            settled()
                            link(V.tensor_tensor(DSC, DSC, DT, ALU.add))
                    link(V.tensor_tensor(DSC, DSC, cn("chunks", qt * T, (qt + 1) * T), ALU.add))
                    src = DSC
                    for r in range(8):
                        link(V.max(M8[:, 0:8], src))
                        link(V.match_replace(DWK, M8[:, 0:8], src, OUT_OF_LIST))
                        src = DWK
                    link(V.tensor_scalar(DMK[:, qt, :], DWK, OUT_OF_LIST / 2, NEG, ALU.is_gt, ALU.mult))
                    if qt:
                        go()
                    pairs(FILL_INDEX[qt])
                attention(units_second(l)[16:])

                dve.wait_ge(at_out, st["g"])
                V.tensor_tensor(DELTA[:, :, 1:T], RP[:, :, 0:T - 1], RP[:, :, 1:T], ALU.subtract)
                link(V.tensor_scalar(DELTA[:, :, 0:1], RP[:, :, 0:1], -1.0, None, ALU.mult))
                for j in range(KD):
                    ins = V.scalar_tensor_tensor(RP[:, j, :], DELTA[:, j, :], pr(f"mu_{l}", j, j + 1), RP[:, j, :],
                                                 ALU.mult, ALU.add)
                link(ins)
                mark(rw_shift)
                pairs(FILL_START)
                for j in range(2):
                    free(V.tensor_scalar(LWV[:, j, :], take()[:, 0:T], pr(f"w0_{l}", j, j + 1), None, ALU.add))
                for j in range(2):
                    free(V.tensor_scalar(AV[:, j, :], take()[:, 0:T], pr(f"a0_{l}", j, j + 1), None, ALU.add))
                copy_units([GV[:, j, :] for j in range(2)])
                settled()
                mark(rw_sig)
                dve.wait_ge(rw_pre, l + 1)
                link(V.tensor_scalar(LWV, LWV, -float(np.exp(-0.5)), None, ALU.mult))
                for j in range(2):
                    ins = V.tensor_tensor_scan(CC[:, j, :], cn("segs"), LWV[:, j, :], 0.0, ALU.mult, ALU.add)
                link(ins)
                V.tensor_tensor(EX, CC, LWV, ALU.subtract).then_inc(rw_c, 1)
                for j in range(2):
                    ins = V.tensor_scalar(KK[:, j, :], RP[:, 2 + j, :], pr(f"kk_{l}", j, j + 1), None, ALU.mult)
                link(ins)
                V.tensor_tensor(KNORM, KK, KK, ALU.mult)
                for j in range(2):
                    ins = V.tensor_scalar(BON[:, j, :], AV[:, j, :], -1.0, pr(f"ka_{l}", j, j + 1), ALU.add, ALU.mult)
                link(ins)
                link(V.scalar_tensor_tensor(RP[:, 2:4, :], BON, 1.0, RP[:, 2:4, :], ALU.add, ALU.mult))
                for j in range(2):
                    ins = V.scalar_tensor_tensor(RKK[:, j, :], RP[:, j, :], pr(f"rk_{l}", j, j + 1), RP[:, 2 + j, :],
                                                 ALU.mult, ALU.mult)
                link(ins)
                go()
                pairs(FILL_LOW)
                b = take()
                kn = KNORM[:, :, :].rearrange("p a b -> p (a b)")
                free(V.tensor_scalar(kn, b[:, :], 1e-12, None, ALU.add))
                settled()
                mark(rw_ks)
                b = take()
                free(V.tensor_tensor(BON, b[:, :].rearrange("p (a b) -> p a b", a=2), RP[:, 4:6, :], ALU.mult))
                dve.wait_ge(rw_kroot, l + 1)
                link(V.reciprocal(KNORM, KNORM))
                link(V.tensor_tensor(KK, KK, KNORM, ALU.mult))
                dve.wait_ge(rw_exp, l + 1)
                V.tensor_tensor(KR[:, :, 0, :], KK, EX, ALU.mult)
                V.tensor_tensor(KR[:, :, 1, :], RP[:, 0:2, :], EC, ALU.mult)
                V.tensor_tensor(KH, RP[:, 2:4, :], EN, ALU.mult)
                link(V.tensor_tensor(BH, KK, AV, ALU.mult))
                link(V.tensor_tensor(BH, BH, EN, ALU.mult))
                go()
                pairs(FILL_NORM)
                for n in range(4):
                    free(V.tensor_copy(TOK[n][:, :, :].rearrange("p a b -> p (a b)"), take()[:, :]))
                for m in range(8):
                    free(V.tensor_tensor(MM[:, m, :], take()[:, :], cn("pairmask"), ALU.mult))
                for cp in range(2):
                    b = take()[:, :].rearrange("p (m c) -> p m c", m=4)
                    free(V.tensor_tensor(XX[:, 4 * cp:4 * cp + 4, 0:P], b, over(cn("inv0"), 4), ALU.mult))
                settled()
                link(V.tensor_tensor(XX[:, :, P:2 * P], MM[:, :, 0:P], over(cn("inv0t"), 8), ALU.mult))
                xx = XX[:, :, :].rearrange("p m (a c) -> p (m a) c", a=2)
                link(V.tensor_tensor(xx, xx, over(ident, 16), ALU.add))
                for lev in range(5):
                    link(V.tensor_tensor(LK, MM[:, :, 0:P], over(cn("levels", lev * P, (lev + 1) * P), 8), ALU.mult))
                    go()
                    pairs(FILL_LEVEL if lev else FILL_MATRIX)
                    for q in range(2):
                        free(V.tensor_copy(PP[:, 4 * q:4 * q + 4, :].rearrange("p a b -> p (a b)"), take()[:, :]))
                    settled()
                    go()
                    pairs(FILL_LEVEL)
                    for q in range(4):
                        x2 = XX[:, 2 * q:2 * q + 2, :].rearrange("p a b -> p (a b)")
                        free(V.tensor_tensor(x2, x2, take()[:, :], ALU.subtract))
                    settled()
                go()
                pairs(FILL_LEVEL)
                free(V.tensor_copy(MVS[:, :, :].rearrange("p a b -> p (a b)"), take()[:, :]))
                free(V.tensor_scalar(GTN[:, :, :].rearrange("p a b -> p (a b)"), take()[:, :], -1.0, None, ALU.mult))
                settled()
                go()
                free(V.tensor_scalar(U0N[:, :, :].rearrange("p a b -> p (a b)"), take()[:, :], -1.0, None, ALU.mult))
                link(V.memset(STATE[:, 0, :], 0.0))
                settled()
                go()
                for c in range(4):
                    cp, rb = c // 2, (c % 2) * 64
                    for par in range(2):
                        b = take()[rb:rb + 64, 0:P].rearrange("p (a b) -> p a b", a=2)
                        m = 4 * par + 2 * cp
                        free(V.tensor_tensor(SA[rb:rb + 64, 2 * par:2 * par + 2, :], b, U0N[rb:rb + 64, m:m + 2, :], ALU.add))
                    settled()
                    go()
                    b = take()
                    if c < 3:
                        link(V.tensor_tensor(STATE[:, 4, :], STATE[:, c, :], b[:, 0:P], ALU.add))
                        for j in range(2):
                            ins = V.tensor_scalar(STATE[:, c + 1, j * 64:(j + 1) * 64], STATE[:, 4, j * 64:(j + 1) * 64],
                                                  EC[:, j, c * 64 + 63:c * 64 + 64], None, ALU.mult)
                        link(ins)
                    free(V.tensor_copy(small(158, 1), b[:, 0:1]))
                    if c < 3:
                        go()
                    yc = YC[:, :, c * 64:(c + 1) * 64]
                    for part in range(2):
                        b = take()[:, 0:P].rearrange("p (a b) -> p a b", a=2)
                        if part:
                            settled_but_last()
                        free(V.tensor_tensor(yc, yc, b, ALU.add) if part else V.tensor_copy(yc, b))
                    settled()
                link(V.tensor_copy(YT, YC))
                go()
                b = take()[:, :].rearrange("p (a b) -> p a b", a=2)
                link(V.scalar_tensor_tensor(YC, b, -1.0 / HD, YT, ALU.mult, ALU.add))
                free(V.tensor_tensor(YS, YC, YC, ALU.mult))
                settled()
                go()
                b = take()[:, :].rearrange("p (a b) -> p a b", a=2)
                free(V.tensor_scalar(YS, b, 1.0 / HD, None, ALU.mult))
                settled()
                mark(rw_var)
                dve.wait_ge(rw_vroot, l + 1)
                link(V.reciprocal(YS, YS))
                link(V.tensor_tensor(YC, YC, YS, ALU.mult))
                for j in range(2):
                    ins = V.tensor_scalar(YC[:, j, :], YC[:, j, :], pr(f"gng_{l}", j, j + 1), pr(f"gnb_{l}", j, j + 1),
                                          ALU.mult, ALU.add)
                link(ins)
                link(V.tensor_tensor(YC, YC, BON, ALU.add))
                link(V.tensor_tensor(CAT2[:, 4:6, :], YC, GV, ALU.mult))
                go()

                assert st["u"] == UB[l]["merge"], (st["u"], UB)
                pairs(KD)
                st["c"] = 0
                input_low(PL, CL, ACC, 18 + 3 * KD * l + KD)
                low_parts(PROJ_START[5 + 2 * l], AHEAD)
                for j in range(KD):
                    ins = V.tensor_scalar(X[:, j, 0:T], X[:, j, 0:T], ALPHA, None, ALU.mult)
                link(ins)
                projections(5 + 2 * l, [(X[:, j, 0:T], 2, lambda d, b, j=j: residual_parts(j, b, T, None))
                                        for j in range(KD)])
                settled()
                go()
                norm(5 + 2 * l, T, X, X)
                dve.wait_ge(n_a, 8 * (6 + 2 * l))
                if l == 1:
                    for t in range(2):
                        free(V.tensor_tensor(LG[:, 8 * t:8 * t + 8], take()[:, 0:8], pr("router_b"), ALU.add))
                    settled()
                    for t in range(2):
                        lg, m8 = LG[:, 8 * t:8 * t + 8], M8[:, 8 * t:8 * t + 8]
                        link(V.max(m8, lg))
                        link(V.max_index(idx8[:, t, :], m8, lg))
                        V.tensor_copy(IDXF[:, 2 * t:2 * t + 2], idx8[:, t, 0:2])
                        link(V.tensor_tensor(EE[:, t:t + 1], m8[:, 1:2], m8[:, 0:1], ALU.subtract))
                    mark(top_v)
                    dve.wait_ge(top_e, 1)
                    link(V.tensor_scalar(EE[:, 2:4], EE[:, 0:2], 1.0, None, ALU.add))
                    link(V.reciprocal(EE[:, 4:6], EE[:, 2:4]))
                    link(V.tensor_tensor(EE[:, 6:8], EE[:, 4:6], EE[:, 0:2], ALU.mult))
                    for t in range(2):
                        V.tensor_scalar(OH[:, 0, :], cn("iota8"), IDXF[:, 2 * t:2 * t + 1], EE[:, 4 + t:5 + t],
                                        ALU.is_equal, ALU.mult)
                        link(V.tensor_scalar(OH[:, 1, :], cn("iota8"), IDXF[:, 2 * t + 1:2 * t + 2], EE[:, 6 + t:7 + t],
                                             ALU.is_equal, ALU.mult))
                        link(V.tensor_tensor(CWT[:, t, :], OH[:, 0, :], OH[:, 1, :], ALU.add))
                    go()
                    copy_units([CWR[0:8, :]])
                    settled()
                    go()
                    copy_units([CW[:, e, :] for e in range(EXPERTS)])
                    settled()
                    go()
                input_low(AH, AL, X, 18 + 3 * KD * l + 2 * KD)
                for j in range(KD):
                    ins = V.tensor_scalar(X[:, j, 0:T], X[:, j, 0:T], ALPHA, None, ALU.mult)
                link(ins)
                go()
                assert st["u"] == UB[l]["ffn"], (st["u"], UB)
                if l == 1:
                    assert st["tmp"] == UB["tmp_experts"], (st, UB)
                ffn(4 + 2 * l, 2 if l == 0 else EXPERTS, T, None, experts=l == 1)
                settled()
                norm(6 + 2 * l, T, X, X, ahead=PROJ_START[6] if l == 0 else None)


def _unit_bases():
    u = 20 + 8 + 4 + KD + 2 * UNITS_FFN
    u += 10 + 4 + 10 + 4 + KD + 2 * UNITS_FFN
    out = {}
    for l in range(2):
        u += 23 + 6 + 4
        out[l] = {"index": u}
        u += 8 + 2 * FILLED
        u += 6 + 2 + 4 + 8 + 2 + 5 * 6 + 3 + 20 + 2
        out[l]["merge"] = u
        u += 2 * KD + KD
        if l:
            u += 2 + 1 + EXPERTS
        out[l]["ffn"] = u
        u += (2 if l == 0 else EXPERTS) * UNITS_FFN
    out["tmp_experts"] = 2 * FH * 3 + 2 * 4 * KD
    return out


def tile_unit(j):
    return j + max(0, min(j - 2, 8))


def gate_chunks(q, ada):
    return 2 * 2 * q + 2 + (KD // 2 * sum(len(x) for x in ADA_HALVES[:q]) if ada else 0)


def part_chunks(ada):
    return gate_chunks(FH, ada) - 2 + FH * KD // CHUNK


UB = _unit_bases()
PART_CHUNKS = part_chunks(False)
FFN_START, PROJ_START = stream_plan()[1:]


def kernel(**inputs):
    import concourse.bacc as bacc
    from concourse.bass_utils import run_bass_kernel_spmd as run

    a = {k: np.asarray(v) for k, v in inputs.items()}
    plan = stream_plan()[0]
    chunks = len(plan) // CHUNK
    stream = np.zeros((chunks, P, CHUNK * P), np.float32)
    for n, blk in enumerate(plan):
        if blk is None:
            continue
        name, idx, row, col, width = blk
        w = a[name][idx]
        dst = stream[n // CHUNK, :, (n % CHUNK) * P:(n % CHUNK + 1) * P]
        if isinstance(col, tuple):
            ws = width if isinstance(width, tuple) else (width,) * len(col)
            at = 0
            for c, k in zip(col, ws):
                dst[:, at:at + k] = w[row:row + P, c:c + k]
                at += k
        else:
            dst[:, 0:width] = w[row:row + P, col:col + width]

    par = np.zeros((P, NPAR), np.float32)

    def put(name, v):
        lo, hi = PO[name]
        par[:, lo:hi] = v

    def cols(v):
        return v.reshape(-1, P).T

    put("eps6", 1e-6)
    put("eps5", 1e-5)
    put("epsgn", 64e-5)
    cv = np.stack([cols(a["c"][0]), cols(a["c_ctx"])], -1)
    put("cvec", cv.reshape(P, -1))
    for l in range(2):
        put(f"ada_b{l}", cols(a["ada_b"][l]))
        put(f"n1g{l}", cols(a["norm1_g"][l]))
        put(f"n2g{l}", cols(a["norm2_g"][l]))
    put("final_g", cols(a["final_g"]))
    put("sgu_b", a["sgu_b"][0].reshape(1, -1))
    put("lqk", np.concatenate([a[n][0] for n in ("diff_lq1", "diff_lk1", "diff_lq2", "diff_lk2")])[None])
    put("subln", cols(a["diff_subln_g"][0]))
    put("odd_sink", a["odd_sink"][0][None])
    put("sgu_w", a["sgu_w"][0].transpose(2, 0, 1).reshape(P, -1))
    put("router_w", a["router_w_2"][0].reshape(KD, P, 8).transpose(1, 0, 2).reshape(P, -1))
    put("router_b", a["router_b_2"][0][None])
    for l in range(2):
        put(f"sinks_{l}", a["swa_sinks_2"][l][None])
        for n, k in (("mu", "rwkv_mu_2"), ("w0", "rwkv_w0_2"), ("a0", "rwkv_a0_2"), ("kk", "rwkv_k_k_2"),
                     ("ka", "rwkv_k_a_2"), ("rk", "rwkv_r_k_2"), ("gng", "rwkv_gn_g_2"), ("gnb", "rwkv_gn_b_2"),
                     ("gate_b", "gate_bias_2")):
            put(f"{n}_{l}", cols(a[k][l]))
        for i in range(2):
            put(f"ln{i + 1}g_{l}", cols(a["ln_g_2"][l, i]))
            put(f"ln{i + 1}b_{l}", cols(a["ln_b_2"][l, i]))
        lo, hi = PO[f"fbias_{l}"]
        par[0:4, lo:hi] = a["fox_f_bias_2"][l][:, None]
        put(f"wa_up_{l}", np.concatenate([a["rwkv_w_up_2"][l], a["rwkv_a_up_2"][l]], 0))
        put(f"g_up_{l}", a["rwkv_g_up_2"][l])

    xin = np.concatenate([a["x"][0], a["ctx"][0]], 0).T.reshape(KD, P, TT).transpose(1, 0, 2)
    arrays = {"stream": stream, "params": par, "consts": constants(), "xin": np.ascontiguousarray(xin)}
    nc = bacc.Bacc("TRN2", target_bir_lowering=False, num_devices=1)
    aps = [nc.dram_tensor(k, v.shape, F32, kind="ExternalInput").ap() for k, v in arrays.items()]
    out = nc.dram_tensor("out", (P, KD, T), F32, kind="ExternalOutput").ap()
    build(nc, *aps, out)
    r = run(nc, [arrays], core_ids=[0])
    y = r.results[0]["out"]
    return np.ascontiguousarray(y.transpose(2, 1, 0).reshape(1, T, D))
```
